# Optimizing a Trainium2 kernel written in Bass

```python
import jax, jax.numpy as jnp
from jax import lax
import numpy as np
import math

D_MODEL = 1024
BATCH = 1
SEQ = 256
DEPTH = 2

GRID_W = 64
CTX_LEN = 256
HEAD_DIM = 64
ATTN_DIM = D_MODEL // 2
N_Q_HEADS = ATTN_DIM // HEAD_DIM
N_KV_HEADS = N_Q_HEADS // 4
Q_PER_KV = N_Q_HEADS // N_KV_HEADS
KV_DIM = N_KV_HEADS * HEAD_DIM
GMLP_DIM = D_MODEL - ATTN_DIM
GMLP_GROUP_DIM = 128
N_GMLP_GROUPS = GMLP_DIM // GMLP_GROUP_DIM
CHUNK = 128
MIX_DIM = ATTN_DIM + GMLP_DIM
IN_DIM = ATTN_DIM + 2 * KV_DIM + 2 * GMLP_DIM
FF_DIM = 4 * D_MODEL
Q_BLOCK = 128
ROPE_THETA = 10000.0
EPS = 1e-6
N_MOD = 6


def rmsnorm(x, g):
    xf = x.astype(jnp.float32)
    y = xf * lax.rsqrt(jnp.mean(xf * xf, axis=-1, keepdims=True) + EPS)
    return (y * g.astype(jnp.float32)).astype(x.dtype)

def group_layernorm(v, g):
    vf = v.astype(jnp.float32)
    mu = jnp.mean(vf, axis=-1, keepdims=True)
    var = jnp.mean(jnp.square(vf - mu), axis=-1, keepdims=True)
    return ((vf - mu) * lax.rsqrt(var + EPS) * g.astype(jnp.float32)).astype(v.dtype)

def modulation(cond, w_mod, b_mod):
    m = jax.nn.silu(cond) @ w_mod + b_mod
    return m.reshape(m.shape[:-1] + (N_MOD, D_MODEL))

def modulate(h, shift, scale):
    return h * (1 + scale) + shift

def axial_rope_tables(n_lat):
    rows = n_lat // GRID_W
    row = jnp.repeat(jnp.arange(rows, dtype=jnp.float32), GRID_W)
    col = jnp.tile(jnp.arange(GRID_W, dtype=jnp.float32), rows)
    n_freq = HEAD_DIM // 4
    inv_freq = ROPE_THETA ** (-jnp.arange(n_freq, dtype=jnp.float32) / n_freq)
    ang = jnp.stack([row[:, None] * inv_freq, col[:, None] * inv_freq], axis=1)
    return jnp.cos(ang), jnp.sin(ang)

def apply_rope(x, cos, sin):
    xf = x.astype(jnp.float32).reshape(x.shape[:-1] + (2, 2, HEAD_DIM // 4))
    x1, x2 = xf[..., 0, :], xf[..., 1, :]
    out = jnp.stack([x1 * cos - x2 * sin, x2 * cos + x1 * sin], axis=-2)
    return out.reshape(x.shape).astype(x.dtype)

def q_heads(q):
    b, n, _ = q.shape
    return q.reshape(b, n, N_KV_HEADS, Q_PER_KV, HEAD_DIM).transpose(0, 2, 3, 1, 4)

def kv_heads(k):
    b, n, _ = k.shape
    return k.reshape(b, n, N_KV_HEADS, HEAD_DIM).transpose(0, 2, 1, 3)

def gqa_blocks(q, k, v):
    b, kvh, g, n, dh = q.shape
    nb = n // Q_BLOCK
    qb = jnp.moveaxis(q.reshape(b, kvh, g, nb, Q_BLOCK, dh), 3, 0)

    def one_block(qblk):
        s = jnp.einsum('bkgqd,bkmd->bkgqm', qblk, k).astype(jnp.float32)
        p = jax.nn.softmax(s, axis=-1).astype(v.dtype)
        return jnp.einsum('bkgqm,bkmd->bkgqd', p, v)

    o = lax.map(one_block, qb)
    o = jnp.moveaxis(o, 0, 3).reshape(b, kvh, g, n, dh)
    return o.transpose(0, 3, 1, 2, 4).reshape(b, n, ATTN_DIM)

def chunk_gmlp(u, vg, w_s, b_s, g_norm):
    b, n, _ = u.shape
    u = jax.nn.gelu(u)
    vg = group_layernorm(jax.nn.gelu(vg).reshape(b, n, N_GMLP_GROUPS, GMLP_GROUP_DIM),
                         g_norm.reshape(N_GMLP_GROUPS, GMLP_GROUP_DIM))
    vc = vg.reshape(b, n // CHUNK, CHUNK, N_GMLP_GROUPS, GMLP_GROUP_DIM)
    mixed = jnp.einsum('gpq,bnqgc->bnpgc', w_s, vc) + b_s.T[None, None, :, :, None]
    return u * mixed.reshape(b, n, GMLP_DIM)

def sqrelu_mlp(h, w1, w2):
    return jnp.square(jax.nn.relu(h @ w1)) @ w2

def first_inputs(seed: int = 0) -> dict:
    key = jax.random.key(seed)
    ks = jax.random.split(key, 17)
    f32 = jnp.float32
    nrm = lambda k, shape, s: (jax.random.normal(k, shape, f32) * s)
    gain = lambda k, shape: 1.0 + 0.02 * jax.random.normal(k, shape, f32)
    return {
        "x": nrm(ks[0], (BATCH, SEQ, D_MODEL), 1.0),
        "c": nrm(ks[1], (BATCH, D_MODEL), 1.0),
        "ctx": nrm(ks[2], (BATCH, CTX_LEN, D_MODEL), 1.0),
        "c_ctx": nrm(ks[3], (D_MODEL,), 1.0),
        "w_mod": nrm(ks[4], (DEPTH, D_MODEL, N_MOD * D_MODEL), D_MODEL ** -0.5),
        "b_mod": nrm(ks[5], (DEPTH, N_MOD * D_MODEL), 0.02),
        "norm1_g": gain(ks[6], (DEPTH, D_MODEL)),
        "w_in": nrm(ks[7], (DEPTH, D_MODEL, IN_DIM), D_MODEL ** -0.5),
        "q_norm_g": gain(ks[8], (DEPTH, HEAD_DIM)),
        "k_norm_g": gain(ks[9], (DEPTH, HEAD_DIM)),
        "gmlp_norm_g": gain(ks[10], (DEPTH, GMLP_DIM)),
        "w_spatial": nrm(ks[11], (DEPTH, N_GMLP_GROUPS, CHUNK, CHUNK), CHUNK ** -0.5),
        "b_spatial": gain(ks[12], (DEPTH, N_GMLP_GROUPS, CHUNK)),
        "w_out": nrm(ks[13], (DEPTH, MIX_DIM, D_MODEL), MIX_DIM ** -0.5),
        "norm2_g": gain(ks[14], (DEPTH, D_MODEL)),
        "w_ff1": nrm(ks[15], (DEPTH, D_MODEL, FF_DIM), D_MODEL ** -0.5),
        "w_ff2": nrm(ks[16], (DEPTH, FF_DIM, D_MODEL), FF_DIM ** -0.5),
    }

def first_block(x, c, ctx, c_ctx, w_mod, b_mod, norm1_g, w_in, q_norm_g, k_norm_g, gmlp_norm_g,
              w_spatial, b_spatial, w_out, norm2_g, w_ff1, w_ff2):
    n_lat = x.shape[1]
    cos, sin = axial_rope_tables(n_lat)
    q_scale = HEAD_DIM ** -0.5
    kv_lo, kv_hi = ATTN_DIM, ATTN_DIM + 2 * KV_DIM
    x_lat, x_ctx = x, ctx
    for l in range(DEPTH):
        last = l == DEPTH - 1
        m_lat = modulation(c, w_mod[l], b_mod[l])
        m_ctx = modulation(c_ctx, w_mod[l], b_mod[l])
        sh1, sc1, ga1, sh2, sc2, ga2 = [m_lat[:, i, None, :] for i in range(N_MOD)]
        csh1, csc1, cga1, csh2, csc2, cga2 = [m_ctx[None, i, None, :] for i in range(N_MOD)]

        h_lat = modulate(rmsnorm(x_lat, norm1_g[l]), sh1, sc1)
        h_ctx = modulate(rmsnorm(x_ctx, norm1_g[l]), csh1, csc1)
        z_lat = h_lat @ w_in[l]
        q_l = z_lat[..., :ATTN_DIM]
        k_l = z_lat[..., kv_lo:kv_lo + KV_DIM]
        v_l = z_lat[..., kv_lo + KV_DIM:kv_hi]
        u_l = z_lat[..., kv_hi:kv_hi + GMLP_DIM]
        g_l = z_lat[..., kv_hi + GMLP_DIM:]
        if last:
            z_ctx = h_ctx @ w_in[l][:, kv_lo:kv_hi]
            k_c, v_c = z_ctx[..., :KV_DIM], z_ctx[..., KV_DIM:]
        else:
            z_ctx = h_ctx @ w_in[l]
            q_c = z_ctx[..., :ATTN_DIM]
            k_c = z_ctx[..., kv_lo:kv_lo + KV_DIM]
            v_c = z_ctx[..., kv_lo + KV_DIM:kv_hi]
            u_c = z_ctx[..., kv_hi:kv_hi + GMLP_DIM]
            g_c = z_ctx[..., kv_hi + GMLP_DIM:]

        qh_l = apply_rope(rmsnorm(q_heads(q_l), q_norm_g[l]), cos, sin) * q_scale
        kh_l = apply_rope(rmsnorm(kv_heads(k_l), k_norm_g[l]), cos, sin)
        kh_c = rmsnorm(kv_heads(k_c), k_norm_g[l])
        vh_c = kv_heads(v_c)
        k_all = jnp.concatenate([kh_c, kh_l], axis=2)
        v_all = jnp.concatenate([vh_c, kv_heads(v_l)], axis=2)
        attn_lat = gqa_blocks(qh_l, k_all, v_all)
        gm_lat = chunk_gmlp(u_l, g_l, w_spatial[l], b_spatial[l], gmlp_norm_g[l])
        x_lat = x_lat + ga1 * (jnp.concatenate([attn_lat, gm_lat], axis=-1) @ w_out[l])
        x_lat = x_lat + ga2 * sqrelu_mlp(modulate(rmsnorm(x_lat, norm2_g[l]), sh2, sc2),
                                         w_ff1[l], w_ff2[l])

        if not last:
            qh_c = rmsnorm(q_heads(q_c), q_norm_g[l]) * q_scale
            attn_ctx = gqa_blocks(qh_c, kh_c, vh_c)
            gm_ctx = chunk_gmlp(u_c, g_c, w_spatial[l], b_spatial[l], gmlp_norm_g[l])
            x_ctx = x_ctx + cga1 * (jnp.concatenate([attn_ctx, gm_ctx], axis=-1) @ w_out[l])
            x_ctx = x_ctx + cga2 * sqrelu_mlp(modulate(rmsnorm(x_ctx, norm2_g[l]), csh2, csc2),
                                              w_ff1[l], w_ff2[l])
    return x_lat


N_DIFF_HEADS = 4
DIFF_V_DIM = 2 * HEAD_DIM
DIFF_QK = N_DIFF_HEADS * 2 * HEAD_DIM
DIFF_WIDTH = N_DIFF_HEADS * DIFF_V_DIM
N_FOX_HEADS = 8
FOX_WIDTH = N_FOX_HEADS * HEAD_DIM
N_BUCKETS = 32
MAX_DISTANCE = 128
N_KEYS = 128
N_EXPERTS = N_KEYS * N_KEYS
PEER_HEADS = 8
PEER_TOPK = 16
PEER_QDIM = 256
PEER_HALF = PEER_QDIM // 2
TOKEN_BLOCK = 128
IN_SIZES = (DIFF_QK, DIFF_QK, DIFF_WIDTH, FOX_WIDTH, FOX_WIDTH, FOX_WIDTH, N_FOX_HEADS, D_MODEL, D_MODEL)
IN_WIDTH = sum(IN_SIZES)


def rms_norm(x, g):
    xf = x.astype(jnp.float32)
    y = xf * lax.rsqrt(jnp.mean(xf * xf, axis=-1, keepdims=True) + EPS)
    return (y * g.astype(jnp.float32)).astype(x.dtype)

def t5_bucket(dist):
    n = jnp.maximum(dist, 0)
    max_exact = N_BUCKETS // 2
    nf = jnp.maximum(n, 1).astype(jnp.float32)
    large = max_exact + (jnp.log(nf / max_exact) / math.log(MAX_DISTANCE / max_exact)
                         * (N_BUCKETS - max_exact)).astype(jnp.int32)
    large = jnp.minimum(large, N_BUCKETS - 1)
    return jnp.where(n < max_exact, n, large)

def diff_attention(q, k, v, rel_bias, lam, lam_init, subln_g):
    B, S = q.shape[0], q.shape[1]
    scale = HEAD_DIM ** -0.5
    lf = lam.astype(jnp.float32)
    lam_full = jnp.exp(jnp.sum(lf[0] * lf[1])) - jnp.exp(jnp.sum(lf[2] * lf[3])) + lam_init
    outs = []
    for blk in range(S // Q_BLOCK):
        q0 = blk * Q_BLOCK
        end = q0 + Q_BLOCK
        logits = jnp.einsum('bqhmd,bkhmd->bhmqk', q[:, q0:end], k[:, :end]).astype(jnp.float32) * scale
        dist = (q0 + jnp.arange(Q_BLOCK))[:, None] - jnp.arange(end)[None, :]
        bias = jnp.transpose(rel_bias[t5_bucket(dist)], (2, 0, 1))[:, None]
        logits = jnp.where(dist >= 0, logits + bias.astype(jnp.float32), -jnp.inf)
        probs = jax.nn.softmax(logits, axis=-1)
        weights = probs[:, :, 0] - lam_full * probs[:, :, 1]
        outs.append(jnp.einsum('bhqk,bkhd->bqhd', weights.astype(v.dtype), v[:, :end]))
    o = jnp.concatenate(outs, axis=1)
    o = rms_norm(o, subln_g) * (1.0 - lam_init)
    return o.reshape(B, S, DIFF_WIDTH)

def forgetting_attention(q, k, v, f_logit):
    B, S = q.shape[0], q.shape[1]
    scale = HEAD_DIM ** -0.5
    c = jnp.swapaxes(jnp.cumsum(jax.nn.log_sigmoid(f_logit.astype(jnp.float32)), axis=1), 1, 2)
    outs = []
    for blk in range(S // Q_BLOCK):
        q0 = blk * Q_BLOCK
        end = q0 + Q_BLOCK
        logits = jnp.einsum('bqhd,bkhd->bhqk', q[:, q0:end], k[:, :end]).astype(jnp.float32) * scale
        decay = c[:, :, q0:end, None] - c[:, :, None, :end]
        dist = (q0 + jnp.arange(Q_BLOCK))[:, None] - jnp.arange(end)[None, :]
        logits = jnp.where(dist >= 0, logits + decay, -jnp.inf)
        probs = jax.nn.softmax(logits, axis=-1)
        outs.append(jnp.einsum('bhqk,bkhd->bqhd', probs.astype(v.dtype), v[:, :end]))
    return jnp.concatenate(outs, axis=1).reshape(B, S, FOX_WIDTH)

def peer_ffn(h, w_query, sub_keys, expert_u, expert_v):
    B, S, D = h.shape
    T = B * S
    t = h.reshape(T, D)
    q = (t @ w_query).reshape(T, PEER_HEADS, 2, PEER_HALF)
    s = jnp.einsum('thpd,pnd->thpn', q, sub_keys).astype(jnp.float32)
    top_s, top_i = lax.top_k(s, PEER_TOPK)
    cand_s = (top_s[:, :, 0, :, None] + top_s[:, :, 1, None, :]).reshape(T, PEER_HEADS, PEER_TOPK * PEER_TOPK)
    cand_i = (top_i[:, :, 0, :, None] * N_KEYS + top_i[:, :, 1, None, :]).reshape(T, PEER_HEADS, PEER_TOPK * PEER_TOPK)
    best_s, best_pos = lax.top_k(cand_s, PEER_TOPK)
    experts = jnp.take_along_axis(cand_i, best_pos, axis=-1).reshape(T, PEER_HEADS * PEER_TOPK)
    gates = jax.nn.softmax(best_s, axis=-1).reshape(T, PEER_HEADS * PEER_TOPK)
    nblk = T // TOKEN_BLOCK

    def expert_block(args):
        tb, eb, gb = args
        act = jax.nn.gelu(jnp.einsum('td,ted->te', tb, expert_u[eb]).astype(jnp.float32), approximate=False)
        return jnp.einsum('te,ted->td', (gb * act).astype(tb.dtype), expert_v[eb])

    out = lax.map(expert_block, (t.reshape(nblk, TOKEN_BLOCK, D),
                                 experts.reshape(nblk, TOKEN_BLOCK, -1),
                                 gates.reshape(nblk, TOKEN_BLOCK, -1)))
    return out.reshape(B, S, D)

def second_inputs(seed: int = 0) -> dict:
    key = jax.random.key(seed)
    ks = jax.random.split(key, 17)
    nrm = lambda k, shape, scale: jax.random.normal(k, shape, jnp.float32) * scale
    return {
        "x": nrm(ks[0], (BATCH, SEQ, D_MODEL), 1.0),
        "norm1_g": 1.0 + nrm(ks[1], (DEPTH, D_MODEL), 0.02),
        "w_in": nrm(ks[2], (DEPTH, D_MODEL, IN_WIDTH), D_MODEL ** -0.5),
        "b_forget": 2.0 + nrm(ks[3], (DEPTH, N_FOX_HEADS), 0.1),
        "diff_lambda": nrm(ks[4], (DEPTH, 4, HEAD_DIM), 0.1),
        "diff_subln_g": 1.0 + nrm(ks[5], (DEPTH, DIFF_V_DIM), 0.02),
        "w_diff_o": nrm(ks[6], (DEPTH, DIFF_WIDTH, D_MODEL), DIFF_WIDTH ** -0.5),
        "w_fox_o": nrm(ks[7], (DEPTH, FOX_WIDTH, D_MODEL), FOX_WIDTH ** -0.5),
        "w_out": nrm(ks[8], (DEPTH, D_MODEL, D_MODEL), D_MODEL ** -0.5),
        "norm2_g": 1.0 + nrm(ks[9], (DEPTH, D_MODEL), 0.02),
        "w_query": nrm(ks[10], (DEPTH, D_MODEL, PEER_HEADS * PEER_QDIM), D_MODEL ** -0.5),
        "sub_keys": nrm(ks[11], (DEPTH, 2, N_KEYS, PEER_HALF), PEER_HALF ** -0.5),
        "expert_u": nrm(ks[12], (DEPTH, N_EXPERTS, D_MODEL), D_MODEL ** -0.5),
        "expert_v": nrm(ks[13], (DEPTH, N_EXPERTS, D_MODEL), (PEER_HEADS * PEER_TOPK) ** -0.5),
        "rel_bias": nrm(ks[14], (N_BUCKETS, N_DIFF_HEADS), 0.5),
        "final_norm_g": 1.0 + nrm(ks[15], (D_MODEL,), 0.02),
    }

def second_block(x, norm1_g, w_in, b_forget, diff_lambda, diff_subln_g, w_diff_o, w_fox_o, w_out,
              norm2_g, w_query, sub_keys, expert_u, expert_v, rel_bias, final_norm_g):
    B, S, D = x.shape
    split_points = np.cumsum(IN_SIZES)[:-1].tolist()
    for layer in range(DEPTH):
        lam_init = 0.8 - 0.6 * math.exp(-0.3 * layer)
        h = rms_norm(x, norm1_g[layer])
        proj = h @ w_in[layer]
        dq, dk, dv, fq, fk, fv, ff, ga, gb = jnp.split(proj, split_points, axis=-1)
        y_diff = diff_attention(dq.reshape(B, S, N_DIFF_HEADS, 2, HEAD_DIM),
                                dk.reshape(B, S, N_DIFF_HEADS, 2, HEAD_DIM),
                                dv.reshape(B, S, N_DIFF_HEADS, DIFF_V_DIM),
                                rel_bias, diff_lambda[layer], lam_init, diff_subln_g[layer])
        y_fox = forgetting_attention(fq.reshape(B, S, N_FOX_HEADS, HEAD_DIM),
                                     fk.reshape(B, S, N_FOX_HEADS, HEAD_DIM),
                                     fv.reshape(B, S, N_FOX_HEADS, HEAD_DIM),
                                     ff + b_forget[layer])
        merged = jax.nn.sigmoid(ga) * (y_diff @ w_diff_o[layer]) + jax.nn.sigmoid(gb) * (y_fox @ w_fox_o[layer])
        x = x + merged @ w_out[layer]
        x = x + peer_ffn(rms_norm(x, norm2_g[layer]), w_query[layer], sub_keys[layer],
                         expert_u[layer], expert_v[layer])
    return rms_norm(x, final_norm_g)


def setup_inputs(seed=0):
    out = dict(first_inputs(seed))
    for name, value in second_inputs(seed + 1).items():
        if name != "x":
            out[name + "_2"] = value
    return out


def reference(
    x, c, ctx, c_ctx, w_mod, b_mod, norm1_g, w_in, q_norm_g, k_norm_g, gmlp_norm_g, w_spatial,
    b_spatial, w_out, norm2_g, w_ff1, w_ff2, norm1_g_2, w_in_2, b_forget_2, diff_lambda_2,
    diff_subln_g_2, w_diff_o_2, w_fox_o_2, w_out_2, norm2_g_2, w_query_2, sub_keys_2,
    expert_u_2, expert_v_2, rel_bias_2, final_norm_g_2,
):
    x = first_block(
        x, c, ctx, c_ctx, w_mod, b_mod, norm1_g, w_in, q_norm_g, k_norm_g, gmlp_norm_g,
        w_spatial, b_spatial, w_out, norm2_g, w_ff1, w_ff2,
    )
    return second_block(
        x, norm1_g_2, w_in_2, b_forget_2, diff_lambda_2, diff_subln_g_2, w_diff_o_2, w_fox_o_2,
        w_out_2, norm2_g_2, w_query_2, sub_keys_2, expert_u_2, expert_v_2, rel_bias_2,
        final_norm_g_2,
    )


_drawn_inputs = setup_inputs


def setup_inputs(seed=0):
    import zlib

    import numpy as np

    out = dict(_drawn_inputs(seed))
    spreads = {}
    factors = {'norm1_g': 4.072,
     'q_norm_g': 8.0,
     'k_norm_g': 8.0,
     'gmlp_norm_g': 6.82,
     'b_spatial': 6.988,
     'norm2_g': 2.834,
     'norm1_g_2': 7.261,
     'b_forget_2': 8.0,
     'diff_lambda_2': 8.0,
     'diff_subln_g_2': 52.488,
     'norm2_g_2': 59.383,
     'final_norm_g_2': 8.412}
    for name, (base, spread) in spreads.items():
        noise = np.random.default_rng([zlib.crc32(name.encode()), seed]).standard_normal(out[name].shape)
        drawn = base * np.exp(spread * noise) if base else spread * noise
        out[name] = __import__('jax').numpy.asarray(drawn.astype(out[name].dtype))
    for name, factor in factors.items():
        out[name] = (out[name] * factor).astype(out[name].dtype)
    return out
```

```python
import math
from contextlib import ExitStack

import numpy as np

import concourse.bass as bass
from concourse import mybir

F32 = mybir.dt.float32
U32 = mybir.dt.uint32
ALU = mybir.AluOpType
ACT = mybir.ActivationFunctionType
AX = mybir.AxisListType

P = 128
D = 1024
KD = D // P
LAYERS = 2
LAT = 2
TILES = 4
SEQ = LAT * P
HD = 64
AH, AKV = 8, 2
QW, KVW, GW = 512, 128, 512
ZW = QW + 2 * KVW
FF = 4 * D
EPS = 1e-6
CH = 512
SLOTS = 4
SCALE = HD ** -0.5
DH, FH = 4, 8
W2IN = 5128
FFCOL = 3072
PH, TOPK, NK = 8, 16, 128
NE = NK * NK
CONSTS = 13
CHUNKS_A, CHUNKS_B = 68, 18
PICKS = PH * TOPK
ROWS = 16
HALF = ROWS // 2
NEG = -1.0e30
REL = 384


def t5_bucket(dist, buckets=32, far=128):
    n = np.maximum(dist, 0)
    exact = buckets // 2
    nf = np.maximum(n, 1).astype(np.float32)
    large = exact + (np.log(nf / np.float32(exact)) / np.float32(math.log(far / exact))
                     * np.float32(buckets - exact)).astype(np.int32)
    return np.where(n < exact, n, np.minimum(large, buckets - 1))


def constants():
    tok = np.arange(SEQ)
    pos = np.stack([tok // 64, tok % 64], 1).astype(np.float32)
    freq = (10000.0 ** (-np.arange(16, dtype=np.float32) / 16)).astype(np.float32)
    ang = (pos[:, :, None] * freq).astype(np.float32)
    cos, sin = np.cos(ang), np.sin(ang)
    rope = np.zeros((SEQ, 2, 2, 2, 16), np.float32)
    rope[:, 0] = cos[:, :, None, :]
    rope[:, 1, :, 0], rope[:, 1, :, 1] = -sin, sin
    dist = 255 - np.arange(REL)
    onehot = np.zeros((33, REL), np.float32)
    onehot[t5_bucket(dist), np.arange(REL)] = dist >= 0
    onehot[32] = np.where(dist >= 0, 0.0, NEG)
    q, k = np.arange(P)[:, None], np.arange(SEQ)[None]
    mask = np.where(128 + q - k >= 0, 0.0, NEG).astype(np.float32)
    lam = [0.8 - 0.6 * math.exp(-0.3 * i) for i in range(LAYERS)]
    pickv = np.zeros((2, 2, P), np.float32)
    pickv[np.arange(2), np.arange(2)] = 1.0
    return {
        "rope": rope.reshape(SEQ, 128), "onehot": onehot, "mask": mask,
        "ones4": np.ones((1, DH), np.float32),
        "pickv": pickv.reshape(2, 256),
        "lam": np.array([[a, 1 - a] for a in lam], np.float32),
        "iota16": np.arange(16, dtype=np.float32)[None], "eye": np.eye(P, dtype=np.float32),
    }


def build(nc, A, out):
    ctx = ExitStack()
    with ctx:
        ctx.enter_context(nc.allow_non_contiguous_dma("small strided loads"))

        def sb(name, shape, dt=F32):
            return ctx.enter_context(nc.sbuf_tensor(name, shape, dt))

        def sem(name):
            return ctx.enter_context(nc.semaphore(name))

        def spread(ap, axis, n):
            ap = ap.unsqueeze(axis)
            shape = list(ap.shape)
            shape[axis] = n
            return ap.broadcast_to(shape)

        ring = sb("ring", [P, SLOTS, KD * CH])
        x = sb("x", [P, TILES, D])
        hT = sb("hT", [P, KD, TILES * P])
        big = sb("big", [P, 16384])
        gate = sb("gate", [P, 2, 2, D])
        xn = sb("xn", [P, 2, D])
        kT = sb("kT", [P, 2, TILES * P])
        wide = sb("wide", [P, D])
        ggain = sb("ggain", [P, GW])
        wsp = sb("wsp", [P, 4, P])
        wsT = sb("wsT", [P, 4, P])
        eye = sb("eye", [P, P])
        rows = sb("rows", [72, P])
        cols = sb("cols", [P, 72])
        cond = sb("cond", [P, 16])
        pickv = sb("pickv", [2, 2, P])
        rope = sb("rope", [P, LAT, 2, HD])
        modcol = sb("modcol", [P, 4, KD, 2])
        modA = sb("modA", [P, 2, KD, 2])
        ss = sb("ss", [P, 4])
        rst = sb("rst", [P, 4])
        st = sb("st", [P, 72])
        nw = sb("nw", [P, 4, 40])
        nm = sb("nm", [P, 4])
        rs = sb("rs", [P, 32])
        rr = sb("rr", [P, 8])
        lam2 = sb("lam2", [P, 8])
        layerE = sb("layerE", [P, 1])
        gcol = sb("gcol", [P, KD])
        iota = sb("iota", [P, 16])
        rel = sb("rel", [33, DH])
        bfc = sb("bfc", [FH, 1])
        picks = sb("picks", [P, LAT, PICKS], U32)
        gates = sb("gates", [P, LAT, PICKS])
        dots = sb("dots", [P, LAT, PICKS])
        d16 = sb("d16", [P, ROWS])
        pick_now = sb("pick_now", [P, 2, HALF], U32)
        bias_rows = nc.dram_tensor("bias_rows", [DH, P, REL], F32).ap()

        h1T = big[:, :].rearrange("p (b t) -> p b t", t=TILES * P)
        modrow = big[0:2, 0:6 * D]
        bmod = big[0:2, 6 * D:12 * D]
        z = big[:, 0:3072].rearrange("p (t n) -> p t n", t=TILES)
        ug = big[:, 3072:7168].rearrange("p (a t n) -> p a t n", a=2, t=TILES)
        gm = big[:, 7168:9216].rearrange("p (t n) -> p t n", t=TILES)
        qT = big[:, 9216:11264].rearrange("p (b t) -> p b t", b=4)
        pr = big[:, 11264:12800].rearrange("p (a n) -> p a n", a=3)
        prT = big[:, 12800:14336].rearrange("p (a n) -> p a n", a=3)
        tA = big[:, 14336:14976]
        tB = big[:, 14976:15616]
        qn = big[:, 15616:16384]
        gq = wide[:, 0:640]
        onehot = kT[0:33, 0, 0:REL]
        brow = kT[0:DH, 1, 0:REL]

        dfT = big[:, 0:4096].rearrange("p (a b t) -> p a b t", a=4, b=4)
        dfv = big[:, 4096:6144].rearrange("p (a t n) -> p a t n", a=2, t=LAT)
        sig = big[:, 6144:10240].rearrange("p (a b t) -> p a b t", a=2, b=KD)
        yy = big[:, 10240:12288].rearrange("p (a t n) -> p a t n", a=2, t=LAT)
        lg = big[:, 12288:13312].rearrange("p (a n) -> p a n", a=4)
        pb = big[:, 13312:14336].rearrange("p (a n) -> p a n", a=4)
        wd = big[:, 14336:14848].rearrange("p (a n) -> p a n", a=2)
        pbT = big[:, 14848:15616].rearrange("p (a n) -> p a n", a=3)
        tM = big[:, 15616:16128].rearrange("p (a n) -> p a n", a=2)
        h2 = hT[:, 0:4, :].rearrange("p a (b t) -> p (a b) t", b=2)
        yT = hT[:, 4:8, :].rearrange("p a (b t) -> p (a b) t", b=2)
        mT = xn[:, :, :].rearrange("p a (b t) -> p (a b) t", b=4)
        qq = big[:, 0:4096].rearrange("p (a t) -> p a t", a=2 * PH)
        sc = big[:, 4096:8192].rearrange("p (t a n) -> p t a n", t=LAT, a=2 * PH)
        w1 = big[:, 8192:10240]
        w2 = big[:, 10240:12288]
        tv = big[:, 14336:14592].rearrange("p (a n) -> p a n", n=16)
        tif = big[:, 14592:14848].rearrange("p (a n) -> p a n", n=16)
        bv = big[:, 14848:14976].rearrange("p (a n) -> p a n", n=16)
        bf = big[:, 14976:15232].rearrange("p (c a n) -> p c a n", c=2, n=16)
        ei = big[:, 15232:15488].rearrange("p (c n) -> p c n", c=2)
        ti = big[:, 15488:15744].bitcast(U32).rearrange("p (a n) -> p a n", n=16)
        bp = big[:, 15744:15872].bitcast(U32).rearrange("p (a n) -> p a n", n=16)
        bi = big[:, 15872:16128].bitcast(U32).rearrange("p (c a n) -> p c a n", c=2, n=16)
        expert = big[:, :].rearrange("p (s n) -> p s n", s=ROWS)
        diag = hT[:, 0:3, :].rearrange("p a (b n) -> p (a b) n", n=P)
        junk = [xn[:, 0, :], hT[:, 6:8, :].rearrange("p a n -> p (a n)")]
        acc = xn[:, 1, :]
        ttok = gate[:, 0, :, :]
        bias = gate[:, 1, 0, :].rearrange("p (h n) -> p h n", h=DH)
        mask = gate[:, 1, 1, 0:SEQ]
        sk = wsp[:, 0:2, :]
        skT = wsT[:, 0:2, :]
        wff = kT[:, 0, 0:64].rearrange("p (k n) -> p k n", k=KD)
        lamrow = kT[:, 0, 64:320].rearrange("p (a n) -> p a n", a=4)
        lamp = kT[:, 0, 320:448].rearrange("p (a n) -> p a n", a=2)
        subln = ggain[:, 0:P]
        fcv = x[0:FH, 2:4, :].rearrange("p a (b n) -> p (a b) n", n=SEQ)

        bank = [ctx.enter_context(nc.psum_tensor(f"bank{i}", [P, 512], F32)) for i in range(8)]

        FIRST = ["col", "rel", "mod", "modT", "gate", "xTv", "xTs", "z", "ws", "qkT", "sp", "s",
                 "pT", "o", "mT", "y", "f1", "f2"]
        SECOND = {"BxTv": 4, "BxTs": 4, "proj": 36, "ff": 1, "sk": 1, "Bs": 32, "BpT": 24, "Bo": 4,
                  "yT": 4, "mg": 8, "By": 4, "q2": 16, "sc": 8, "acc": 2}
        filled = {f: sem("filled_" + f) for f in FIRST + list(SECOND)}
        emptied = {f: sem("emptied_" + f) for f in FIRST + list(SECOND)}
        landed = [sem(f"chunk_landed{i}") for i in range(SLOTS)]
        chunk_used = sem("chunk_used")
        consts_in, x_in, bmod_in, wide_in = sem("consts_in"), sem("x_in"), sem("bmod_in"), sem("wide_in")
        bias_out, bias_in, final_in = sem("bias_out"), sem("bias_in"), sem("final_in")
        modA_ready = sem("modA_ready")
        xn_ready, qn_ready, vn_ready = sem("xn_ready"), sem("qn_ready"), sem("vn_ready")
        nm_ready, pv_done, mix_ready = sem("nm_ready"), sem("pv_done"), sem("mix_ready")
        layer_done = sem("layer_done")
        result_ready, out_done = sem("result_ready"), sem("out_done")
        row_in = [sem(f"row_in{i}") for i in range(ROWS)]
        VROWS = [j for j in range(ROWS) if j % 4 == 3]
        PROWS = [j for j in range(ROWS) if j % 4 != 3]
        NV, NP, RUN = len(VROWS), len(PROWS), PICKS // ROWS
        PER = {"Bxn": 4, "ff_z": 1, "ff_e": 1, "c_ready": 1, "p_ready": 32, "w_ready": 8,
               "Bpv": 24, "y_ready": 4, "mT_ready": 8, "lam_z": 1, "lam_e": 1, "gate_z": 2,
               "gate_e": 2, "picked": 2, "dotted": 2, "acted": 2, "weighed": 2, "acc_ready": 2,
               "small_in": 6 * 16, "gain_in": 16, "picks_now": 2 * RUN * 2 * LAT,
               "free_v": LAT * (PICKS + NV * RUN), "free_p": LAT * NP * RUN,
               "diag_ready": LAT * NP * RUN}
        S = {f: sem(f) for f in PER}
        PER |= SECOND | {"layer_done": 1, "row_in": 16 * RUN * 2 * LAT}
        PER |= {f"landed{s}": 16 * len(range(s, CHUNKS_B, SLOTS)) for s in range(SLOTS)}

        block = ctx.enter_context(nc.Block())

        class Side:

            def __init__(self):
                self.layer, self.n, self.held = None, {}, [None] * 8

            def at(self, n, name):
                return n if self.layer is None else self.layer * PER[name] + n

            def next(self, fam):
                self.n[fam] = self.n.get(fam, 0) + 1
                return self.at(self.n[fam], fam)

            def freed(self, b):
                if self.held[b] is None:
                    return (consts_in, 16 * CONSTS) if self.layer is None else (layer_done, self.layer + 1)
                old, n = self.held[b]
                return emptied[old], self.at(n, old)

            def claim(self, fam, b):
                self.n[fam] = self.n.get(fam, 0) + 1
                self.held[b] = (fam, self.n[fam])
                return bank[b]

            def new_layer(self, layer):
                self.layer, self.n, self.held = layer, {}, [None] * 8

        GROUPS, n = [], 0
        for kind, heads, maps in ((0, DH, 2), (1, FH, 1)):
            for qt in range(LAT):
                for h in range(heads):
                    GROUPS.append((kind, qt, h, n))
                    n += maps
        GROUP_OF = [g for g, (kind, *_) in enumerate(GROUPS) for _ in range(2 - kind)]
        LAST_GROUP = [3, 7, 15, 23]

        @block.sync
        def _(sp):
            count = 0

            def put(src, slot):
                k, w = src.shape[1], src.shape[2]
                dst = ring[:, slot, 0:k * w].rearrange("p (k n) -> p k n", k=k)
                sp.dma_start(dst, src).then_inc(landed[slot], 16)

            def chunk(src):
                nonlocal count
                if count >= SLOTS:
                    sp.wait_ge(chunk_used, count - SLOTS + 1)
                put(src, count % SLOTS)
                count += 1

            for layer in range(LAYERS):
                w = A["w_mod"][layer].rearrange("(k p) n -> p k n", p=P)
                for c in range(12):
                    chunk(w[:, :, c * CH:(c + 1) * CH])
                w = A["w_in"][layer].rearrange("(k p) n -> p k n", p=P)
                for a, b in ((0, 512), (512, 768), (768, 1280), (1280, 1792)):
                    chunk(w[:, :, a:b])
                w = A["w_out"][layer].rearrange("(k p) n -> p k n", p=P)
                for c in range(2):
                    chunk(w[:, :, c * CH:(c + 1) * CH])
                w = A["w_ff1"][layer].rearrange("(k p) n -> p k n", p=P)
                for c in range(8):
                    chunk(w[:, :, c * CH:(c + 1) * CH])
                w = A["w_ff2"][layer].rearrange("(c k p) n -> c p k n", p=P, k=KD)
                for h in range(2):
                    for c in range(4):
                        chunk(w[c, :, :, h * CH:(h + 1) * CH])
            assert count == CHUNKS_A

            with sp.Fori(0, LAYERS) as l:
                c = 0

                def chunk_of_layer(src):
                    nonlocal c
                    sp.wait_ge(chunk_used, l * CHUNKS_B + CHUNKS_A + max(0, c - SLOTS + 1))
                    sp.nop(nofuse=True)
                    put(src, c % SLOTS)
                    c += 1

                def of_layer(name):
                    w = A[name].rearrange("l (k p) n -> l p k n", p=P)
                    return w[bass.ds(l, 1)].rearrange("l p k n -> (l p) k n")

                w = of_layer("w_in_2")
                for a in (0, 512, 1024, 1536, 2048, 2560, 3080, 3592, 4104, 4616):
                    chunk_of_layer(w[:, :, a:a + CH])
                chunk_of_layer(of_layer("w_diff_o_2"))
                chunk_of_layer(of_layer("w_fox_o_2"))
                for name, m in (("w_out_2", 2), ("w_query_2", 4)):
                    w = of_layer(name)
                    for i in range(m):
                        chunk_of_layer(w[:, :, i * CH:(i + 1) * CH])
                assert c == CHUNKS_B
            sp.wait_ge(result_ready, 1)
            sp.dma_start(out.rearrange("o (t p) n -> (o p) t n", p=P), xn[:, :, :]).then_inc(out_done, 16)
            sp.wait_ge(out_done, 16)

        @block.gpsimd
        def _(pool):
            me = Side()

            def load(dst, src, s):
                pool.dma_start(dst, src).then_inc(s, 16)

            load(eye[:, :], A["eye"], consts_in)
            load(rows[0:8, :], A["c"].rearrange("a (k p) -> (a k) p", p=P), consts_in)
            load(rows[8:16, :], A["c_ctx"].rearrange("(k p) -> k p", p=P), consts_in)
            for i, name in enumerate(("norm1_g", "norm2_g", "norm1_g_2")):
                load(rows[16 + 16 * i:32 + 16 * i, :], A[name].rearrange("l (k p) -> (l k) p", p=P), consts_in)
            load(rows[64:72, :], A["b_spatial"].rearrange("l g p -> (l g) p"), consts_in)
            load(onehot, A["onehot"], consts_in)
            load(rel[0:32, :], A["rel_bias_2"], consts_in)
            load(rel[32:33, :], A["ones4"], consts_in)
            load(pickv[:, :, :], A["pickv"].rearrange("a (b p) -> a b p", b=2), consts_in)
            load(rope[:, :, :, :], A["rope"].rearrange("(t p) (a n) -> p t a n", p=P, a=2), consts_in)
            load(iota[:, :], A["iota16"].broadcast_to([P, 16]), consts_in)
            load(x[:, 0:2, :], A["x"].rearrange("o (t p) n -> (o p) t n", p=P), x_in)
            load(x[:, 2:4, :], A["ctx"].rearrange("o (t p) n -> (o p) t n", p=P), x_in)
            for layer in range(LAYERS):
                if layer:
                    pool.wait_ge(filled["f2"], 2 * TILES)
                load(bmod, A["b_mod"][layer:layer + 1, :].broadcast_to([2, 6 * D]), bmod_in)
                for a in range(AH + AKV):
                    g = A["q_norm_g" if a < AH else "k_norm_g"][layer:layer + 1]
                    load(gq[:, a * HD:(a + 1) * HD], g.broadcast_to([P, HD]), wide_in)
                load(ggain[:, :], A["gmlp_norm_g"][layer:layer + 1].broadcast_to([P, GW]), wide_in)
                load(wsp[:, :, :], A["w_spatial"][layer].rearrange("g p q -> p g q"), wide_in)
                if layer == 0:
                    pool.wait_ge(emptied["rel"], 1)
                    load(bias_rows, spread(brow, 1, P), bias_out)
            pool.wait_ge(bias_out, 16)
            pool.wait_ge(layer_done, 1)
            load(bias, bass.AP(tensor=bias_rows.tensor, offset=P - 1, ap=[[REL - 1, P], [P * REL, DH], [1, SEQ]]), bias_in)
            load(mask, A["mask"], bias_in)
            pool.sem_inc(S["free_v"], ROWS)
            pool.sem_inc(S["free_p"], NP)

            with pool.Fori(0, LAYERS) as l:
                me.new_layer(l)
                pool.wait_ge(layer_done, me.at(1, "layer_done"))

                def of_layer(name):
                    return A[name][bass.ds(l, 1)]

                load(wff, A["w_in_2"].rearrange("l (k p) n -> l p k n", p=P)[bass.ds(l, 1), :, :, FFCOL:FFCOL + FH]
                     .rearrange("l p k n -> (l p) k n"), S["small_in"])
                load(bfc[:, :], of_layer("b_forget_2").rearrange("l (h o) -> (l h) o", o=1), S["small_in"])
                load(lamrow, of_layer("diff_lambda_2").rearrange("l a n -> l (a n)").broadcast_to([P, 4 * HD])
                     .rearrange("p (a n) -> p a n", a=4), S["small_in"])
                load(lam2[:, 0:2], of_layer("lam").broadcast_to([P, 2]), S["small_in"])
                load(subln, of_layer("diff_subln_g_2").broadcast_to([P, P]), S["small_in"])
                load(sk, A["sub_keys_2"].rearrange("l a n d -> l n a d")[bass.ds(l, 1)]
                     .rearrange("l n a d -> (l n) a d"), S["small_in"])
                load(wide[:, :], of_layer("norm2_g_2").broadcast_to([P, D]), S["gain_in"])

                pool.wait_ge(S["picked"], me.at(LAT, "picked"))
                for t in range(LAT):
                    for v, name in enumerate(("expert_u_2", "expert_v_2")):
                        table = A[name].rearrange("l e n -> (l e) n")
                        base_v = t * (PICKS + NV * RUN) + v * PICKS
                        base_p = t * NP * RUN
                        if v:
                            pool.wait_ge(S["free_v"], me.at(ROWS + base_v - HALF, "free_v"))
                        elif t:
                            pool.wait_ge(S["free_v"], me.at(ROWS + base_v - NV // 2, "free_v"))
                            pool.wait_ge(S["free_p"], me.at(NP + base_p - NP // 2, "free_p"))
                        pool.nop(nofuse=True)
                        with pool.Fori(0, RUN) as i:
                            for half in range(2):
                                rate = NV if v else ROWS
                                pool.wait_ge(S["free_v"], me.at(i * rate + ROWS + base_v - rate + rate // 2 * (half + 1), "free_v"))
                                if v:
                                    pool.wait_ge(S["free_p"], me.at(i * NP + base_p + NP // 2 * (half + 1), "free_p"))
                                elif half:
                                    pool.wait_ge(S["free_p"], me.at(NP + base_p, "free_p"))
                                pool.tensor_copy(pick_now[:, half, :],
                                                 picks[:, t, bass.ds(i * ROWS + half * HALF, HALF)]
                                                 ).then_inc(S["picks_now"], 1)
                                pool.wait_ge(S["picks_now"], me.at(i * 2 + (2 * t + v) * 2 * RUN + half + 1, "picks_now"))
                                pool.nop(nofuse=True)
                                for j in range(HALF):
                                    s = half * HALF + j
                                    pool.indirect_dma_start(
                                        out=expert[:, s, :], out_offset=None, in_=table,
                                        in_offset=bass.IndirectOffsetOnAxis(ap=pick_now[:, half, j:j + 1], axis=0),
                                    ).then_inc(row_in[s], 16)
            pool.wait_ge(layer_done, 1 + LAYERS)
            load(wide[:, :], A["final_norm_g_2"].rearrange("(o n) -> o n", o=1).broadcast_to([P, D]), final_in)

        @block.tensor
        def _(pe):
            me = Side()
            chunks = 0

            def next_chunk():
                nonlocal chunks
                slot, n = chunks % SLOTS, chunks // SLOTS + 1
                if me.layer is None:
                    pe.wait_ge(landed[slot], 16 * n)
                else:
                    before = len(range(slot, CHUNKS_A, SLOTS))
                    pe.wait_ge(landed[slot], me.at(16 * (n + before), f"landed{slot}"))
                chunks += 1
                return slot

            def fill(fam, ins):
                ins.then_inc(filled[fam], 1)

            read = 0

            def used(m=1):
                nonlocal read
                read += m

            def tell(ins):
                nonlocal read
                if read:
                    ins.then_inc(chunk_used, read)
                    read = 0

            def norm_T(fams, source, ready, tiles, name=None, first=0):
                for t in range(tiles):
                    pe.wait_ge(ready, me.at(first + t + 1, name))
                    for half, fam in enumerate(fams):
                        pe.wait_ge(*me.freed((2 * t + half) % 8))
                        o = me.claim(fam, (2 * t + half) % 8)
                        for b in range(4):
                            k = 4 * half + b
                            last = nc.tensor.transpose(o[:, b * P:(b + 1) * P], source(t)[:, k * P:(k + 1) * P], eye[:, :])
                            if b == 0:
                                tell(last)
                        fill(fam, last)

            def product(o, lhs, rhs):
                n = len(lhs)
                last = None
                for k in range(n):
                    last = nc.tensor.matmul(o, lhs[k], rhs[k], start=k == 0, stop=k == n - 1)
                    if k == 0 and n == KD:
                        tell(last)
                return last

            pe.wait_ge(consts_in, 16 * CONSTS)
            pe.wait_ge(*me.freed(0))
            fill("col", nc.tensor.transpose(me.claim("col", 0)[:, 0:72], rows[:, :], eye[0:72, 0:72]))
            pe.wait_ge(*me.freed(1))
            fill("rel", nc.tensor.matmul(me.claim("rel", 1)[0:DH, 0:REL], rel[:, :], onehot, start=True, stop=True))
            pe.wait_ge(emptied["col"], me.at(1, "col"))
            units, tiles_before = 0, 0
            for layer in range(LAYERS):
                NT = TILES if layer == 0 else LAT
                for c in range(12):
                    slot = next_chunk()
                    pe.wait_ge(*me.freed(c % 8))
                    o = me.claim("mod", c % 8)
                    last = product(o[0:2, :], [cond[:, k::KD] for k in range(KD)],
                                   [ring[:, slot, k * CH:(k + 1) * CH] for k in range(KD)])
                    fill("mod", last)
                    used()
                pe.wait_ge(emptied["mod"], me.at(me.n["mod"], "mod"))
                pe.wait_ge(*me.freed(4))
                o = me.claim("modT", 4)
                for i, kind in enumerate((0, 1, 3, 4)):
                    for k in range(KD):
                        at = (i * KD + k) * 2
                        last = nc.tensor.transpose(o[:, at:at + 2], modrow[:, kind * D + k * P:kind * D + (k + 1) * P],
                                                   eye[0:2, 0:2])
                        if at == 0:
                            tell(last)
                fill("modT", last)
                b = 5
                for g, kind in enumerate((2, 5)):
                    for v in range(2 if layer == 0 else 1):
                        for half in range(2):
                            pe.wait_ge(*me.freed(b % 8))
                            o = me.claim("gate", b % 8)
                            at = kind * D + half * CH
                            fill("gate", nc.tensor.matmul(o[:, :], pickv[:, v, :], modrow[:, at:at + CH],
                                                          start=True, stop=True))
                            b += 1
                norm_T(("xTv", "xTs"), lambda t: xn[:, t % 2, :], xn_ready, TILES, first=tiles_before)
                tiles_before += TILES
                pe.wait_ge(emptied["xTv"], me.at(me.n["xTv"], "xTv"))
                pe.wait_ge(emptied["xTs"], me.at(me.n["xTs"], "xTs"))
                b = 0
                for c in range(4):
                    slot, w = next_chunk(), (512, 256, 512, 512)[c]
                    for t in range(TILES if c == 1 else NT):
                        pe.wait_ge(*me.freed(b % 8))
                        o = me.claim("z", b % 8)
                        last = product(o[:, 0:w], [hT[:, k, t * P:(t + 1) * P] for k in range(KD)],
                                       [ring[:, slot, k * w:(k + 1) * w] for k in range(KD)])
                        fill("z", last)
                        b += 1
                    used()
                pe.wait_ge(wide_in, 12 * 16 * (layer + 1))
                pe.wait_ge(*me.freed(b % 8))
                o = me.claim("ws", b % 8)
                for g in range(4):
                    last = nc.tensor.transpose(o[:, g * P:(g + 1) * P], wsp[:, g, :], eye[:, :])
                    if g == 0:
                        tell(last)
                fill("ws", last)
                b += 1
                for t in range(TILES):
                    pe.wait_ge(qn_ready, layer * TILES + t + 1)
                    for a, m in ((0, 4), (4, 2)):
                        if a == 0 and t >= NT:
                            continue
                        pe.wait_ge(*me.freed(b % 8))
                        o = me.claim("qkT", b % 8)
                        for i in range(m):
                            last = nc.tensor.transpose(o[:, i * P:(i + 1) * P], qn[:, (a + i) * P:(a + i + 1) * P], eye[:, :])
                        fill("qkT", last)
                        b += 1
                pe.wait_ge(emptied["ws"], me.at(me.n["ws"], "ws"))
                for t in range(NT):
                    pe.wait_ge(vn_ready, (TILES if layer else 0) + t + 1)
                    pe.wait_ge(*me.freed(b % 8))
                    o = me.claim("sp", b % 8)
                    for g in range(4):
                        last = nc.tensor.matmul(o[:, g * P:(g + 1) * P], wsT[:, g, :], ug[:, 1, t, g * P:(g + 1) * P],
                                                start=True, stop=True)
                    fill("sp", last)
                    b += 1
                pe.wait_ge(emptied["qkT"], me.at(me.n["qkT"], "qkT"))
                N = NT * AH
                for n in range(N + 2):
                    if n < N:
                        t, h = divmod(n, AH)
                        a = HD * (h % 2)
                        lo, hi = (0, 512) if t < LAT else (256, 512)
                        pe.wait_ge(*me.freed(n % 3))
                        o = me.claim("s", n % 3)
                        fill("s", nc.tensor.matmul(o[:, 0:hi - lo], qT[a:a + HD, h // 2, t * P:(t + 1) * P],
                                                   kT[a:a + HD, h // 4, lo:hi], start=True, stop=True))
                    if 1 <= n <= N:
                        m = n - 1
                        pe.wait_ge(emptied["s"], me.at(units + m + 1, "s"))
                        pe.wait_ge(*me.freed(3 + m % 3))
                        o = me.claim("pT", 3 + m % 3)
                        for i in range(4 if m // AH < LAT else 2):
                            last = nc.tensor.transpose(o[:, i * P:(i + 1) * P], pr[:, m % 3, i * P:(i + 1) * P], eye[:, :])
                        fill("pT", last)
                    if n >= 2:
                        m = n - 2
                        t, h = divmod(m, AH)
                        pe.wait_ge(emptied["pT"], me.at(units + m + 1, "pT"))
                        if h == 0:
                            pe.wait_ge(*me.freed(6 + t % 2))
                            o_bank = me.claim("o", 6 + t % 2)
                        blocks = range(4) if t < LAT else range(2, 4)
                        v0 = QW + KVW + HD * (h // 4)
                        last = product(o_bank[:, h * HD:(h + 1) * HD],
                                       [prT[:, m % 3, (i - blocks[0]) * P:(i - blocks[0] + 1) * P] for i in blocks],
                                       [z[:, i, v0:v0 + HD] for i in blocks])
                        last.then_inc(pv_done, 1)
                units += N
                for t in range(NT):
                    pe.wait_ge(mix_ready, (TILES if layer else 0) + t + 1)
                    for half, src in enumerate((z[:, t, 0:512], gm[:, t, :])):
                        pe.wait_ge(*me.freed((2 * t + half) % 8))
                        o = me.claim("mT", (2 * t + half) % 8)
                        for i in range(4):
                            last = nc.tensor.transpose(o[:, i * P:(i + 1) * P], src[:, i * P:(i + 1) * P], eye[:, :])
                        fill("mT", last)
                pe.wait_ge(emptied["mT"], me.at(me.n["mT"], "mT"))
                for half in range(2):
                    slot = next_chunk()
                    for t in range(NT):
                        pe.wait_ge(*me.freed((half * NT + t) % 8))
                        o = me.claim("y", (half * NT + t) % 8)
                        last = product(o[:, :], [hT[:, k, t * P:(t + 1) * P] for k in range(KD)],
                                       [ring[:, slot, k * CH:(k + 1) * CH] for k in range(KD)])
                        fill("y", last)
                    used()
                norm_T(("xTv", "xTs"), lambda t: xn[:, t % 2, :], xn_ready, NT, first=tiles_before)
                tiles_before += NT
                pe.wait_ge(emptied["xTv"], me.at(me.n["xTv"], "xTv"))
                pe.wait_ge(emptied["xTs"], me.at(me.n["xTs"], "xTs"))
                for c in range(8):
                    slot = next_chunk()
                    for i in range(4):
                        pe.wait_ge(*me.freed((c * 4 + i) % 8))
                        o = me.claim("f1", (c * 4 + i) % 8)
                        last = product(o[:, 0:NT * P],
                                       [ring[:, slot, k * CH + i * P:k * CH + (i + 1) * P] for k in range(KD)],
                                       [hT[:, k, 0:NT * P] for k in range(KD)])
                        fill("f1", last)
                    used()
                for half in range(2):
                    outs = []
                    for t in range(NT):
                        pe.wait_ge(*me.freed(half * NT + t))
                        outs.append(me.claim("f2", half * NT + t))
                    for c in range(4):
                        slot = next_chunk()
                        if half == 0:
                            pe.wait_ge(emptied["f1"], me.at(me.n["f1"] - 32 + 8 * (c + 1), "f1"))
                        for t in range(NT):
                            for k in range(KD):
                                last = nc.tensor.matmul(outs[t][:, :], h1T[:, c * KD + k, t * P:(t + 1) * P],
                                                        ring[:, slot, k * CH:(k + 1) * CH],
                                                        start=c == 0 and k == 0, stop=c == 3 and k == KD - 1)
                                if k == 0:
                                    tell(last)
                            if c == 3:
                                fill("f2", last)
                        used()

            tell(pe.drain())

            with pe.Fori(0, LAYERS) as l:
                me.new_layer(l)
                chunks = 0
                pe.wait_ge(layer_done, me.at(1, "layer_done"))
                norm_T(("BxTv", "BxTs"), lambda t: xn[:, t, :], S["Bxn"], LAT, name="Bxn")
                pe.wait_ge(emptied["BxTv"], me.at(2, "BxTv"))
                pe.wait_ge(emptied["BxTs"], me.at(2, "BxTs"))
                b = 4

                def columns(fam, slot, block, w=CH):
                    nonlocal b
                    pe.wait_ge(*me.freed(b % 8))
                    o = me.claim(fam, b % 8)
                    last = product(o[:, 0:SEQ], [ring[:, slot, k * w + block * P:k * w + (block + 1) * P] for k in range(KD)],
                                   [h2[:, k, :] for k in range(KD)])
                    fill(fam, last)
                    b += 1
                    return last

                for c in range(6):
                    slot = next_chunk()
                    if c % 3 == 2:
                        for t in range(LAT):
                            pe.wait_ge(*me.freed(b % 8))
                            o = me.claim("proj", b % 8)
                            last = product(o[:, :], [h2[:, k, t * P:(t + 1) * P] for k in range(KD)],
                                           [ring[:, slot, k * CH:(k + 1) * CH] for k in range(KD)])
                            fill("proj", last)
                            b += 1
                    else:
                        for i in range(4):
                            last = columns("proj", slot, i)
                    used()
                pe.wait_ge(S["small_in"], me.at(PER["small_in"], "small_in"))
                pe.wait_ge(*me.freed(b % 8))
                o = me.claim("ff", b % 8)
                b += 1
                fill("ff", product(o[0:FH, 0:SEQ], [wff[:, k, :] for k in range(KD)], [h2[:, k, :] for k in range(KD)]))
                for c in range(4):
                    slot = next_chunk()
                    for i in range(4):
                        last = columns("proj", slot, i)
                    used()
                pe.wait_ge(*me.freed(b % 8))
                o = me.claim("sk", b % 8)
                b += 1
                for i in range(2):
                    last = nc.tensor.transpose(o[:, i * P:(i + 1) * P], sk[:, i, :], eye[:, :])
                    if i == 0:
                        tell(last)
                fill("sk", last)
                pe.wait_ge(emptied["proj"], me.at(20, "proj"))
                for g in range(len(GROUPS) + 3):
                    if g < len(GROUPS):
                        kind, qt, h, s = GROUPS[g]
                        nk = (qt + 1) * P
                        for m in range(2 - kind):
                            if kind == 0:
                                a, blk = HD * m, h
                            else:
                                a, blk = HD * (h % 2), h // 2
                            pe.wait_ge(*me.freed((s + m) % 4))
                            o = me.claim("Bs", (s + m) % 4)
                            last = nc.tensor.matmul(o[:, 0:nk], dfT[a:a + HD, 2 * kind, blk, qt * P:(qt + 1) * P],
                                                    dfT[a:a + HD, 2 * kind + 1, blk, 0:nk], start=True, stop=kind == 0)
                            if kind:
                                if s == 16:
                                    pe.wait_ge(S["c_ready"], me.at(1, "c_ready"))
                                one = eye[0:FH, h:h + 1]
                                nc.tensor.matmul(o[:, 0:nk], fcv[:, 3, qt * P:(qt + 1) * P], one.broadcast_to([FH, nk]),
                                                 start=False, stop=False)
                                last = nc.tensor.matmul(o[:, 0:nk], one.broadcast_to([FH, P]), fcv[:, 4, 0:nk],
                                                        start=False, stop=True)
                            fill("Bs", last)
                    if 2 <= g < len(GROUPS) + 2:
                        kind, qt, h, s = GROUPS[g - 2]
                        if kind == 0:
                            pe.wait_ge(S["w_ready"], me.at(g - 1, "w_ready"))
                        else:
                            pe.wait_ge(S["p_ready"], me.at(s + 1, "p_ready"))
                        pe.wait_ge(*me.freed(4 + g % 2))
                        o = me.claim("BpT", 4 + g % 2)
                        src = pb[:, s % 4, :] if kind else wd[:, (g - 2) % 2, :]
                        for i in range(qt + 1):
                            last = nc.tensor.transpose(o[:, i * P:(i + 1) * P], src[:, i * P:(i + 1) * P], eye[:, :])
                        fill("BpT", last)
                    if g >= 3:
                        kind, qt, h, s = GROUPS[g - 3]
                        pe.wait_ge(emptied["BpT"], me.at(g - 2, "BpT"))
                        vw = 2 * HD if kind == 0 else HD
                        if h == 0:
                            pe.wait_ge(*me.freed(6 + qt))
                            o_bank = me.claim("Bo", 6 + qt)
                        last = product(o_bank[:, h * vw:(h + 1) * vw],
                                       [pbT[:, (g - 3) % 3, i * P:(i + 1) * P] for i in range(qt + 1)],
                                       [dfv[:, kind, i, h * vw:(h + 1) * vw] for i in range(qt + 1)])
                        last.then_inc(S["Bpv"], 1)
                for n in range(4):
                    kind, qt = divmod(n, 2)
                    pe.wait_ge(S["y_ready"], me.at(n + 1, "y_ready"))
                    pe.wait_ge(*me.freed(n))
                    o = me.claim("yT", n)
                    for i in range(4):
                        last = nc.tensor.transpose(o[:, i * P:(i + 1) * P], yy[:, kind, qt, i * P:(i + 1) * P], eye[:, :])
                    fill("yT", last)
                pe.wait_ge(emptied["yT"], me.at(4, "yT"))
                slots = [next_chunk(), next_chunk()]
                for j in range(KD):
                    pe.wait_ge(*me.freed(j % 8))
                    o = me.claim("mg", j % 8)
                    for a in range(2):
                        last = product(o[:, a * SEQ:(a + 1) * SEQ],
                                       [ring[:, slots[a], k * D + j * P:k * D + (j + 1) * P] for k in range(4)],
                                       [yT[:, 4 * a + k, :] for k in range(4)])
                    fill("mg", last)
                used(2)
                pe.wait_ge(S["mT_ready"], me.at(KD, "mT_ready"))
                for half in range(2):
                    slot = next_chunk()
                    for t in range(LAT):
                        pe.wait_ge(*me.freed(half * LAT + t))
                        o = me.claim("By", half * LAT + t)
                        last = product(o[:, :], [mT[:, k, t * P:(t + 1) * P] for k in range(KD)],
                                       [ring[:, slot, k * CH:(k + 1) * CH] for k in range(KD)])
                        fill("By", last)
                    used()
                norm_T(("BxTv", "BxTs"), lambda t: ttok[:, t, :], S["Bxn"], LAT, name="Bxn", first=LAT)
                pe.wait_ge(emptied["BxTv"], me.at(4, "BxTv"))
                pe.wait_ge(emptied["BxTs"], me.at(4, "BxTs"))
                for c in range(4):
                    slot = next_chunk()
                    for i in range(4):
                        last = columns("q2", slot, i)
                    used()
                pe.wait_ge(emptied["q2"], me.at(16, "q2"))
                for t in range(LAT):
                    for q in range(4):
                        pe.wait_ge(*me.freed((t * 4 + q) % 8))
                        o = me.claim("sc", (t * 4 + q) % 8)
                        for i in range(4):
                            last = nc.tensor.matmul(o[:, i * P:(i + 1) * P], qq[:, 4 * q + i, t * P:(t + 1) * P],
                                                    skT[:, i % 2, :], start=True, stop=True)
                            if i == 0:
                                tell(last)
                        fill("sc", last)
                for t in range(LAT):
                    outs = [bank[2 * t], bank[2 * t + 1]]
                    if t == 0:
                        pe.wait_ge(emptied["sc"], me.at(8, "sc"))
                    for half in range(2):
                        nc.tensor.matmul(outs[half][:, :], eye[:, :], x[:, t, half * CH:(half + 1) * CH],
                                         start=True, stop=False, skip_group_check=True)
                    with pe.Fori(0, RUN) as i:
                        for n, j in enumerate(PROWS):
                            pe.wait_ge(row_in[j], me.at(i * 16 + (2 * t + 1) * RUN * 16 + 16, "row_in"))
                            pe.wait_ge(S["diag_ready"], me.at(i * NP + t * NP * RUN + n + 1, "diag_ready"))
                            for half in range(2):
                                last = nc.tensor.matmul(outs[half][:, :], diag[:, n, :],
                                                        expert[:, j, half * CH:(half + 1) * CH],
                                                        start=False, stop=False, skip_group_check=True)
                            last.then_inc(S["free_p"], 1)
                    pe.wait_ge(S["acc_ready"], me.at(t + 1, "acc_ready"))
                    for half in range(2):
                        last = nc.tensor.matmul(outs[half][:, :], eye[:, :], acc[:, half * CH:(half + 1) * CH],
                                                start=False, stop=True, skip_group_check=True)
                    fill("acc", last)

        @block.scalar
        def _(act):
            me = Side()

            def free(fam, ins):
                ins.then_inc(emptied[fam], 1)

            act.wait_ge(filled["col"], me.next("col"))
            nc.scalar.activation(cols[:, :], bank[0][:, 0:72], ACT.Copy)
            free("col", nc.scalar.activation(cond[:, :], bank[0][:, 0:16], ACT.Silu))
            act.wait_ge(filled["rel"], me.next("rel"))
            free("rel", nc.scalar.activation(brow, bank[1][0:DH, 0:REL], ACT.Copy))
            units = 0
            for layer in range(LAYERS):
                NT = TILES if layer == 0 else LAT
                b = 5
                for g in range(2):
                    for v in range(2 if layer == 0 else 1):
                        for half in range(2):
                            act.wait_ge(filled["gate"], me.next("gate"))
                            free("gate", nc.scalar.activation(gate[:, g, v, half * CH:(half + 1) * CH],
                                                              bank[b % 8][:, :], ACT.Copy))
                            b += 1

                def norm_evac(which, tiles):
                    act.wait_ge(modA_ready, layer + 1)
                    for t in range(tiles):
                        act.wait_ge(filled["xTs"], me.next("xTs"))
                        for i in range(4):
                            k = 4 + i
                            last = nc.scalar.activation(hT[:, k, t * P:(t + 1) * P],
                                                        bank[(2 * t + 1) % 8][:, i * P:(i + 1) * P], ACT.Identity,
                                                        bias=modcol[:, 2 * which, k, t // 2:t // 2 + 1],
                                                        scale=modA[:, which, k, t // 2:t // 2 + 1])
                        free("xTs", last)

                norm_evac(0, TILES)
                b = 0
                for c in range(4):
                    for t in range(TILES if c == 1 else NT):
                        act.wait_ge(filled["z"], me.next("z"))
                        if c == 0:
                            o, i, f = z[:, t, 0:512], bank[b % 8][:, :], ACT.Copy
                        elif c == 1:
                            o, i, f = z[:, t, 512:768], bank[b % 8][:, 0:256], ACT.Copy
                        else:
                            o, i, f = ug[:, c - 2, t, :], bank[b % 8][:, :], ACT.Gelu_apprx_tanh
                        free("z", nc.scalar.activation(o, i, f))
                        b += 1
                act.wait_ge(filled["ws"], me.next("ws"))
                free("ws", nc.scalar.activation(wsT[:, :, :].rearrange("p g n -> p (g n)"), bank[b % 8][:, :], ACT.Copy))
                b += 1
                if layer == 0:
                    act.wait_ge(bias_out, 16)
                for t in range(TILES):
                    if t < NT:
                        act.wait_ge(filled["qkT"], me.next("qkT"))
                        free("qkT", nc.scalar.activation(
                            qT[:, :, t * P:(t + 1) * P], bank[b % 8][:, :].rearrange("p (a n) -> p a n", a=4),
                            ACT.Copy, scale=SCALE))
                        b += 1
                    act.wait_ge(filled["qkT"], me.next("qkT"))
                    free("qkT", nc.scalar.activation(
                        kT[:, :, t * P:(t + 1) * P], bank[b % 8][:, 0:256].rearrange("p (a n) -> p a n", a=2), ACT.Copy))
                    b += 1
                N = NT * AH
                for n in range(N + 1):
                    if n < N:
                        t, h = divmod(n, AH)
                        w = 512 if t < LAT else 256
                        act.wait_ge(nm_ready, units + n + 1)
                        if n >= 3:
                            act.wait_ge(filled["pT"], units + n - 2)
                        free("s", nc.scalar.activation(pr[:, n % 3, 0:w], bank[n % 3][:, 0:w], ACT.Exp,
                                                       bias=nm[:, n % 4:n % 4 + 1], accum_out=rs[:, n:n + 1]))
                    if n >= 1:
                        m = n - 1
                        w = 512 if m // AH < LAT else 256
                        act.wait_ge(filled["pT"], me.next("pT"))
                        if m >= 3:
                            act.wait_ge(pv_done, units + m - 2)
                        free("pT", nc.scalar.activation(prT[:, m % 3, 0:w], bank[3 + m % 3][:, 0:w], ACT.Copy))
                units += N
                for t in range(NT):
                    for half in range(2):
                        act.wait_ge(filled["mT"], me.next("mT"))
                        free("mT", nc.scalar.activation(
                            hT[:, 4 * half:4 * half + 4, t * P:(t + 1) * P],
                            bank[(2 * t + half) % 8][:, :].rearrange("p (a n) -> p a n", a=4), ACT.Copy))
                norm_evac(1, NT)

            with act.Fori(0, LAYERS) as l:
                me.new_layer(l)
                for t in range(LAT):
                    act.wait_ge(filled["BxTs"], me.next("BxTs"))
                    for i in range(4):
                        last = nc.scalar.activation(h2[:, 4 + i, t * P:(t + 1) * P],
                                                    bank[2 * t + 1][:, i * P:(i + 1) * P], ACT.Copy,
                                                    scale=gcol[:, 4 + i:5 + i])
                    free("BxTs", last)
                b = 4
                for c in range(6):
                    for i in range(2 if c % 3 == 2 else 4):
                        act.wait_ge(filled["proj"], me.next("proj"))
                        if c % 3 == 2:
                            ins = nc.scalar.activation(dfv[:, c // 3, i, :], bank[b % 8][:, :], ACT.Copy)
                        else:
                            ins = nc.scalar.activation(dfT[:, c // 3 * 2 + c % 3, i, :], bank[b % 8][:, 0:SEQ], ACT.Copy,
                                                       scale=SCALE if c % 3 == 0 else 1.0)
                        free("proj", ins)
                        b += 1
                b += 1
                for c in range(4):
                    for i in range(4):
                        act.wait_ge(filled["proj"], me.next("proj"))
                        free("proj", nc.scalar.activation(sig[:, c // 2, c % 2 * 4 + i, :], bank[b % 8][:, 0:SEQ],
                                                          ACT.Sigmoid))
                        b += 1
                act.wait_ge(filled["sk"], me.next("sk"))
                free("sk", nc.scalar.activation(skT.rearrange("p a n -> p (a n)"), bank[b % 8][:, 0:256], ACT.Copy))
                act.wait_ge(S["ff_z"], me.at(1, "ff_z"))
                nc.scalar.activation(fcv[:, 1, :], fcv[:, 1, :], ACT.Exp)
                act.drain()
                nc.scalar.activation(fcv[:, 2, :], fcv[:, 1, :], ACT.Ln, bias=1.0).then_inc(S["ff_e"], 1)
                act.wait_ge(S["lam_z"], me.at(1, "lam_z"))
                nc.scalar.activation(lam2[:, 4:6], lam2[:, 2:4], ACT.Exp).then_inc(S["lam_e"], 1)
                for g in range(len(GROUPS) + 2):
                    if g < len(GROUPS):
                        kind, qt, h, s0 = GROUPS[g]
                        nk = (qt + 1) * P
                        for s in range(s0, s0 + 2 - kind):
                            act.wait_ge(emptied["Bs"], me.at(s + 1, "Bs"))
                            if s >= 4:
                                old = GROUP_OF[s - 4]
                                if old < 2 * DH:
                                    act.wait_ge(S["w_ready"], me.at(old + 1, "w_ready"))
                                else:
                                    act.wait_ge(filled["BpT"], me.at(old + 1, "BpT"))
                            nc.scalar.activation(pb[:, s % 4, 0:nk], lg[:, s % 4, 0:nk], ACT.Exp, scale=-1.0,
                                                 bias=nm[:, s % 4:s % 4 + 1], accum_out=rs[:, s:s + 1]
                                                 ).then_inc(S["p_ready"], 1)
                    if g >= 2:
                        kind, qt, h, s = GROUPS[g - 2]
                        act.wait_ge(filled["BpT"], me.next("BpT"))
                        if g >= 5:
                            act.wait_ge(S["Bpv"], me.at(g - 4, "Bpv"))
                        w = (qt + 1) * P
                        free("BpT", nc.scalar.activation(pbT[:, (g - 2) % 3, 0:w], bank[4 + g % 2][:, 0:w], ACT.Copy))
                for n in range(4):
                    kind, qt = divmod(n, 2)
                    act.wait_ge(filled["yT"], me.next("yT"))
                    free("yT", nc.scalar.activation(yT[:, 4 * kind:4 * kind + 4, qt * P:(qt + 1) * P],
                                                    bank[n][:, :].rearrange("p (a n) -> p a n", a=4), ACT.Copy))
                for t in range(LAT):
                    act.wait_ge(filled["BxTs"], me.next("BxTs"))
                    free("BxTs", nc.scalar.activation(h2[:, 4:8, t * P:(t + 1) * P],
                                                      bank[2 * t + 1][:, :].rearrange("p (a n) -> p a n", a=4), ACT.Copy))
                b = 4 + 37 + 1
                for i in range(16):
                    act.wait_ge(filled["q2"], me.next("q2"))
                    free("q2", nc.scalar.activation(qq[:, i, :], bank[b % 8][:, 0:SEQ], ACT.Copy))
                    b += 1
                for t in range(LAT):
                    for q in range(4):
                        act.wait_ge(filled["sc"], me.next("sc"))
                        free("sc", nc.scalar.activation(sc[:, t, 4 * q:4 * q + 4, :],
                                                        bank[(t * 4 + q) % 8][:, :].rearrange("p (a n) -> p a n", a=4),
                                                        ACT.Copy))
                for t in range(LAT):
                    act.wait_ge(S["gate_z"], me.at(t + 1, "gate_z"))
                    nc.scalar.activation(gates[:, t, :], gates[:, t, :], ACT.Exp).then_inc(S["gate_e"], 1)
                for t in range(LAT):
                    act.wait_ge(S["dotted"], me.at(t + 1, "dotted"))
                    nc.scalar.activation(dots[:, t, :], dots[:, t, :], ACT.Gelu).then_inc(S["acted"], 1)
                    act.wait_ge(S["weighed"], me.at(t + 1, "weighed"))
                    with act.Fori(0, RUN) as i:
                        for n, j in enumerate(PROWS):
                            act.wait_ge(S["free_p"], me.at(i * NP + t * NP * RUN + n + 1, "free_p"))
                            nc.scalar.activation(diag[:, n, :], eye[:, :], ACT.Copy,
                                                 scale=dots[:, t, bass.ds(i * ROWS + j, 1)]).then_inc(S["diag_ready"], 1)

        @block.vector
        def _(dve):
            me = Side()
            v = nc.vector

            def flush():
                return dve.drain()

            def free(fam, ins):
                ins.then_inc(emptied[fam], 1)

            def rstd(o, i, n):
                w = i.shape[1]
                m, y, a, b = (nw[:, k, 0:w] for k in range(4))
                v.tensor_scalar(m, i, 1.0 / n, EPS, ALU.mult, ALU.add)
                flush()
                v.tensor_single_scalar(a.bitcast(U32), m.bitcast(U32), 1, ALU.logical_shift_right)
                flush()
                v.tensor_scalar(y.bitcast(U32), a.bitcast(U32), -1.0, float(0x5F3759DF), ALU.mult, ALU.add)
                flush()
                for step in range(3):
                    v.tensor_tensor(a, y, y, ALU.mult)
                    flush()
                    v.scalar_tensor_tensor(b, a, -0.5, m, ALU.mult, ALU.mult)
                    flush()
                    v.scalar_tensor_tensor(y if step < 2 else o, b, 1.5, y, ALU.add, ALU.mult)
                    flush()

            def row_stats(tiles):
                for t in range(tiles):
                    v.tensor_tensor_reduce(out=xn[:, t % 2, :], in0=x[:, t, :], in1=x[:, t, :], scale=1.0,
                                           scalar=0.0, op0=ALU.mult, op1=ALU.add, accum_out=ss[:, t:t + 1])
                    if t % 2:
                        flush()
                rstd(rst[:, 0:tiles], ss[:, 0:tiles], D)

            def row_norm(t, o):
                return v.tensor_scalar(o, x[:, t, :], rst[:, t:t + 1], None, ALU.mult)

            dve.wait_ge(emptied["col"], me.at(1, "col"))
            dve.wait_ge(x_in, 32)
            v.memset(st[:, :], 1.0)
            flush()
            transposed, units = 0, 0
            for layer in range(LAYERS):
                NT = TILES if layer == 0 else LAT
                dve.wait_ge(bmod_in, 16 * (layer + 1))
                for c in range(12):
                    dve.wait_ge(filled["mod"], me.next("mod"))
                    at = slice(c * CH, (c + 1) * CH)
                    free("mod", v.tensor_tensor(modrow[:, at], bank[c % 8][0:2, :], bmod[:, at], ALU.add))
                dve.wait_ge(filled["modT"], me.next("modT"))
                free("modT", v.tensor_copy(modcol[:, :, :, :].rearrange("p a k v -> p (a k v)"), bank[4][:, 0:64]))
                flush()
                for which in range(2):
                    g = cols[:, 16 + 16 * which + 8 * layer:24 + 16 * which + 8 * layer]
                    v.scalar_tensor_tensor(modA[:, which, :, :], modcol[:, 2 * which + 1, :, :], 1.0,
                                           spread(g, 2, 2), ALU.add, ALU.mult)
                flush().then_inc(modA_ready, 1)

                def norm(which, tiles):
                    nonlocal transposed
                    if transposed:
                        dve.wait_ge(filled["xTs"], transposed)
                    row_stats(tiles)
                    for t in range(tiles + 1):
                        if t < tiles:
                            if transposed + t - 2 >= 0:
                                dve.wait_ge(filled["xTs"], transposed + t - 1)
                            row_norm(t, xn[:, t % 2, :]).then_inc(xn_ready, 1)
                        if t >= 1:
                            dve.wait_ge(filled["xTv"], me.next("xTv"))
                            u = t - 1
                            for i in range(4):
                                last = v.tensor_scalar(hT[:, i, u * P:(u + 1) * P], bank[2 * u % 8][:, i * P:(i + 1) * P],
                                                       modA[:, which, i, u // 2:u // 2 + 1],
                                                       modcol[:, 2 * which, i, u // 2:u // 2 + 1], ALU.mult, ALU.add)
                            free("xTv", last)
                    transposed += tiles

                norm(0, TILES)
                zcount = (0 if layer == 0 else 16)
                dve.wait_ge(wide_in, 12 * 16 * (layer + 1))
                def heads(ap, t):
                    return ap[:, (0 if t < NT else AH) * HD:(AH + AKV) * HD].rearrange("p (h n) -> p h n", n=HD)

                def head_stats(t):
                    return st[:, t * 10 + (0 if t < NT else AH):t * 10 + 10]

                for t in range(TILES):
                    dve.wait_ge(emptied["z"], me.at(zcount + NT + t + 1, "z"))
                    a, zt = heads(tA, t), heads(z[:, t, :], t)
                    v.tensor_tensor(a, zt, zt, ALU.mult)
                    flush()
                    v.tensor_reduce(head_stats(t), a, AX.X, ALU.add)
                    flush()
                rstd(st[:, 0:40], st[:, 0:40], HD)
                for t in range(TILES):
                    a, b, zt = heads(tA, t), heads(tB, t), heads(z[:, t, :], t)
                    nh = a.shape[1]
                    v.tensor_tensor(a, zt, spread(head_stats(t), 2, HD), ALU.mult)
                    flush()
                    v.tensor_tensor(a, a, heads(gq, t), ALU.mult)
                    flush()
                    if t < LAT:
                        for off in range(0, HD, 16):
                            oth = off + 16 if off % 32 == 0 else off - 16
                            v.tensor_tensor(b[:, :, off:off + 16], a[:, :, oth:oth + 16],
                                            spread(rope[:, t, 1, off:off + 16], 1, nh), ALU.mult)
                        flush()
                        v.tensor_tensor(a, a, spread(rope[:, t, 0, :], 1, nh), ALU.mult)
                        flush()
                    if layer or t:
                        dve.wait_ge(filled["qkT"], 2 * TILES * layer + t + min(t, NT))
                    kq, kb = a[:, nh - AKV:nh, :], b[:, nh - AKV:nh, :]
                    qo = qn[:, 0:QW].rearrange("p (h n) -> p h n", n=HD)
                    ko = qn[:, QW:768].rearrange("p (j c n) -> p j c n", j=AKV, c=2)
                    if t < LAT:
                        v.tensor_tensor(qo, a[:, 0:AH, :], b[:, 0:AH, :], ALU.add)
                    elif t < NT:
                        v.tensor_copy(qo, a[:, 0:AH, :])
                    for c in range(2):
                        if t < LAT:
                            v.tensor_tensor(ko[:, :, c, :], kq, kb, ALU.add)
                        else:
                            v.tensor_copy(ko[:, :, c, :], kq)
                    flush().then_inc(qn_ready, 1)
                groups = lambda t: ug[:, 1, t, :].rearrange("p (g n) -> p g n", g=4)
                for t in range(NT):
                    dve.wait_ge(emptied["z"], me.at(zcount + NT + TILES + NT + t + 1, "z"))
                    v.tensor_reduce(st[:, 40 + 4 * t:44 + 4 * t], groups(t), AX.X, ALU.add)
                flush()
                v.tensor_scalar(st[:, 40:40 + 4 * NT], st[:, 40:40 + 4 * NT], 1.0 / P, None, ALU.mult)
                flush()
                for t in range(NT):
                    v.tensor_tensor(groups(t), groups(t), spread(st[:, 40 + 4 * t:44 + 4 * t], 2, P), ALU.subtract)
                    flush()
                    v.tensor_tensor(tA[:, 0:GW], ug[:, 1, t, :], ug[:, 1, t, :], ALU.mult)
                    flush()
                    v.tensor_reduce(st[:, 56 + 4 * t:60 + 4 * t], tA[:, 0:GW].rearrange("p (g n) -> p g n", g=4),
                                    AX.X, ALU.add)
                    flush()
                rstd(st[:, 56:56 + 4 * NT], st[:, 56:56 + 4 * NT], P)
                for t in range(NT):
                    v.tensor_tensor(groups(t), groups(t), spread(st[:, 56 + 4 * t:60 + 4 * t], 2, P), ALU.mult)
                    flush()
                    v.tensor_tensor(ug[:, 1, t, :], ug[:, 1, t, :], ggain[:, :], ALU.mult)
                    flush().then_inc(vn_ready, 1)
                b = NT * 3 + TILES + 1 + TILES + NT
                for t in range(NT):
                    dve.wait_ge(filled["sp"], me.next("sp"))
                    for g in range(4):
                        at = slice(g * P, (g + 1) * P)
                        c = 64 + 4 * layer + g
                        last = v.scalar_tensor_tensor(gm[:, t, at], bank[b % 8][:, at], cols[:, c:c + 1], ug[:, 0, t, at],
                                                      ALU.add, ALU.mult)
                    free("sp", last)
                    b += 1
                N = NT * AH

                def attn_out(t):
                    w = rs[:, t * AH:(t + 1) * AH]
                    dve.wait_ge(pv_done, units + (t + 1) * AH)
                    v.reciprocal(rr[:, :], w)
                    flush()
                    free("o", v.tensor_tensor(z[:, t, 0:512].rearrange("p (h n) -> p h n", n=HD),
                                              bank[6 + t % 2][:, :].rearrange("p (h n) -> p h n", n=HD),
                                              spread(rr[:, :], 2, HD), ALU.mult))
                    flush().then_inc(mix_ready, 1)

                for n in range(N):
                    t = n // AH
                    w = 512 if t < LAT else 256
                    if t and n % AH == 3:
                        attn_out(t - 1)
                    dve.wait_ge(filled["s"], me.next("s"))
                    if n >= 4:
                        dve.wait_ge(emptied["s"], me.at(units + n - 3, "s"))
                    v.tensor_reduce(nm[:, n % 4:n % 4 + 1], bank[n % 3][:, 0:w], AX.X, ALU.max, negate=True
                                    ).then_inc(nm_ready, 1)
                attn_out(NT - 1)
                units += N

                def gated(fam, which, at, banks):
                    for half in range(2):
                        for t in range(NT):
                            dve.wait_ge(filled[fam], me.next(fam))
                            cut = slice(half * CH, (half + 1) * CH)
                            tmp = xn[:, t % 2, 0:CH]
                            free(fam, v.tensor_tensor(tmp, bank[banks(half, t)][:, :], gate[:, which, t // 2, cut], ALU.mult))
                            flush()
                            v.tensor_tensor(x[:, t, cut], x[:, t, cut], tmp, ALU.add)
                            flush()

                gated("y", 0, 0, lambda half, t: (half * NT + t) % 8)
                norm(1, NT)
                for c in range(32):
                    dve.wait_ge(filled["f1"], me.next("f1"))
                    s = bank[c % 8][:, 0:NT * P]
                    v.tensor_scalar(xn[:, c % 2, 0:NT * P], s, 0.0, None, ALU.max)
                    flush()
                    free("f1", v.tensor_tensor(h1T[:, c, 0:NT * P], s, xn[:, c % 2, 0:NT * P], ALU.mult))
                gated("f2", 1, 0, lambda half, t: half * NT + t)
            v.memset(layerE[:, :], 0.0)
            flush().then_inc(layer_done, 1)

            dve.wait_ge(bias_in, 32)
            with dve.Fori(0, LAYERS) as l:
                me.new_layer(l)
                v.tensor_copy(gcol[:, :], cols[:, bass.ds(l * KD + 48, KD)])
                flush()
                row_stats(LAT)
                for t in range(LAT):
                    row_norm(t, xn[:, t, :]).then_inc(S["Bxn"], 1)
                for t in range(LAT):
                    dve.wait_ge(filled["BxTv"], me.next("BxTv"))
                    for i in range(4):
                        last = v.tensor_scalar(h2[:, i, t * P:(t + 1) * P], bank[2 * t][:, i * P:(i + 1) * P],
                                               gcol[:, i:i + 1], None, ALU.mult)
                    free("BxTv", last)
                dve.wait_ge(S["small_in"], me.at(PER["small_in"], "small_in"))
                v.tensor_tensor(lamp, lamrow[:, 0::2, :], lamrow[:, 1::2, :], ALU.mult)
                v.tensor_scalar(subln, subln, lam2[:, 1:2], None, ALU.mult)
                flush()
                v.tensor_reduce(lam2[:, 2:4], lamp, AX.X, ALU.add)
                flush().then_inc(S["lam_z"], 1)
                dve.wait_ge(filled["ff"], me.next("ff"))
                free("ff", v.tensor_scalar(fcv[:, 0, :], bank[(4 + 20) % 8][0:FH, 0:SEQ], bfc[:, :], None, ALU.add))
                flush()
                v.tensor_scalar(fcv[:, 1, :], fcv[:, 0, :], -1.0, None, ALU.mult)
                v.memset(fcv[:, 5, :], 1.0)
                flush()
                v.tensor_tensor(fcv[:, 1, :], fcv[:, 1, :], fcv[:, 0, :], ALU.min)
                flush().then_inc(S["ff_z"], 1)
                dve.wait_ge(S["ff_e"], me.at(1, "ff_e"))
                v.scalar_tensor_tensor(fcv[:, 2, :], fcv[:, 0, :], 0.0, fcv[:, 2, :], ALU.min, ALU.subtract)
                flush()
                v.tensor_tensor_scan(fcv[:, 3, :], fcv[:, 5, :], fcv[:, 2, :], 0.0, ALU.mult, ALU.add)
                flush()
                v.tensor_scalar(fcv[:, 4, :], fcv[:, 3, :], -1.0, None, ALU.mult)
                dve.wait_ge(S["lam_e"], me.at(1, "lam_e"))
                v.tensor_tensor(lam2[:, 6:7], lam2[:, 5:6], lam2[:, 4:5], ALU.subtract)
                flush().then_inc(S["c_ready"], 1)
                v.tensor_tensor(lam2[:, 7:8], lam2[:, 6:7], lam2[:, 0:1], ALU.subtract)
                flush()

                def heads_out(n):
                    kind, qt = divmod(n, 2)
                    dve.wait_ge(S["Bpv"], me.at(LAST_GROUP[n] + 1, "Bpv"))
                    y = yy[:, kind, qt, :]
                    if kind:
                        v.reciprocal(rr[:, :], rs[:, 16 + 8 * qt:24 + 8 * qt])
                        flush()
                        free("Bo", v.tensor_tensor(y.rearrange("p (h n) -> p h n", n=HD),
                                                   bank[6 + qt][:, :].rearrange("p (h n) -> p h n", n=HD),
                                                   spread(rr[:, :], 2, HD), ALU.mult))
                        flush().then_inc(S["y_ready"], 1)
                        return
                    free("Bo", v.tensor_copy(y, bank[6 + qt][:, :]))
                    flush()
                    v.tensor_tensor(tM.rearrange("p a n -> p (a n)"), y, y, ALU.mult)
                    flush()
                    v.tensor_reduce(st[:, 0:4], tM.rearrange("p a (b n) -> p (a b) n", n=P), AX.X, ALU.add)
                    flush()
                    rstd(st[:, 0:4], st[:, 0:4], P)
                    yv = y.rearrange("p (h n) -> p h n", n=P)
                    v.tensor_tensor(yv, yv, spread(st[:, 0:4], 2, P), ALU.mult)
                    flush()
                    v.tensor_tensor(yv, yv, spread(subln, 1, DH), ALU.mult)
                    flush().then_inc(S["y_ready"], 1)

                outs = 0
                for g in range(len(GROUPS) + 1):
                    if outs < 4 and g - 5 >= LAST_GROUP[outs]:
                        heads_out(outs)
                        outs += 1
                    if g < len(GROUPS):
                        kind, qt, h, s0 = GROUPS[g]
                        nk = (qt + 1) * P
                        for s in range(s0, s0 + 2 - kind):
                            dve.wait_ge(filled["Bs"], me.next("Bs"))
                            dve.nop(nofuse=True)
                            if s >= 4:
                                dve.wait_ge(S["p_ready"], me.at(s - 3, "p_ready"))
                                dve.nop(nofuse=True)
                            add = mask if kind else bias[:, h, :]
                            v.tensor_tensor_reduce(out=lg[:, s % 4, 0:nk], in0=bank[s % 4][:, 0:nk],
                                                   in1=add[:, SEQ - nk:SEQ], scale=-1.0, scalar=3.0e38, op0=ALU.add,
                                                   op1=ALU.min, accum_out=nm[:, s % 4:s % 4 + 1]
                                                   ).then_inc(emptied["Bs"], 1)
                    if g >= 1:
                        kind, qt, h, s = GROUPS[g - 1]
                        if kind == 0:
                            nk = (qt + 1) * P
                            dve.wait_ge(S["p_ready"], me.at(s + 2, "p_ready"))
                            v.reciprocal(rr[:, 0:2], rs[:, s:s + 2])
                            flush()
                            v.tensor_scalar(rr[:, 2:3], rr[:, 1:2], lam2[:, 7:8], None, ALU.mult)
                            if g >= 3:
                                dve.wait_ge(filled["BpT"], me.at(g - 2, "BpT"))
                            wv = wd[:, (g - 1) % 2, 0:nk]
                            v.tensor_scalar(wv, pb[:, s % 4, 0:nk], rr[:, 0:1], None, ALU.mult)
                            flush()
                            v.scalar_tensor_tensor(wv, pb[:, (s + 1) % 4, 0:nk], rr[:, 2:3], wv, ALU.mult, ALU.add)
                            flush().then_inc(S["w_ready"], 1)
                while outs < 4:
                    heads_out(outs)
                    outs += 1
                dve.wait_ge(emptied["proj"], me.at(36, "proj"))
                for j in range(KD):
                    dve.wait_ge(filled["mg"], me.next("mg"))
                    free("mg", v.tensor_tensor(tM, bank[j % 8][:, :].rearrange("p (a n) -> p a n", a=2),
                                               sig[:, :, j, :], ALU.mult))
                    flush()
                    v.tensor_tensor(mT[:, j, :], tM[:, 0, :], tM[:, 1, :], ALU.add)
                    flush().then_inc(S["mT_ready"], 1)
                for half in range(2):
                    for t in range(LAT):
                        dve.wait_ge(filled["By"], me.next("By"))
                        cut = slice(half * CH, (half + 1) * CH)
                        free("By", v.tensor_tensor(x[:, t, cut], x[:, t, cut], bank[half * LAT + t][:, :], ALU.add))
                flush()
                dve.wait_ge(S["gain_in"], me.at(16, "gain_in"))
                row_stats(LAT)
                for t in range(LAT):
                    row_norm(t, xn[:, t, :])
                    flush()
                    v.tensor_tensor(ttok[:, t, :], xn[:, t, :], wide[:, :], ALU.mult).then_inc(S["Bxn"], 1)
                for t in range(LAT):
                    dve.wait_ge(filled["BxTv"], me.next("BxTv"))
                    free("BxTv", v.tensor_copy(h2[:, 0:4, t * P:(t + 1) * P],
                                               bank[2 * t][:, :].rearrange("p (a n) -> p a n", a=4)))

                def top16(src, spare, o, where, n, w):
                    s = [src[:, i * w:(i + 1) * w] for i in range(n)]
                    r = [spare[:, i * w:(i + 1) * w] for i in range(n)]
                    for i in range(n):
                        v.max(out=o[:, i, 0:8], in_=s[i])
                    flush()
                    for i in range(n):
                        v.max_index(out=where[:, i, 0:8], in_max=o[:, i, 0:8], in_values=s[i])
                        v.match_replace(out=r[i], in_to_replace=o[:, i, 0:8], in_values=s[i], imm_value=-3.0e38)
                    flush()
                    for i in range(n):
                        v.max(out=o[:, i, 8:16], in_=r[i])
                    flush()
                    for i in range(n):
                        v.max_index(out=where[:, i, 8:16], in_max=o[:, i, 8:16], in_values=r[i])
                    flush()

                for t in range(LAT):
                    dve.wait_ge(emptied["sc"], me.at(4 * t + 4, "sc"))
                    dve.nop(nofuse=True)
                    top16(sc[:, t, :, :].rearrange("p a n -> p (a n)"), w1, tv, ti, 2 * PH, NK)
                    v.tensor_copy(tif, ti)
                    for h in range(PH):
                        v.tensor_tensor(w1[:, h * 256:(h + 1) * 256].rearrange("p (a b) -> p a b", a=16),
                                        spread(tv[:, 2 * h, :], 2, 16), spread(tv[:, 2 * h + 1, :], 1, 16), ALU.add)
                    flush()
                    top16(w1, w2, bv, bp, PH, 256)
                    v.tensor_single_scalar(bi[:, 0], bp, 4, ALU.logical_shift_right)
                    v.tensor_single_scalar(bi[:, 1], bp, 15, ALU.bitwise_and)
                    v.tensor_tensor(gates[:, t, :].rearrange("p (h n) -> p h n", n=16), bv,
                                    bv[:, :, 0:1].broadcast_to([P, PH, 16]), ALU.subtract)
                    flush().then_inc(S["gate_z"], 1)
                    v.tensor_copy(bf, bi)
                    flush()
                    for c in range(2):
                        v.tensor_tensor(w1.rearrange("p (a b) -> p a b", b=16),
                                        spread(bf[:, c].rearrange("p h n -> p (h n)"), 2, 16),
                                        spread(iota[:, :], 1, PICKS), ALU.is_equal)
                        flush()
                        for h in range(PH):
                            wv = w1[:, h * 256:(h + 1) * 256].rearrange("p (a b) -> p a b", a=16)
                            v.tensor_tensor(wv, wv, spread(tif[:, 2 * h + c, :], 1, 16), ALU.mult)
                        flush()
                        v.tensor_reduce(ei[:, c, :], w1.rearrange("p (a b) -> p a b", b=16), AX.X, ALU.add)
                        flush()
                    v.tensor_scalar(ei[:, 0, :], ei[:, 0, :], float(NK), layerE[:, :], ALU.mult, ALU.add)
                    flush()
                    v.tensor_tensor(ei[:, 0, :], ei[:, 0, :], ei[:, 1, :], ALU.add)
                    flush()
                    v.tensor_copy(picks[:, t, :], ei[:, 0, :])
                    flush().then_inc(S["picked"], 1)
                    dve.wait_ge(S["gate_e"], me.at(t + 1, "gate_e"))
                    gt = gates[:, t, :].rearrange("p (h n) -> p h n", n=16)
                    v.tensor_reduce(rr[:, :], gt, AX.X, ALU.add)
                    flush()
                    v.reciprocal(rr[:, :], rr[:, :])
                    flush()
                    v.tensor_tensor(gt, gt, spread(rr[:, :], 2, 16), ALU.mult)
                    flush()

                for t in range(LAT):
                    with dve.Fori(0, RUN) as i:
                        for j in range(ROWS):
                            dve.wait_ge(row_in[j], me.at(i * 16 + 2 * t * RUN * 16 + 16, "row_in"))
                            v.tensor_tensor_reduce(out=junk[j % 2], in0=expert[:, j, :], in1=ttok[:, t, :], scale=1.0,
                                                   scalar=0.0, op0=ALU.mult, op1=ALU.add, accum_out=d16[:, j:j + 1]
                                                   ).then_inc(S["free_v"], 1)
                            if j % 2:
                                flush()
                        v.tensor_copy(dots[:, t, bass.ts(i, ROWS)], d16[:, :])
                        flush()
                    flush().then_inc(S["dotted"], 1)
                    v.memset(acc, 0.0)
                    dve.wait_ge(S["acted"], me.at(t + 1, "acted"))
                    v.tensor_tensor(dots[:, t, :], dots[:, t, :], gates[:, t, :], ALU.mult)
                    flush().then_inc(S["weighed"], 1)
                    with dve.Fori(0, RUN) as i:
                        for j in VROWS:
                            dve.wait_ge(row_in[j], me.at(i * 16 + (2 * t + 1) * RUN * 16 + 16, "row_in"))
                            v.scalar_tensor_tensor(acc, expert[:, j, :], dots[:, t, bass.ds(i * ROWS + j, 1)], acc,
                                                   ALU.mult, ALU.add).then_inc(S["free_v"], 1)
                            flush()
                    flush().then_inc(S["acc_ready"], 1)
                    if t == LAT - 1:
                        for u in range(LAT):
                            dve.wait_ge(filled["acc"], me.next("acc"))
                            for half in range(2):
                                last = v.tensor_copy(x[:, u, half * CH:(half + 1) * CH], bank[2 * u + half][:, :])
                            free("acc", last)
                    else:
                        dve.wait_ge(filled["acc"], me.at(t + 1, "acc"))
                        dve.nop(nofuse=True)
                v.tensor_scalar(layerE[:, :], layerE[:, :], float(NE), None, ALU.add)
                flush().then_inc(layer_done, 1)

            dve.wait_ge(final_in, 16)
            row_stats(LAT)
            for t in range(LAT):
                row_norm(t, xn[:, t, :])
                flush()
                v.tensor_tensor(xn[:, t, :], xn[:, t, :], wide[:, :], ALU.mult)
            flush().then_inc(result_ready, 1)
        return nc


def used():
    raise NotImplementedError


_INS = ["x", "c", "ctx", "c_ctx", "w_mod", "b_mod", "norm1_g", "w_in", "q_norm_g", "k_norm_g",
        "gmlp_norm_g", "w_spatial", "b_spatial", "w_out", "norm2_g", "w_ff1", "w_ff2", "norm1_g_2",
        "w_in_2", "b_forget_2", "diff_lambda_2", "diff_subln_g_2", "w_diff_o_2", "w_fox_o_2",
        "w_out_2", "norm2_g_2", "w_query_2", "sub_keys_2", "expert_u_2", "expert_v_2",
        "rel_bias_2", "final_norm_g_2"]


def kernel(**inputs):
    import concourse.bacc as bacc
    from concourse.bass_utils import run_bass_kernel_spmd as run

    nc = bacc.Bacc("TRN2", target_bir_lowering=False, num_devices=1)
    arrays, views = {}, {}
    named = {k: np.ascontiguousarray(inputs[k]) for k in _INS}
    for name, a in {**named, **constants()}.items():
        arrays[f"in_{name}"] = a
        views[name] = nc.dram_tensor(f"in_{name}", a.shape, mybir.dt.from_np(a.dtype), kind="ExternalInput").ap()
    out = nc.dram_tensor("out_x", (1, SEQ, D), F32, kind="ExternalOutput").ap()
    build(nc, views, out)
    r = run(nc, [arrays], core_ids=[0])
    return r.results[0]["out_x"]
```

```python
import math
from contextlib import ExitStack

import numpy as np

import concourse.bass as bass
from concourse import mybir

F32 = mybir.dt.float32
U32 = mybir.dt.uint32
ALU = mybir.AluOpType
ACT = mybir.ActivationFunctionType
AX = mybir.AxisListType

P = 128
D = 1024
KD = D // P
LAYERS = 2
LAT = 2
TILES = 4
SEQ = LAT * P
HD = 64
AH, AKV = 8, 2
QW, KVW, GW = 512, 128, 512
ZW = QW + 2 * KVW
FF = 4 * D
EPS = 1e-6
CH = 512
SLOTS = 4
SCALE = HD ** -0.5
DH, FH = 4, 8
W2IN = 5128
FFCOL = 3072
PH, TOPK, NK = 8, 16, 128
NE = NK * NK
VECTORS, CONSTS = 7, 9
CHUNKS_A, CHUNKS_B = 68, 18
SEARCH_SLOT = (CHUNKS_B - 4) % SLOTS
PICKS = PH * TOPK
ROWS = 16
HALF = ROWS // 2
NEG = -1.0e30
REL = 384


def t5_bucket(dist, buckets=32, far=128):
    n = np.maximum(dist, 0)
    exact = buckets // 2
    nf = np.maximum(n, 1).astype(np.float32)
    large = exact + (np.log(nf / np.float32(exact)) / np.float32(math.log(far / exact))
                     * np.float32(buckets - exact)).astype(np.int32)
    return np.where(n < exact, n, np.minimum(large, buckets - 1))


def constants():
    tok = np.arange(SEQ)
    pos = np.stack([tok // 64, tok % 64], 1).astype(np.float32)
    freq = (10000.0 ** (-np.arange(16, dtype=np.float32) / 16)).astype(np.float32)
    ang = (pos[:, :, None] * freq).astype(np.float32)
    cos, sin = np.cos(ang), np.sin(ang)
    rope = np.zeros((SEQ, 2, 2, 2, 16), np.float32)
    rope[:, 0] = cos[:, :, None, :]
    rope[:, 1, :, 0], rope[:, 1, :, 1] = -sin, sin
    dist = 255 - np.arange(REL)
    onehot = np.zeros((33, REL), np.float32)
    onehot[t5_bucket(dist), np.arange(REL)] = dist >= 0
    onehot[32] = np.where(dist >= 0, 0.0, NEG)
    q, k = np.arange(P)[:, None], np.arange(SEQ)[None]
    mask = np.where(128 + q - k >= 0, 0.0, NEG).astype(np.float32)
    lam = [0.8 - 0.6 * math.exp(-0.3 * i) for i in range(LAYERS)]
    pickv = np.zeros((2, 2, P), np.float32)
    pickv[np.arange(2), np.arange(2)] = 1.0
    return {
        "rope": rope.reshape(SEQ, 128), "onehot": onehot, "mask": mask,
        "ones4": np.ones((1, DH), np.float32),
        "pickv": pickv.reshape(2, 256),
        "lam": np.array([[a, 1 - a] for a in lam], np.float32),
        "iota16": np.arange(16, dtype=np.float32)[None], "eye": np.eye(P, dtype=np.float32),
    }


def build(nc, A, out):
    ctx = ExitStack()
    with ctx:
        ctx.enter_context(nc.allow_non_contiguous_dma("small strided loads"))

        def sb(name, shape, dt=F32):
            return ctx.enter_context(nc.sbuf_tensor(name, shape, dt))

        def sem(name):
            return ctx.enter_context(nc.semaphore(name))

        def spread(ap, axis, n):
            ap = ap.unsqueeze(axis)
            shape = list(ap.shape)
            shape[axis] = n
            return ap.broadcast_to(shape)

        ring = sb("ring", [P, SLOTS, KD * CH])
        x = sb("x", [P, TILES, D])
        hT = sb("hT", [P, KD, TILES * P])
        big = sb("big", [P, 16384])
        gate = sb("gate", [P, 2, 2, D])
        xn = sb("xn", [P, 2, D])
        kT = sb("kT", [P, 2, TILES * P])
        wide = sb("wide", [P, D])
        ggain = sb("ggain", [P, GW])
        wsp = sb("wsp", [P, 4, P])
        wsT = sb("wsT", [P, 4, P])
        eye = sb("eye", [P, P])
        rows = sb("rows", [72, P])
        cols = sb("cols", [P, 72])
        cond = sb("cond", [P, KD, 32])
        pickv = sb("pickv", [P, 2, P])
        rope = sb("rope", [P, LAT, 2, HD])
        modcol = sb("modcol", [P, 4, KD, 2])
        modA = sb("modA", [P, 2, KD, 2])
        ss = sb("ss", [P, 4])
        rst = sb("rst", [P, 4])
        st = sb("st", [P, 72])
        nw = sb("nw", [P, 4, 40])
        nm = sb("nm", [P, 4])
        rs = sb("rs", [P, 32])
        rr = sb("rr", [P, 8])
        lam2 = sb("lam2", [P, 8])
        layerE = sb("layerE", [P, 1])
        gcol = sb("gcol", [P, KD])
        iota = sb("iota", [P, 16])
        rel = sb("rel", [33, DH])
        bfc = sb("bfc", [FH, 1])
        picks = sb("picks", [P, LAT, PICKS], U32)
        gates = sb("gates", [P, LAT, PICKS])
        dots = sb("dots", [P, LAT, PICKS])
        d16 = sb("d16", [P, ROWS])
        pick_now = sb("pick_now", [P, 2, HALF], U32)
        bias_rows = nc.dram_tensor("bias_rows", [DH, P, REL], F32).ap()

        h1T = big[:, :].rearrange("p (b t) -> p b t", t=TILES * P)
        modrow = [kT[:, 0, :], kT[:, 1, :], wsT[:, :, :].rearrange("p g n -> p (g n)")]
        bmod = [wide[:, 0:CH], wide[:, CH:2 * CH], ggain[:, :]]
        modt = xn[:, :, CH:2 * CH]
        z = big[:, 0:3072].rearrange("p (t n) -> p t n", t=TILES)
        ug = big[:, 3072:7168].rearrange("p (a t n) -> p a t n", a=2, t=TILES)
        gm = big[:, 7168:9216].rearrange("p (t n) -> p t n", t=TILES)
        qT = big[:, 9216:11264].rearrange("p (b t) -> p b t", b=4)
        pr = big[:, 11264:12800].rearrange("p (a n) -> p a n", a=3)
        prT = big[:, 12800:14336].rearrange("p (a n) -> p a n", a=3)
        tA = big[:, 14336:14976]
        tB = big[:, 14976:15616]
        qn = big[:, 15616:16384]
        gq = wide[:, 0:640]
        onehot = hT[0:33, 4, 0:REL]
        brow = hT[0:DH, 5, 0:REL]

        dfT = big[:, 0:4096].rearrange("p (a b t) -> p a b t", a=4, b=4)
        dfv = big[:, 4096:6144].rearrange("p (a t n) -> p a t n", a=2, t=LAT)
        sig = big[:, 6144:10240].rearrange("p (a b t) -> p a b t", a=2, b=KD)
        yy = big[:, 10240:12288].rearrange("p (a t n) -> p a t n", a=2, t=LAT)
        lg = big[:, 12288:13312].rearrange("p (a n) -> p a n", a=4)
        pb = big[:, 13312:14336].rearrange("p (a n) -> p a n", a=4)
        wd = big[:, 14336:14848].rearrange("p (a n) -> p a n", a=2)
        pbT = big[:, 14848:15616].rearrange("p (a n) -> p a n", a=3)
        tM = big[:, 15616:16128].rearrange("p (a n) -> p a n", a=2)
        h2 = hT[:, 0:4, :].rearrange("p a (b t) -> p (a b) t", b=2)
        yT = hT[:, 4:8, :].rearrange("p a (b t) -> p (a b) t", b=2)
        mT = xn[:, :, :].rearrange("p a (b t) -> p (a b) t", b=4)
        qq = big[:, 0:4096].rearrange("p (a t) -> p a t", a=2 * PH)
        scratch = ring[:, SEARCH_SLOT, :]
        scores = [big[:, 4096:6144], scratch[:, 0:2048]]
        sc = [s.rearrange("p (a n) -> p a n", a=2 * PH) for s in scores]
        w1 = scratch[:, 2048:3072]
        w2 = scratch[:, 3072:3584]
        tv = scratch[:, 3584:3648].rearrange("p (a n) -> p a n", n=16)
        tif = scratch[:, 3648:3712].rearrange("p (a n) -> p a n", n=16)
        ti = scratch[:, 3712:3776].bitcast(U32).rearrange("p (a n) -> p a n", n=16)
        bv = scratch[:, 3776:3808].rearrange("p (a n) -> p a n", n=16)
        bp = scratch[:, 3808:3840].bitcast(U32).rearrange("p (a n) -> p a n", n=16)
        bf = scratch[:, 3840:3904].rearrange("p (c a n) -> p c a n", c=2, n=16)
        bi = scratch[:, 3904:3968].bitcast(U32).rearrange("p (c a n) -> p c a n", c=2, n=16)
        ei = scratch[:, 3968:4096].rearrange("p (c n) -> p c n", c=2)
        expert = big[:, :].rearrange("p (s n) -> p s n", s=ROWS)
        diag = hT[:, 0:3, :].rearrange("p a (b n) -> p (a b) n", n=P)
        junk = [xn[:, 0, :], hT[:, 6:8, :].rearrange("p a n -> p (a n)")]
        acc = xn[:, 1, :]
        ttok = gate[:, 0, :, :]
        bias = gate[:, 1, 0, :].rearrange("p (h n) -> p h n", h=DH)
        mask = gate[:, 1, 1, 0:SEQ]
        sk = wsp[:, 0:2, :]
        skT = wsT[:, 0:2, :]
        wff = kT[:, 0, 0:64].rearrange("p (k n) -> p k n", k=KD)
        lamrow = kT[:, 0, 64:320].rearrange("p (a n) -> p a n", a=4)
        lamp = kT[:, 0, 320:448].rearrange("p (a n) -> p a n", a=2)
        subln = ggain[:, 0:P]
        fcv = x[0:FH, 2:4, :].rearrange("p a (b n) -> p (a b) n", n=SEQ)

        bank = [ctx.enter_context(nc.psum_tensor(f"bank{i}", [P, 512], F32)) for i in range(8)]

        FIRST = ["col", "rel", "mod", "modT", "gate", "xTv", "xTs", "z", "ws", "qkT", "sp", "s",
                 "pT", "o", "mT", "y", "f1", "f2"]
        SECOND = {"BxTv": 4, "BxTs": 4, "proj": 36, "ff": 1, "sk": 1, "Bs": 32, "BpT": 24, "Bo": 4,
                  "yT": 4, "mg": 8, "By": 4, "q2": 16, "sc": 8, "acc": 2}
        filled = {f: sem("filled_" + f) for f in FIRST + list(SECOND)}
        emptied = {f: sem("emptied_" + f) for f in FIRST + list(SECOND)}
        landed = [sem(f"chunk_landed{i}") for i in range(SLOTS)]
        chunk_used = sem("chunk_used")
        scratch_free = sem("scratch_free")
        vectors_in, consts_in, x_in, bmod_in, wide_in = sem("vectors_in"), sem("consts_in"), sem("x_in"), sem("bmod_in"), sem("wide_in")
        bias_out, bias_in, final_in = sem("bias_out"), sem("bias_in"), sem("final_in")
        cond_zero, modA_ready = sem("cond_zero"), sem("modA_ready")
        xn_ready, qn_ready, vn_ready = sem("xn_ready"), sem("qn_ready"), sem("vn_ready")
        nm_ready, pv_done, mix_ready = sem("nm_ready"), sem("pv_done"), sem("mix_ready")
        layer_done = sem("layer_done")
        result_ready, out_done = sem("result_ready"), sem("out_done")
        row_in = [sem(f"row_in{i}") for i in range(ROWS)]
        VROWS = [j for j in range(ROWS) if j % 4 == 3]
        PROWS = [j for j in range(ROWS) if j % 4 != 3]
        NV, NP, RUN = len(VROWS), len(PROWS), PICKS // ROWS
        PER = {"Bxn": 4, "ff_z": 1, "ff_e": 1, "c_ready": 1, "p_ready": 32, "w_ready": 8,
               "Bpv": 24, "y_ready": 4, "mT_ready": 8, "lam_z": 1, "lam_e": 1, "gate_z": 2,
               "gate_e": 2, "picked": 2, "dotted": 2, "acted": 2, "weighed": 2, "acc_ready": 2,
               "small_in": 6 * 16, "gain_in": 16, "picks_now": 2 * RUN * 2 * LAT,
               "free_v": LAT * (PICKS + NV * RUN), "free_p": LAT * NP * RUN,
               "diag_ready": LAT * NP * RUN}
        S = {f: sem(f) for f in PER}
        PER |= SECOND | {"layer_done": 1, "row_in": 16 * RUN * 2 * LAT}
        PER |= {f"landed{s}": 16 * len(range(s, CHUNKS_B, SLOTS)) for s in range(SLOTS)}

        block = ctx.enter_context(nc.Block())

        class Side:

            def __init__(self):
                self.layer, self.n, self.held = None, {}, [None] * 8

            def at(self, n, name):
                return n if self.layer is None else self.layer * PER[name] + n

            def next(self, fam):
                self.n[fam] = self.n.get(fam, 0) + 1
                return self.at(self.n[fam], fam)

            def freed(self, b):
                if self.held[b] is None:
                    return (consts_in, 16 * CONSTS) if self.layer is None else (layer_done, self.layer + 1)
                old, n = self.held[b]
                return emptied[old], self.at(n, old)

            def claim(self, fam, b):
                self.n[fam] = self.n.get(fam, 0) + 1
                self.held[b] = (fam, self.n[fam])
                return bank[b]

            def new_layer(self, layer):
                self.layer, self.n, self.held = layer, {}, [None] * 8

        GROUPS, n = [], 0
        for kind, heads, maps in ((0, DH, 2), (1, FH, 1)):
            for qt in range(LAT):
                for h in range(heads):
                    GROUPS.append((kind, qt, h, n))
                    n += maps
        GROUP_OF = [g for g, (kind, *_) in enumerate(GROUPS) for _ in range(2 - kind)]
        LAST_GROUP = [3, 7, 15, 23]

        BETWEEN = [("ff", 0, 0)] + [("cols", c, i) for c in (3, 4) for i in range(4)]
        BETWEEN += [("rows", 5, t) for t in range(LAT)] + [("cols", c, i) for c in range(6, 10) for i in range(4)]
        assert len(BETWEEN) == len(GROUPS) + 3

        COLUMN = {0: 0, 1: 1, 3: 2, 4: 3}
        SHIFTS = [[(kind, half) for kind in COLUMN for half in range(2) if (2 * kind + half) % 4 == g] for g in range(4)]

        @block.sync
        def _(sp):
            count = 0

            def put(src, slot):
                k, w = src.shape[1], src.shape[2]
                dst = ring[:, slot, 0:k * w].rearrange("p (k n) -> p k n", k=k)
                sp.dma_start(dst, src).then_inc(landed[slot], 16)

            def chunk(src):
                nonlocal count
                if count >= SLOTS:
                    sp.wait_ge(chunk_used, count - SLOTS + 1)
                put(src, count % SLOTS)
                count += 1

            def mod_chunk(layer, c):
                chunk(A["w_mod"][layer].rearrange("(k p) n -> p k n", p=P)[:, :, c * CH:(c + 1) * CH])

            for c in range(12):
                mod_chunk(0, c)
            for layer in range(LAYERS):
                w = A["w_in"][layer].rearrange("(k p) n -> p k n", p=P)
                for a, b in ((0, 512), (512, 768), (768, 1280), (1280, 1792)):
                    chunk(w[:, :, a:b])
                w = A["w_out"][layer].rearrange("(k p) n -> p k n", p=P)
                for c in range(2):
                    chunk(w[:, :, c * CH:(c + 1) * CH])
                w = A["w_ff1"][layer].rearrange("(k p) n -> p k n", p=P)
                for c in range(8):
                    chunk(w[:, :, c * CH:(c + 1) * CH])
                    if layer == 0:
                        mod_chunk(1, c)
                w = A["w_ff2"][layer].rearrange("(c k p) n -> c p k n", p=P, k=KD)
                for h in range(2):
                    for c in range(4):
                        chunk(w[c, :, :, h * CH:(h + 1) * CH])
                        if layer == 0 and h == 0:
                            mod_chunk(1, 8 + c)
            assert count == CHUNKS_A

            with sp.Fori(0, LAYERS) as l:
                c = 0

                def chunk_of_layer(src):
                    nonlocal c
                    sp.wait_ge(chunk_used, l * CHUNKS_B + CHUNKS_A + max(0, c - SLOTS + 1))
                    sp.nop(nofuse=True)
                    if c == SEARCH_SLOT:
                        sp.wait_ge(scratch_free, l + 1)
                        sp.nop(nofuse=True)
                    put(src, c % SLOTS)
                    c += 1

                def of_layer(name):
                    w = A[name].rearrange("l (k p) n -> l p k n", p=P)
                    return w[bass.ds(l, 1)].rearrange("l p k n -> (l p) k n")

                w = of_layer("w_in_2")
                for a in (0, 512, 1024, 1536, 2048, 2560, 3080, 3592, 4104, 4616):
                    chunk_of_layer(w[:, :, a:a + CH])
                chunk_of_layer(of_layer("w_diff_o_2"))
                chunk_of_layer(of_layer("w_fox_o_2"))
                for name, m in (("w_out_2", 2), ("w_query_2", 4)):
                    w = of_layer(name)
                    for i in range(m):
                        chunk_of_layer(w[:, :, i * CH:(i + 1) * CH])
                assert c == CHUNKS_B
            sp.wait_ge(result_ready, 1)
            sp.dma_start(out.rearrange("o (t p) n -> (o p) t n", p=P), xn[:, :, :]).then_inc(out_done, 16)
            sp.wait_ge(out_done, 16)

        @block.gpsimd
        def _(pool):
            me = Side()

            def load(dst, src, s):
                pool.dma_start(dst, src).then_inc(s, 16)

            load(onehot, A["onehot"], consts_in)
            load(rel[0:32, :], A["rel_bias_2"], consts_in)
            load(rel[32:33, :], A["ones4"], consts_in)
            for q in range(4):
                load(pickv[32 * q:32 * q + 2, :, :], A["pickv"].rearrange("a (b p) -> a b p", b=2), consts_in)
            load(rope[:, :, :, :], A["rope"].rearrange("(t p) (a n) -> p t a n", p=P, a=2), consts_in)
            load(iota[:, :], A["iota16"].broadcast_to([P, 16]), consts_in)
            for layer in range(LAYERS):
                if layer:
                    pool.wait_ge(emptied["sp"], me.at(TILES, "sp"))
                for c in range(12):
                    q = 32 * (c % 4)
                    load(bmod[c // 4][q:q + 2, :], A["b_mod"][layer:layer + 1, c * CH:(c + 1) * CH].broadcast_to([2, CH]),
                         bmod_in)
                pool.wait_ge(emptied["mod"], me.at(12 * (layer + 1), "mod"))
                for a in range(AH + AKV):
                    g = A["q_norm_g" if a < AH else "k_norm_g"][layer:layer + 1]
                    load(gq[:, a * HD:(a + 1) * HD], g.broadcast_to([P, HD]), wide_in)
                load(ggain[:, :], A["gmlp_norm_g"][layer:layer + 1].broadcast_to([P, GW]), wide_in)
                load(wsp[:, :, :], A["w_spatial"][layer].rearrange("g p q -> p g q"), wide_in)
                if layer == 0:
                    pool.wait_ge(emptied["rel"], 1)
                    load(bias_rows, spread(brow, 1, P), bias_out)
            pool.wait_ge(bias_out, 16)
            pool.wait_ge(layer_done, 1)
            load(bias, bass.AP(tensor=bias_rows.tensor, offset=P - 1, ap=[[REL - 1, P], [P * REL, DH], [1, SEQ]]), bias_in)
            load(mask, A["mask"], bias_in)
            pool.sem_inc(S["free_v"], ROWS)
            pool.sem_inc(S["free_p"], NP)

            with pool.Fori(0, LAYERS) as l:
                me.new_layer(l)
                pool.wait_ge(layer_done, me.at(1, "layer_done"))

                def of_layer(name):
                    return A[name][bass.ds(l, 1)]

                load(wff, A["w_in_2"].rearrange("l (k p) n -> l p k n", p=P)[bass.ds(l, 1), :, :, FFCOL:FFCOL + FH]
                     .rearrange("l p k n -> (l p) k n"), S["small_in"])
                load(bfc[:, :], of_layer("b_forget_2").rearrange("l (h o) -> (l h) o", o=1), S["small_in"])
                load(lamrow, of_layer("diff_lambda_2").rearrange("l a n -> l (a n)").broadcast_to([P, 4 * HD])
                     .rearrange("p (a n) -> p a n", a=4), S["small_in"])
                load(lam2[:, 0:2], of_layer("lam").broadcast_to([P, 2]), S["small_in"])
                load(subln, of_layer("diff_subln_g_2").broadcast_to([P, P]), S["small_in"])
                load(sk, A["sub_keys_2"].rearrange("l a n d -> l n a d")[bass.ds(l, 1)]
                     .rearrange("l n a d -> (l n) a d"), S["small_in"])
                load(wide[:, :], of_layer("norm2_g_2").broadcast_to([P, D]), S["gain_in"])

                for t in range(LAT):
                    pool.wait_ge(S["picked"], me.at(t + 1, "picked"))
                    if t == 0:
                        pool.wait_ge(emptied["sc"], me.at(8, "sc"))
                        pool.nop(nofuse=True)
                    for v, name in enumerate(("expert_u_2", "expert_v_2")):
                        table = A[name].rearrange("l e n -> (l e) n")
                        base_v = t * (PICKS + NV * RUN) + v * PICKS
                        base_p = t * NP * RUN
                        if v:
                            pool.wait_ge(S["free_v"], me.at(ROWS + base_v - HALF, "free_v"))
                        elif t:
                            pool.wait_ge(S["free_v"], me.at(ROWS + base_v - NV // 2, "free_v"))
                            pool.wait_ge(S["free_p"], me.at(NP + base_p - NP // 2, "free_p"))
                        pool.nop(nofuse=True)
                        with pool.Fori(0, RUN) as i:
                            for half in range(2):
                                rate = NV if v else ROWS
                                pool.wait_ge(S["free_v"], me.at(i * rate + ROWS + base_v - rate + rate // 2 * (half + 1), "free_v"))
                                if v:
                                    pool.wait_ge(S["free_p"], me.at(i * NP + base_p + NP // 2 * (half + 1), "free_p"))
                                elif half:
                                    pool.wait_ge(S["free_p"], me.at(NP + base_p, "free_p"))
                                pool.tensor_copy(pick_now[:, half, :],
                                                 picks[:, t, bass.ds(i * ROWS + half * HALF, HALF)]
                                                 ).then_inc(S["picks_now"], 1)
                                pool.wait_ge(S["picks_now"], me.at(i * 2 + (2 * t + v) * 2 * RUN + half + 1, "picks_now"))
                                pool.nop(nofuse=True)
                                for j in range(HALF):
                                    s = half * HALF + j
                                    pool.indirect_dma_start(
                                        out=expert[:, s, :], out_offset=None, in_=table,
                                        in_offset=bass.IndirectOffsetOnAxis(ap=pick_now[:, half, j:j + 1], axis=0),
                                    ).then_inc(row_in[s], 16)
            pool.wait_ge(layer_done, 1 + LAYERS)
            load(wide[:, :], A["final_norm_g_2"].rearrange("(o n) -> o n", o=1).broadcast_to([P, D]), final_in)

        @block.tensor
        def _(pe):
            me = Side()
            chunks = 0

            def next_chunk():
                nonlocal chunks
                slot, n = chunks % SLOTS, chunks // SLOTS + 1
                if me.layer is None:
                    pe.wait_ge(landed[slot], 16 * n)
                else:
                    before = len(range(slot, CHUNKS_A, SLOTS))
                    pe.wait_ge(landed[slot], me.at(16 * (n + before), f"landed{slot}"))
                chunks += 1
                return slot

            def fill(fam, ins):
                ins.then_inc(filled[fam], 1)

            read = 0

            def used(m=1):
                nonlocal read
                read += m

            def tell(ins):
                nonlocal read
                if read:
                    ins.then_inc(chunk_used, read)
                    read = 0

            def norm_T(fams, source, ready, tiles, name=None, first=0):
                for t in range(tiles):
                    pe.wait_ge(ready, me.at(first + t + 1, name))
                    for half, fam in enumerate(fams):
                        pe.wait_ge(*me.freed((2 * t + half) % 8))
                        o = me.claim(fam, (2 * t + half) % 8)
                        for b in range(4):
                            k = 4 * half + b
                            last = nc.tensor.transpose(o[:, b * P:(b + 1) * P], source(t)[:, k * P:(k + 1) * P], eye[:, :])
                            if b == 0:
                                tell(last)
                        fill(fam, last)

            def product(o, lhs, rhs):
                n = len(lhs)
                last = None
                for k in range(n):
                    last = nc.tensor.matmul(o, lhs[k], rhs[k], start=k == 0, stop=k == n - 1)
                    if k == 0 and n == KD:
                        tell(last)
                return last

            pe.wait_ge(vectors_in, 16 * VECTORS)
            pe.wait_ge(*me.freed(0))
            fill("col", nc.tensor.transpose(me.claim("col", 0)[:, 0:72], rows[:, :], eye[0:72, 0:72]))
            pe.wait_ge(emptied["col"], me.at(1, "col"))

            def modulation(b):
                slot = next_chunk()
                pe.wait_ge(*me.freed(b))
                o = me.claim("mod", b)
                for i in range(2):
                    for g in range(4):
                        k = 2 * g + i
                        last = nc.tensor.matmul(o[32 * g:32 * g + 32, :], cond[:, k, :], ring[:, slot, k * CH:(k + 1) * CH],
                                                start=i == 0, stop=i == 1)
                        if i == g == 0:
                            tell(last)
                fill("mod", last)
                used()

            for c in range(12):
                modulation(c % 8)
            pe.wait_ge(consts_in, 16 * CONSTS)
            pe.wait_ge(*me.freed(5))
            fill("rel", nc.tensor.matmul(me.claim("rel", 5)[0:DH, 0:REL], rel[:, :], onehot, start=True, stop=True))
            units, tiles_before = 0, 0
            for layer in range(LAYERS):
                NT = TILES if layer == 0 else LAT
                pe.wait_ge(emptied["mod"], me.at(12 * (layer + 1), "mod"))
                for g in range(4):
                    q = 32 * g
                    pe.wait_ge(*me.freed(1 + g))
                    o = me.claim("modT", 1 + g)
                    for n, (kind, half) in enumerate(SHIFTS[g]):
                        c = 2 * kind + half
                        for i in range(4):
                            last = nc.tensor.matmul(o[:, 8 * n + 2 * i:8 * n + 2 * i + 2],
                                                    modrow[c // 4][q:q + 2, i * P:(i + 1) * P], eye[q:q + 2, q:q + 2],
                                                    start=True, stop=True)
                            if g == n == i == 0:
                                tell(last)
                    fill("modT", last)
                b = 6
                for g, kind in enumerate((2, 5)):
                    for v in range(2 if layer == 0 else 1):
                        for half in range(2):
                            c = kind * 2 + half
                            q = 32 * (c % 4)
                            pe.wait_ge(*me.freed(b % 8))
                            o = me.claim("gate", b % 8)
                            fill("gate", nc.tensor.matmul(o[:, :], pickv[q:q + 2, v, :], modrow[c // 4][q:q + 2, :],
                                                          start=True, stop=True))
                            b += 1
                norm_T(("xTv", "xTs"), lambda t: xn[:, t % 2, :], xn_ready, TILES, first=tiles_before)
                tiles_before += TILES
                pe.wait_ge(emptied["xTv"], me.at(me.n["xTv"], "xTv"))
                pe.wait_ge(emptied["xTs"], me.at(me.n["xTs"], "xTs"))
                b = 0
                for c in range(4):
                    slot, w = next_chunk(), (512, 256, 512, 512)[c]
                    for t in range(TILES if c == 1 else NT):
                        pe.wait_ge(*me.freed(b % 8))
                        o = me.claim("z", b % 8)
                        last = product(o[:, 0:w], [hT[:, k, t * P:(t + 1) * P] for k in range(KD)],
                                       [ring[:, slot, k * w:(k + 1) * w] for k in range(KD)])
                        fill("z", last)
                        b += 1
                    used()
                pe.wait_ge(wide_in, 12 * 16 * (layer + 1))
                pe.wait_ge(*me.freed(b % 8))
                o = me.claim("ws", b % 8)
                for g in range(4):
                    last = nc.tensor.transpose(o[:, g * P:(g + 1) * P], wsp[:, g, :], eye[:, :])
                    if g == 0:
                        tell(last)
                fill("ws", last)
                b += 1
                for t in range(TILES):
                    pe.wait_ge(qn_ready, layer * TILES + t + 1)
                    for a, m in ((0, 4), (4, 2)):
                        if a == 0 and t >= NT:
                            continue
                        pe.wait_ge(*me.freed(b % 8))
                        o = me.claim("qkT", b % 8)
                        for i in range(m):
                            last = nc.tensor.transpose(o[:, i * P:(i + 1) * P], qn[:, (a + i) * P:(a + i + 1) * P], eye[:, :])
                        fill("qkT", last)
                        b += 1
                pe.wait_ge(emptied["ws"], me.at(me.n["ws"], "ws"))
                for t in range(NT):
                    pe.wait_ge(vn_ready, (TILES if layer else 0) + t + 1)
                    pe.wait_ge(*me.freed(b % 8))
                    o = me.claim("sp", b % 8)
                    for g in range(4):
                        last = nc.tensor.matmul(o[:, g * P:(g + 1) * P], wsT[:, g, :], ug[:, 1, t, g * P:(g + 1) * P],
                                                start=True, stop=True)
                    fill("sp", last)
                    b += 1
                pe.wait_ge(emptied["qkT"], me.at(me.n["qkT"], "qkT"))
                N = NT * AH
                for n in range(N + 2):
                    if n < N:
                        t, h = divmod(n, AH)
                        a = HD * (h % 2)
                        lo, hi = (0, 512) if t < LAT else (256, 512)
                        pe.wait_ge(*me.freed(n % 3))
                        o = me.claim("s", n % 3)
                        fill("s", nc.tensor.matmul(o[:, 0:hi - lo], qT[a:a + HD, h // 2, t * P:(t + 1) * P],
                                                   kT[a:a + HD, h // 4, lo:hi], start=True, stop=True))
                    if 1 <= n <= N:
                        m = n - 1
                        pe.wait_ge(emptied["s"], me.at(units + m + 1, "s"))
                        pe.wait_ge(*me.freed(3 + m % 3))
                        o = me.claim("pT", 3 + m % 3)
                        for i in range(4 if m // AH < LAT else 2):
                            last = nc.tensor.transpose(o[:, i * P:(i + 1) * P], pr[:, m % 3, i * P:(i + 1) * P], eye[:, :])
                        fill("pT", last)
                    if n >= 2:
                        m = n - 2
                        t, h = divmod(m, AH)
                        pe.wait_ge(emptied["pT"], me.at(units + m + 1, "pT"))
                        if h == 0:
                            pe.wait_ge(*me.freed(6 + t % 2))
                            o_bank = me.claim("o", 6 + t % 2)
                        blocks = range(4) if t < LAT else range(2, 4)
                        v0 = QW + KVW + HD * (h // 4)
                        last = product(o_bank[:, h * HD:(h + 1) * HD],
                                       [prT[:, m % 3, (i - blocks[0]) * P:(i - blocks[0] + 1) * P] for i in blocks],
                                       [z[:, i, v0:v0 + HD] for i in blocks])
                        last.then_inc(pv_done, 1)
                units += N
                for t in range(NT):
                    pe.wait_ge(mix_ready, (TILES if layer else 0) + t + 1)
                    for half, src in enumerate((z[:, t, 0:512], gm[:, t, :])):
                        pe.wait_ge(*me.freed((2 * t + half) % 8))
                        o = me.claim("mT", (2 * t + half) % 8)
                        for i in range(4):
                            last = nc.tensor.transpose(o[:, i * P:(i + 1) * P], src[:, i * P:(i + 1) * P], eye[:, :])
                        fill("mT", last)
                pe.wait_ge(emptied["mT"], me.at(me.n["mT"], "mT"))
                for half in range(2):
                    slot = next_chunk()
                    for t in range(NT):
                        pe.wait_ge(*me.freed((half * NT + t) % 8))
                        o = me.claim("y", (half * NT + t) % 8)
                        last = product(o[:, :], [hT[:, k, t * P:(t + 1) * P] for k in range(KD)],
                                       [ring[:, slot, k * CH:(k + 1) * CH] for k in range(KD)])
                        fill("y", last)
                    used()
                norm_T(("xTv", "xTs"), lambda t: xn[:, t % 2, :], xn_ready, NT, first=tiles_before)
                tiles_before += NT
                pe.wait_ge(emptied["xTv"], me.at(me.n["xTv"], "xTv"))
                pe.wait_ge(emptied["xTs"], me.at(me.n["xTs"], "xTs"))
                for c in range(8):
                    slot = next_chunk()
                    for i in range(4):
                        pe.wait_ge(*me.freed((c * 4 + i) % 7))
                        o = me.claim("f1", (c * 4 + i) % 7)
                        last = product(o[:, 0:NT * P],
                                       [ring[:, slot, k * CH + i * P:k * CH + (i + 1) * P] for k in range(KD)],
                                       [hT[:, k, 0:NT * P] for k in range(KD)])
                        fill("f1", last)
                    used()
                    if layer == 0:
                        modulation(7)
                for half in range(2):
                    outs = []
                    for t in range(NT):
                        pe.wait_ge(*me.freed(half * NT + t))
                        outs.append(me.claim("f2", half * NT + t))
                    for c in range(4):
                        slot = next_chunk()
                        if half == 0:
                            pe.wait_ge(emptied["f1"], me.at(me.n["f1"] - 32 + 8 * (c + 1), "f1"))
                        for t in range(NT):
                            for k in range(KD):
                                last = nc.tensor.matmul(outs[t][:, :], h1T[:, c * KD + k, t * P:(t + 1) * P],
                                                        ring[:, slot, k * CH:(k + 1) * CH],
                                                        start=c == 0 and k == 0, stop=c == 3 and k == KD - 1)
                                if k == 0:
                                    tell(last)
                            if c == 3:
                                fill("f2", last)
                        used()
                        if layer == 0 and half == 0:
                            modulation(7)

            tell(pe.drain())

            with pe.Fori(0, LAYERS) as l:
                me.new_layer(l)
                chunks = 0
                pe.wait_ge(layer_done, me.at(1, "layer_done"))
                norm_T(("BxTv", "BxTs"), lambda t: xn[:, t, :], S["Bxn"], LAT, name="Bxn")
                pe.wait_ge(emptied["BxTv"], me.at(2, "BxTv"))
                pe.wait_ge(emptied["BxTs"], me.at(2, "BxTs"))
                b = 4

                def columns(fam, b, slot, block):
                    pe.wait_ge(*me.freed(b % 8))
                    o = me.claim(fam, b % 8)
                    fill(fam, product(o[:, 0:SEQ],
                                      [ring[:, slot, k * CH + block * P:k * CH + (block + 1) * P] for k in range(KD)],
                                      [h2[:, k, :] for k in range(KD)]))

                def tokens(b, slot, t):
                    pe.wait_ge(*me.freed(b % 8))
                    o = me.claim("proj", b % 8)
                    fill("proj", product(o[:, :], [h2[:, k, t * P:(t + 1) * P] for k in range(KD)],
                                         [ring[:, slot, k * CH:(k + 1) * CH] for k in range(KD)]))

                for c in range(3):
                    slot = next_chunk()
                    for i in range(LAT if c == 2 else 4):
                        if c == 2:
                            tokens(b, slot, i)
                        else:
                            columns("proj", b, slot, i)
                        b += 1
                    used()
                pe.wait_ge(S["small_in"], me.at(PER["small_in"], "small_in"))
                pe.wait_ge(*me.freed(b % 8))
                o = me.claim("sk", b % 8)
                for i in range(2):
                    last = nc.tensor.transpose(o[:, i * P:(i + 1) * P], sk[:, i, :], eye[:, :])
                    if i == 0:
                        tell(last)
                fill("sk", last)
                pe.wait_ge(emptied["proj"], me.at(10, "proj"))
                for g, (what, c, i) in enumerate(BETWEEN):
                    if what == "ff":
                        pe.wait_ge(*me.freed(2))
                        o = me.claim("ff", 2)
                        fill("ff", product(o[0:FH, 0:SEQ], [wff[:, k, :] for k in range(KD)],
                                           [h2[:, k, :] for k in range(KD)]))
                    else:
                        if i == 0:
                            slot = next_chunk()
                        if what == "cols":
                            columns("proj", 2 + g % 2, slot, i)
                        else:
                            tokens(2 + g % 2, slot, i)
                        if i == (3 if what == "cols" else 1):
                            used()
                    if g < len(GROUPS):
                        kind, qt, h, s = GROUPS[g]
                        nk = (qt + 1) * P
                        if s == 16:
                            pe.wait_ge(emptied["proj"], me.at(18, "proj"))
                            pe.wait_ge(S["c_ready"], me.at(1, "c_ready"))
                        for m in range(2 - kind):
                            if kind == 0:
                                a, blk = HD * m, h
                            else:
                                a, blk = HD * (h % 2), h // 2
                            pe.wait_ge(*me.freed((s + m) % 2))
                            o = me.claim("Bs", (s + m) % 2)
                            last = nc.tensor.matmul(o[:, 0:nk], dfT[a:a + HD, 2 * kind, blk, qt * P:(qt + 1) * P],
                                                    dfT[a:a + HD, 2 * kind + 1, blk, 0:nk], start=True, stop=kind == 0)
                            if kind:
                                one = eye[0:FH, h:h + 1]
                                nc.tensor.matmul(o[:, 0:nk], fcv[:, 3, qt * P:(qt + 1) * P], one.broadcast_to([FH, nk]),
                                                 start=False, stop=False)
                                last = nc.tensor.matmul(o[:, 0:nk], one.broadcast_to([FH, P]), fcv[:, 4, 0:nk],
                                                        start=False, stop=True)
                            fill("Bs", last)
                    if 2 <= g < len(GROUPS) + 2:
                        kind, qt, h, s = GROUPS[g - 2]
                        if kind == 0:
                            pe.wait_ge(S["w_ready"], me.at(g - 1, "w_ready"))
                        else:
                            pe.wait_ge(S["p_ready"], me.at(s + 1, "p_ready"))
                        pe.wait_ge(*me.freed(4 + g % 2))
                        o = me.claim("BpT", 4 + g % 2)
                        src = pb[:, s % 4, :] if kind else wd[:, (g - 2) % 2, :]
                        for i in range(qt + 1):
                            last = nc.tensor.transpose(o[:, i * P:(i + 1) * P], src[:, i * P:(i + 1) * P], eye[:, :])
                        fill("BpT", last)
                    if g >= 3:
                        kind, qt, h, s = GROUPS[g - 3]
                        if kind and g - 3 == 2 * DH:
                            pe.wait_ge(emptied["proj"], me.at(20, "proj"))
                        pe.wait_ge(emptied["BpT"], me.at(g - 2, "BpT"))
                        vw = 2 * HD if kind == 0 else HD
                        if h == 0:
                            pe.wait_ge(*me.freed(6 + qt))
                            o_bank = me.claim("Bo", 6 + qt)
                        last = product(o_bank[:, h * vw:(h + 1) * vw],
                                       [pbT[:, (g - 3) % 3, i * P:(i + 1) * P] for i in range(qt + 1)],
                                       [dfv[:, kind, i, h * vw:(h + 1) * vw] for i in range(qt + 1)])
                        last.then_inc(S["Bpv"], 1)
                for n in range(4):
                    kind, qt = divmod(n, 2)
                    pe.wait_ge(S["y_ready"], me.at(n + 1, "y_ready"))
                    pe.wait_ge(*me.freed(n))
                    o = me.claim("yT", n)
                    for i in range(4):
                        last = nc.tensor.transpose(o[:, i * P:(i + 1) * P], yy[:, kind, qt, i * P:(i + 1) * P], eye[:, :])
                    fill("yT", last)
                pe.wait_ge(emptied["yT"], me.at(4, "yT"))
                slots = [next_chunk(), next_chunk()]
                for j in range(KD):
                    pe.wait_ge(*me.freed(j % 8))
                    o = me.claim("mg", j % 8)
                    for a in range(2):
                        last = product(o[:, a * SEQ:(a + 1) * SEQ],
                                       [ring[:, slots[a], k * D + j * P:k * D + (j + 1) * P] for k in range(4)],
                                       [yT[:, 4 * a + k, :] for k in range(4)])
                    fill("mg", last)
                used(2)
                pe.wait_ge(S["mT_ready"], me.at(KD, "mT_ready"))
                for half in range(2):
                    slot = next_chunk()
                    for t in range(LAT):
                        pe.wait_ge(*me.freed(half * LAT + t))
                        o = me.claim("By", half * LAT + t)
                        last = product(o[:, :], [mT[:, k, t * P:(t + 1) * P] for k in range(KD)],
                                       [ring[:, slot, k * CH:(k + 1) * CH] for k in range(KD)])
                        fill("By", last)
                    used()
                norm_T(("BxTv", "BxTs"), lambda t: ttok[:, t, :], S["Bxn"], LAT, name="Bxn", first=LAT)
                pe.wait_ge(emptied["BxTv"], me.at(4, "BxTv"))
                pe.wait_ge(emptied["BxTs"], me.at(4, "BxTs"))
                for c in range(5):
                    if c < 4:
                        slot = next_chunk()
                        for i in range(4):
                            columns("q2", 4 * (c % 2) + i, slot, i)
                        used()
                    if c >= 1:
                        pe.wait_ge(emptied["q2"], me.at(4 * c, "q2"))
                        for t in range(LAT):
                            b = 4 * (c % 2) + t if c < 4 else 4 + t
                            pe.wait_ge(*me.freed(b))
                            o = me.claim("sc", b)
                            for i in range(4):
                                last = nc.tensor.matmul(o[:, i * P:(i + 1) * P], qq[:, 4 * c - 4 + i, t * P:(t + 1) * P],
                                                        skT[:, i % 2, :], start=True, stop=True)
                                if i == 0:
                                    tell(last)
                            fill("sc", last)
                for t in range(LAT):
                    outs = [bank[2 * t], bank[2 * t + 1]]
                    if t == 0:
                        pe.wait_ge(emptied["sc"], me.at(8, "sc"))
                    for half in range(2):
                        nc.tensor.matmul(outs[half][:, :], eye[:, :], x[:, t, half * CH:(half + 1) * CH],
                                         start=True, stop=False, skip_group_check=True)
                    with pe.Fori(0, RUN) as i:
                        for n, j in enumerate(PROWS):
                            pe.wait_ge(row_in[j], me.at(i * 16 + (2 * t + 1) * RUN * 16 + 16, "row_in"))
                            pe.wait_ge(S["diag_ready"], me.at(i * NP + t * NP * RUN + n + 1, "diag_ready"))
                            for half in range(2):
                                last = nc.tensor.matmul(outs[half][:, :], diag[:, n, :],
                                                        expert[:, j, half * CH:(half + 1) * CH],
                                                        start=False, stop=False, skip_group_check=True)
                            last.then_inc(S["free_p"], 1)
                    pe.wait_ge(S["acc_ready"], me.at(t + 1, "acc_ready"))
                    for half in range(2):
                        last = nc.tensor.matmul(outs[half][:, :], eye[:, :], acc[:, half * CH:(half + 1) * CH],
                                                start=False, stop=True, skip_group_check=True)
                    fill("acc", last)

        @block.scalar
        def _(act):
            me = Side()

            def free(fam, ins):
                ins.then_inc(emptied[fam], 1)

            def load(dst, src, s):
                act.dma_start(dst, src).then_inc(s, 16)

            load(eye[:, :], A["eye"], vectors_in)
            load(rows[0:8, :], A["c"].rearrange("a (k p) -> (a k) p", p=P), vectors_in)
            load(rows[8:16, :], A["c_ctx"].rearrange("(k p) -> k p", p=P), vectors_in)
            for i, name in enumerate(("norm1_g", "norm2_g", "norm1_g_2")):
                load(rows[16 + 16 * i:32 + 16 * i, :], A[name].rearrange("l (k p) -> (l k) p", p=P), vectors_in)
            load(rows[64:72, :], A["b_spatial"].rearrange("l g p -> (l g) p"), vectors_in)
            load(x[:, 0:2, :], A["x"].rearrange("o (t p) n -> (o p) t n", p=P), x_in)
            load(x[:, 2:4, :], A["ctx"].rearrange("o (t p) n -> (o p) t n", p=P), x_in)
            act.wait_ge(filled["col"], me.next("col"))
            nc.scalar.activation(cols[:, :], bank[0][:, 0:72], ACT.Copy)
            act.wait_ge(cond_zero, 1)
            free("col", nc.scalar.activation(cond[:, :, 0:2], bank[0][:, 0:16].rearrange("p (v k) -> p k v", v=2), ACT.Silu))
            act.wait_ge(filled["rel"], me.next("rel"))
            free("rel", nc.scalar.activation(brow, bank[5][0:DH, 0:REL], ACT.Copy))
            units = 0
            for layer in range(LAYERS):
                NT = TILES if layer == 0 else LAT
                b = 6
                for g in range(2):
                    for v in range(2 if layer == 0 else 1):
                        for half in range(2):
                            act.wait_ge(filled["gate"], me.next("gate"))
                            free("gate", nc.scalar.activation(gate[:, g, v, half * CH:(half + 1) * CH],
                                                              bank[b % 8][:, :], ACT.Copy))
                            b += 1

                def norm_evac(which, tiles):
                    act.wait_ge(modA_ready, layer + 1)
                    for t in range(tiles):
                        act.wait_ge(filled["xTs"], me.next("xTs"))
                        for i in range(4):
                            k = 4 + i
                            last = nc.scalar.activation(hT[:, k, t * P:(t + 1) * P],
                                                        bank[(2 * t + 1) % 8][:, i * P:(i + 1) * P], ACT.Identity,
                                                        bias=modcol[:, 2 * which, k, t // 2:t // 2 + 1],
                                                        scale=modA[:, which, k, t // 2:t // 2 + 1])
                        free("xTs", last)

                if layer == 0:
                    act.wait_ge(bias_out, 16)
                norm_evac(0, TILES)
                b = 0
                for c in range(4):
                    for t in range(TILES if c == 1 else NT):
                        act.wait_ge(filled["z"], me.next("z"))
                        if c == 0:
                            o, i, f = z[:, t, 0:512], bank[b % 8][:, :], ACT.Copy
                        elif c == 1:
                            o, i, f = z[:, t, 512:768], bank[b % 8][:, 0:256], ACT.Copy
                        else:
                            o, i, f = ug[:, c - 2, t, :], bank[b % 8][:, :], ACT.Gelu_apprx_tanh
                        free("z", nc.scalar.activation(o, i, f))
                        b += 1
                act.wait_ge(filled["ws"], me.next("ws"))
                free("ws", nc.scalar.activation(wsT[:, :, :].rearrange("p g n -> p (g n)"), bank[b % 8][:, :], ACT.Copy))
                b += 1
                for t in range(TILES):
                    if t < NT:
                        act.wait_ge(filled["qkT"], me.next("qkT"))
                        free("qkT", nc.scalar.activation(
                            qT[:, :, t * P:(t + 1) * P], bank[b % 8][:, :].rearrange("p (a n) -> p a n", a=4),
                            ACT.Copy, scale=SCALE))
                        b += 1
                    act.wait_ge(filled["qkT"], me.next("qkT"))
                    free("qkT", nc.scalar.activation(
                        kT[:, :, t * P:(t + 1) * P], bank[b % 8][:, 0:256].rearrange("p (a n) -> p a n", a=2), ACT.Copy))
                    b += 1
                N = NT * AH
                for n in range(N + 1):
                    if n < N:
                        t, h = divmod(n, AH)
                        w = 512 if t < LAT else 256
                        act.wait_ge(nm_ready, units + n + 1)
                        if n >= 3:
                            act.wait_ge(filled["pT"], units + n - 2)
                        free("s", nc.scalar.activation(pr[:, n % 3, 0:w], bank[n % 3][:, 0:w], ACT.Exp,
                                                       bias=nm[:, n % 4:n % 4 + 1], accum_out=rs[:, n:n + 1]))
                    if n >= 1:
                        m = n - 1
                        w = 512 if m // AH < LAT else 256
                        act.wait_ge(filled["pT"], me.next("pT"))
                        if m >= 3:
                            act.wait_ge(pv_done, units + m - 2)
                        free("pT", nc.scalar.activation(prT[:, m % 3, 0:w], bank[3 + m % 3][:, 0:w], ACT.Copy))
                units += N
                for t in range(NT):
                    for half in range(2):
                        act.wait_ge(filled["mT"], me.next("mT"))
                        free("mT", nc.scalar.activation(
                            hT[:, 4 * half:4 * half + 4, t * P:(t + 1) * P],
                            bank[(2 * t + half) % 8][:, :].rearrange("p (a n) -> p a n", a=4), ACT.Copy))
                norm_evac(1, NT)

            with act.Fori(0, LAYERS) as l:
                me.new_layer(l)
                for t in range(LAT):
                    act.wait_ge(filled["BxTs"], me.next("BxTs"))
                    for i in range(4):
                        last = nc.scalar.activation(h2[:, 4 + i, t * P:(t + 1) * P],
                                                    bank[2 * t + 1][:, i * P:(i + 1) * P], ACT.Copy,
                                                    scale=gcol[:, 4 + i:5 + i])
                    free("BxTs", last)

                def projected(c, i, b):
                    act.wait_ge(filled["proj"], me.next("proj"))
                    if c >= 6:
                        ins = nc.scalar.activation(sig[:, c // 8, c % 2 * 4 + i, :], bank[b][:, 0:SEQ], ACT.Sigmoid)
                    elif c % 3 == 2:
                        ins = nc.scalar.activation(dfv[:, c // 3, i, :], bank[b][:, :], ACT.Copy)
                    else:
                        ins = nc.scalar.activation(dfT[:, c // 3 * 2 + c % 3, i, :], bank[b][:, 0:SEQ], ACT.Copy,
                                                   scale=SCALE if c % 3 == 0 else 1.0)
                    free("proj", ins)

                b = 4
                for c in range(3):
                    for i in range(LAT if c == 2 else 4):
                        projected(c, i, b % 8)
                        b += 1
                act.wait_ge(filled["sk"], me.next("sk"))
                free("sk", nc.scalar.activation(skT.rearrange("p a n -> p (a n)"), bank[b % 8][:, 0:256], ACT.Copy))
                act.wait_ge(S["lam_z"], me.at(1, "lam_z"))
                nc.scalar.activation(lam2[:, 4:6], lam2[:, 2:4], ACT.Exp).then_inc(S["lam_e"], 1)
                act.wait_ge(S["ff_z"], me.at(1, "ff_z"))
                nc.scalar.activation(fcv[:, 1, :], fcv[:, 1, :], ACT.Exp)
                act.drain()
                nc.scalar.activation(fcv[:, 2, :], fcv[:, 1, :], ACT.Ln, bias=1.0).then_inc(S["ff_e"], 1)
                for g, (what, c, i) in enumerate(BETWEEN):
                    if what != "ff":
                        projected(c, i, 2 + g % 2)
                    if g < len(GROUPS):
                        kind, qt, h, s0 = GROUPS[g]
                        nk = (qt + 1) * P
                        for s in range(s0, s0 + 2 - kind):
                            act.wait_ge(emptied["Bs"], me.at(s + 1, "Bs"))
                            if s >= 4:
                                old = GROUP_OF[s - 4]
                                if old < 2 * DH:
                                    act.wait_ge(S["w_ready"], me.at(old + 1, "w_ready"))
                                else:
                                    act.wait_ge(filled["BpT"], me.at(old + 1, "BpT"))
                            nc.scalar.activation(pb[:, s % 4, 0:nk], lg[:, s % 4, 0:nk], ACT.Exp, scale=-1.0,
                                                 bias=nm[:, s % 4:s % 4 + 1], accum_out=rs[:, s:s + 1]
                                                 ).then_inc(S["p_ready"], 1)
                    if 2 <= g < len(GROUPS) + 2:
                        kind, qt, h, s = GROUPS[g - 2]
                        act.wait_ge(filled["BpT"], me.next("BpT"))
                        if g >= 5:
                            act.wait_ge(S["Bpv"], me.at(g - 4, "Bpv"))
                        w = (qt + 1) * P
                        free("BpT", nc.scalar.activation(pbT[:, (g - 2) % 3, 0:w], bank[4 + g % 2][:, 0:w], ACT.Copy))
                for n in range(4):
                    kind, qt = divmod(n, 2)
                    act.wait_ge(filled["yT"], me.next("yT"))
                    free("yT", nc.scalar.activation(yT[:, 4 * kind:4 * kind + 4, qt * P:(qt + 1) * P],
                                                    bank[n][:, :].rearrange("p (a n) -> p a n", a=4), ACT.Copy))
                for t in range(LAT):
                    act.wait_ge(filled["BxTs"], me.next("BxTs"))
                    free("BxTs", nc.scalar.activation(h2[:, 4:8, t * P:(t + 1) * P],
                                                      bank[2 * t + 1][:, :].rearrange("p (a n) -> p a n", a=4), ACT.Copy))
                for c in range(5):
                    if c < 4:
                        for i in range(4):
                            act.wait_ge(filled["q2"], me.next("q2"))
                            free("q2", nc.scalar.activation(qq[:, 4 * c + i, :], bank[4 * (c % 2) + i][:, 0:SEQ], ACT.Copy))
                    if c >= 1:
                        for t in range(LAT):
                            act.wait_ge(filled["sc"], me.next("sc"))
                            b = 4 * (c % 2) + t if c < 4 else 4 + t
                            free("sc", nc.scalar.activation(sc[t][:, 4 * c - 4:4 * c, :],
                                                            bank[b][:, :].rearrange("p (a n) -> p a n", a=4), ACT.Copy))
                for t in range(LAT):
                    act.wait_ge(S["gate_z"], me.at(t + 1, "gate_z"))
                    nc.scalar.activation(gates[:, t, :], gates[:, t, :], ACT.Exp).then_inc(S["gate_e"], 1)
                    act.wait_ge(S["dotted"], me.at(t + 1, "dotted"))
                    nc.scalar.activation(dots[:, t, :], dots[:, t, :], ACT.Gelu).then_inc(S["acted"], 1)
                    act.wait_ge(S["weighed"], me.at(t + 1, "weighed"))
                    with act.Fori(0, RUN) as i:
                        for n, j in enumerate(PROWS):
                            act.wait_ge(S["free_p"], me.at(i * NP + t * NP * RUN + n + 1, "free_p"))
                            nc.scalar.activation(diag[:, n, :], eye[:, :], ACT.Copy,
                                                 scale=dots[:, t, bass.ds(i * ROWS + j, 1)]).then_inc(S["diag_ready"], 1)

        @block.vector
        def _(dve):
            me = Side()
            v = nc.vector

            def flush():
                return dve.drain()

            def free(fam, ins):
                ins.then_inc(emptied[fam], 1)

            def rstd(o, i, n):
                w = i.shape[1]
                m, y, a, b = (nw[:, k, 0:w] for k in range(4))
                v.tensor_scalar(m, i, 1.0 / n, EPS, ALU.mult, ALU.add)
                flush()
                v.tensor_single_scalar(a.bitcast(U32), m.bitcast(U32), 1, ALU.logical_shift_right)
                flush()
                v.tensor_scalar(y.bitcast(U32), a.bitcast(U32), -1.0, float(0x5F3759DF), ALU.mult, ALU.add)
                flush()
                for step in range(3):
                    v.tensor_tensor(a, y, y, ALU.mult)
                    flush()
                    v.scalar_tensor_tensor(b, a, -0.5, m, ALU.mult, ALU.mult)
                    flush()
                    v.scalar_tensor_tensor(y if step < 2 else o, b, 1.5, y, ALU.add, ALU.mult)
                    flush()

            def row_stats(tiles):
                for t in range(tiles):
                    v.tensor_tensor_reduce(out=xn[:, t % 2, :], in0=x[:, t, :], in1=x[:, t, :], scale=1.0,
                                           scalar=0.0, op0=ALU.mult, op1=ALU.add, accum_out=ss[:, t:t + 1])
                    if t % 2:
                        flush()
                rstd(rst[:, 0:tiles], ss[:, 0:tiles], D)

            def row_norm(t, o):
                return v.tensor_scalar(o, x[:, t, :], rst[:, t:t + 1], None, ALU.mult)

            v.memset(cond[:, :, :], 0.0).then_inc(cond_zero, 1)
            dve.wait_ge(emptied["col"], me.at(1, "col"))
            dve.wait_ge(x_in, 32)
            v.memset(st[:, :], 1.0)

            def modulation(c, b):
                q = 32 * (c % 4)
                dve.wait_ge(filled["mod"], me.next("mod"))
                row, spare = modrow[c // 4][q:q + 2, :], [modt[q:q + 2, i, :] for i in range(2)]
                v.tensor_copy(row, bank[b][0:2, :])
                v.tensor_copy(spare[0], bank[b][32:34, :])
                v.tensor_copy(spare[1], bank[b][64:66, :])
                flush()
                v.tensor_tensor(row, row, spare[0], ALU.add)
                flush()
                v.tensor_copy(spare[0], bank[b][96:98, :])
                v.tensor_tensor(row, row, spare[1], ALU.add)
                flush()
                v.tensor_tensor(row, row, spare[0], ALU.add)
                flush()
                free("mod", v.tensor_tensor(row, row, bmod[c // 4][q:q + 2, :], ALU.add))
                flush()

            dve.wait_ge(bmod_in, 16 * 12)
            for c in range(12):
                modulation(c, c % 8)
            transposed, units = 0, 0
            for layer in range(LAYERS):
                NT = TILES if layer == 0 else LAT
                for g in range(4):
                    dve.wait_ge(filled["modT"], me.next("modT"))
                    for n, (kind, half) in enumerate(SHIFTS[g]):
                        last = v.tensor_copy(modcol[:, COLUMN[kind], 4 * half:4 * half + 4, :],
                                             bank[1 + g][:, 8 * n:8 * n + 8].rearrange("p (k v) -> p k v", v=2))
                    free("modT", last)
                flush()
                for which in range(2):
                    g = cols[:, 16 + 16 * which + 8 * layer:24 + 16 * which + 8 * layer]
                    v.scalar_tensor_tensor(modA[:, which, :, :], modcol[:, 2 * which + 1, :, :], 1.0,
                                           spread(g, 2, 2), ALU.add, ALU.mult)
                flush().then_inc(modA_ready, 1)

                def norm(which, tiles):
                    nonlocal transposed
                    if transposed:
                        dve.wait_ge(filled["xTs"], transposed)
                    row_stats(tiles)
                    for t in range(tiles + 1):
                        if t < tiles:
                            if transposed + t - 2 >= 0:
                                dve.wait_ge(filled["xTs"], transposed + t - 1)
                            row_norm(t, xn[:, t % 2, :]).then_inc(xn_ready, 1)
                        if t >= 1:
                            dve.wait_ge(filled["xTv"], me.next("xTv"))
                            u = t - 1
                            for i in range(4):
                                last = v.tensor_scalar(hT[:, i, u * P:(u + 1) * P], bank[2 * u % 8][:, i * P:(i + 1) * P],
                                                       modA[:, which, i, u // 2:u // 2 + 1],
                                                       modcol[:, 2 * which, i, u // 2:u // 2 + 1], ALU.mult, ALU.add)
                            free("xTv", last)
                    transposed += tiles

                norm(0, TILES)
                zcount = (0 if layer == 0 else 16)
                dve.wait_ge(wide_in, 12 * 16 * (layer + 1))
                def heads(ap, t):
                    return ap[:, (0 if t < NT else AH) * HD:(AH + AKV) * HD].rearrange("p (h n) -> p h n", n=HD)

                def head_stats(t):
                    return st[:, t * 10 + (0 if t < NT else AH):t * 10 + 10]

                for t in range(TILES):
                    dve.wait_ge(emptied["z"], me.at(zcount + NT + t + 1, "z"))
                    a, zt = heads(tA, t), heads(z[:, t, :], t)
                    v.tensor_tensor(a, zt, zt, ALU.mult)
                    flush()
                    v.tensor_reduce(head_stats(t), a, AX.X, ALU.add)
                    flush()
                rstd(st[:, 0:40], st[:, 0:40], HD)
                for t in range(TILES):
                    a, b, zt = heads(tA, t), heads(tB, t), heads(z[:, t, :], t)
                    nh = a.shape[1]
                    v.tensor_tensor(a, zt, spread(head_stats(t), 2, HD), ALU.mult)
                    flush()
                    v.tensor_tensor(a, a, heads(gq, t), ALU.mult)
                    flush()
                    if t < LAT:
                        for off in range(0, HD, 16):
                            oth = off + 16 if off % 32 == 0 else off - 16
                            v.tensor_tensor(b[:, :, off:off + 16], a[:, :, oth:oth + 16],
                                            spread(rope[:, t, 1, off:off + 16], 1, nh), ALU.mult)
                        flush()
                        v.tensor_tensor(a, a, spread(rope[:, t, 0, :], 1, nh), ALU.mult)
                        flush()
                    if layer or t:
                        dve.wait_ge(filled["qkT"], 2 * TILES * layer + t + min(t, NT))
                    kq, kb = a[:, nh - AKV:nh, :], b[:, nh - AKV:nh, :]
                    qo = qn[:, 0:QW].rearrange("p (h n) -> p h n", n=HD)
                    ko = qn[:, QW:768].rearrange("p (j c n) -> p j c n", j=AKV, c=2)
                    if t < LAT:
                        v.tensor_tensor(qo, a[:, 0:AH, :], b[:, 0:AH, :], ALU.add)
                    elif t < NT:
                        v.tensor_copy(qo, a[:, 0:AH, :])
                    for c in range(2):
                        if t < LAT:
                            v.tensor_tensor(ko[:, :, c, :], kq, kb, ALU.add)
                        else:
                            v.tensor_copy(ko[:, :, c, :], kq)
                    flush().then_inc(qn_ready, 1)
                groups = lambda t: ug[:, 1, t, :].rearrange("p (g n) -> p g n", g=4)
                for t in range(NT):
                    dve.wait_ge(emptied["z"], me.at(zcount + NT + TILES + NT + t + 1, "z"))
                    v.tensor_reduce(st[:, 40 + 4 * t:44 + 4 * t], groups(t), AX.X, ALU.add)
                flush()
                v.tensor_scalar(st[:, 40:40 + 4 * NT], st[:, 40:40 + 4 * NT], 1.0 / P, None, ALU.mult)
                flush()
                for t in range(NT):
                    v.tensor_tensor(groups(t), groups(t), spread(st[:, 40 + 4 * t:44 + 4 * t], 2, P), ALU.subtract)
                    flush()
                    v.tensor_tensor(tA[:, 0:GW], ug[:, 1, t, :], ug[:, 1, t, :], ALU.mult)
                    flush()
                    v.tensor_reduce(st[:, 56 + 4 * t:60 + 4 * t], tA[:, 0:GW].rearrange("p (g n) -> p g n", g=4),
                                    AX.X, ALU.add)
                    flush()
                rstd(st[:, 56:56 + 4 * NT], st[:, 56:56 + 4 * NT], P)
                for t in range(NT):
                    v.tensor_tensor(groups(t), groups(t), spread(st[:, 56 + 4 * t:60 + 4 * t], 2, P), ALU.mult)
                    flush()
                    v.tensor_tensor(ug[:, 1, t, :], ug[:, 1, t, :], ggain[:, :], ALU.mult)
                    flush().then_inc(vn_ready, 1)
                b = NT * 3 + TILES + 1 + TILES + NT
                for t in range(NT):
                    dve.wait_ge(filled["sp"], me.next("sp"))
                    for g in range(4):
                        at = slice(g * P, (g + 1) * P)
                        c = 64 + 4 * layer + g
                        last = v.scalar_tensor_tensor(gm[:, t, at], bank[b % 8][:, at], cols[:, c:c + 1], ug[:, 0, t, at],
                                                      ALU.add, ALU.mult)
                    free("sp", last)
                    b += 1
                N = NT * AH

                def attn_out(t):
                    w = rs[:, t * AH:(t + 1) * AH]
                    dve.wait_ge(pv_done, units + (t + 1) * AH)
                    v.reciprocal(rr[:, :], w)
                    flush()
                    free("o", v.tensor_tensor(z[:, t, 0:512].rearrange("p (h n) -> p h n", n=HD),
                                              bank[6 + t % 2][:, :].rearrange("p (h n) -> p h n", n=HD),
                                              spread(rr[:, :], 2, HD), ALU.mult))
                    flush().then_inc(mix_ready, 1)

                for n in range(N):
                    t = n // AH
                    w = 512 if t < LAT else 256
                    if t and n % AH == 3:
                        attn_out(t - 1)
                    dve.wait_ge(filled["s"], me.next("s"))
                    if n >= 4:
                        dve.wait_ge(emptied["s"], me.at(units + n - 3, "s"))
                    v.tensor_reduce(nm[:, n % 4:n % 4 + 1], bank[n % 3][:, 0:w], AX.X, ALU.max, negate=True
                                    ).then_inc(nm_ready, 1)
                attn_out(NT - 1)
                units += N

                def gated(fam, which, at, banks):
                    for half in range(2):
                        for t in range(NT):
                            dve.wait_ge(filled[fam], me.next(fam))
                            cut = slice(half * CH, (half + 1) * CH)
                            tmp = xn[:, t % 2, 0:CH]
                            free(fam, v.tensor_tensor(tmp, bank[banks(half, t)][:, :], gate[:, which, t // 2, cut], ALU.mult))
                            flush()
                            v.tensor_tensor(x[:, t, cut], x[:, t, cut], tmp, ALU.add)
                            flush()

                gated("y", 0, 0, lambda half, t: (half * NT + t) % 8)
                norm(1, NT)
                for c in range(32):
                    dve.wait_ge(filled["f1"], me.next("f1"))
                    s = bank[c % 7][:, 0:NT * P]
                    v.tensor_scalar(xn[:, c % 2, 0:NT * P], s, 0.0, None, ALU.max)
                    flush()
                    free("f1", v.tensor_tensor(h1T[:, c, 0:NT * P], s, xn[:, c % 2, 0:NT * P], ALU.mult))
                    if layer == 0 and c % 4 == 3:
                        if c == 3:
                            dve.wait_ge(bmod_in, 2 * 16 * 12)
                        modulation(c // 4, 7)
                if layer == 0:
                    for c in range(8, 12):
                        modulation(c, 7)
                gated("f2", 1, 0, lambda half, t: half * NT + t)
            v.memset(layerE[:, :], 0.0)
            flush().then_inc(layer_done, 1)

            dve.drain().then_inc(scratch_free, 1)
            dve.wait_ge(bias_in, 32)
            with dve.Fori(0, LAYERS) as l:
                me.new_layer(l)
                v.tensor_copy(gcol[:, :], cols[:, bass.ds(l * KD + 48, KD)])
                flush()
                row_stats(LAT)
                for t in range(LAT):
                    row_norm(t, xn[:, t, :]).then_inc(S["Bxn"], 1)
                for t in range(LAT):
                    dve.wait_ge(filled["BxTv"], me.next("BxTv"))
                    for i in range(4):
                        last = v.tensor_scalar(h2[:, i, t * P:(t + 1) * P], bank[2 * t][:, i * P:(i + 1) * P],
                                               gcol[:, i:i + 1], None, ALU.mult)
                    free("BxTv", last)
                dve.wait_ge(S["small_in"], me.at(PER["small_in"], "small_in"))
                v.tensor_tensor(lamp, lamrow[:, 0::2, :], lamrow[:, 1::2, :], ALU.mult)
                v.tensor_scalar(subln, subln, lam2[:, 1:2], None, ALU.mult)
                flush()
                v.tensor_reduce(lam2[:, 2:4], lamp, AX.X, ALU.add)
                flush().then_inc(S["lam_z"], 1)
                dve.wait_ge(filled["ff"], me.next("ff"))
                free("ff", v.tensor_scalar(fcv[:, 0, :], bank[2][0:FH, 0:SEQ], bfc[:, :], None, ALU.add))
                flush()
                v.tensor_scalar(fcv[:, 1, :], fcv[:, 0, :], -1.0, None, ALU.mult)
                v.memset(fcv[:, 5, :], 1.0)
                flush()
                v.tensor_tensor(fcv[:, 1, :], fcv[:, 1, :], fcv[:, 0, :], ALU.min)
                flush().then_inc(S["ff_z"], 1)
                dve.wait_ge(S["ff_e"], me.at(1, "ff_e"))
                v.scalar_tensor_tensor(fcv[:, 2, :], fcv[:, 0, :], 0.0, fcv[:, 2, :], ALU.min, ALU.subtract)
                flush()
                v.tensor_tensor_scan(fcv[:, 3, :], fcv[:, 5, :], fcv[:, 2, :], 0.0, ALU.mult, ALU.add)
                flush()
                v.tensor_scalar(fcv[:, 4, :], fcv[:, 3, :], -1.0, None, ALU.mult)
                dve.wait_ge(S["lam_e"], me.at(1, "lam_e"))
                v.tensor_tensor(lam2[:, 6:7], lam2[:, 5:6], lam2[:, 4:5], ALU.subtract)
                flush().then_inc(S["c_ready"], 1)
                v.tensor_tensor(lam2[:, 7:8], lam2[:, 6:7], lam2[:, 0:1], ALU.subtract)
                flush()

                def heads_out(n):
                    kind, qt = divmod(n, 2)
                    dve.wait_ge(S["Bpv"], me.at(LAST_GROUP[n] + 1, "Bpv"))
                    y = yy[:, kind, qt, :]
                    if kind:
                        v.reciprocal(rr[:, :], rs[:, 16 + 8 * qt:24 + 8 * qt])
                        flush()
                        free("Bo", v.tensor_tensor(y.rearrange("p (h n) -> p h n", n=HD),
                                                   bank[6 + qt][:, :].rearrange("p (h n) -> p h n", n=HD),
                                                   spread(rr[:, :], 2, HD), ALU.mult))
                        flush().then_inc(S["y_ready"], 1)
                        return
                    free("Bo", v.tensor_copy(y, bank[6 + qt][:, :]))
                    flush()
                    v.tensor_tensor(tM.rearrange("p a n -> p (a n)"), y, y, ALU.mult)
                    flush()
                    v.tensor_reduce(st[:, 0:4], tM.rearrange("p a (b n) -> p (a b) n", n=P), AX.X, ALU.add)
                    flush()
                    rstd(st[:, 0:4], st[:, 0:4], P)
                    yv = y.rearrange("p (h n) -> p h n", n=P)
                    v.tensor_tensor(yv, yv, spread(st[:, 0:4], 2, P), ALU.mult)
                    flush()
                    v.tensor_tensor(yv, yv, spread(subln, 1, DH), ALU.mult)
                    flush().then_inc(S["y_ready"], 1)

                outs = 0
                for g in range(len(GROUPS) + 1):
                    if outs < 4 and g - 5 >= LAST_GROUP[outs]:
                        heads_out(outs)
                        outs += 1
                    if g < len(GROUPS):
                        kind, qt, h, s0 = GROUPS[g]
                        nk = (qt + 1) * P
                        for s in range(s0, s0 + 2 - kind):
                            dve.wait_ge(filled["Bs"], me.next("Bs"))
                            dve.nop(nofuse=True)
                            if s >= 4:
                                dve.wait_ge(S["p_ready"], me.at(s - 3, "p_ready"))
                                dve.nop(nofuse=True)
                            add = mask if kind else bias[:, h, :]
                            v.tensor_tensor_reduce(out=lg[:, s % 4, 0:nk], in0=bank[s % 2][:, 0:nk],
                                                   in1=add[:, SEQ - nk:SEQ], scale=-1.0, scalar=3.0e38, op0=ALU.add,
                                                   op1=ALU.min, accum_out=nm[:, s % 4:s % 4 + 1]
                                                   ).then_inc(emptied["Bs"], 1)
                    if g >= 1:
                        kind, qt, h, s = GROUPS[g - 1]
                        if kind == 0:
                            nk = (qt + 1) * P
                            dve.wait_ge(S["p_ready"], me.at(s + 2, "p_ready"))
                            v.reciprocal(rr[:, 0:2], rs[:, s:s + 2])
                            flush()
                            v.tensor_scalar(rr[:, 2:3], rr[:, 1:2], lam2[:, 7:8], None, ALU.mult)
                            if g >= 3:
                                dve.wait_ge(filled["BpT"], me.at(g - 2, "BpT"))
                            wv = wd[:, (g - 1) % 2, 0:nk]
                            v.tensor_scalar(wv, pb[:, s % 4, 0:nk], rr[:, 0:1], None, ALU.mult)
                            flush()
                            v.scalar_tensor_tensor(wv, pb[:, (s + 1) % 4, 0:nk], rr[:, 2:3], wv, ALU.mult, ALU.add)
                            flush().then_inc(S["w_ready"], 1)
                while outs < 4:
                    heads_out(outs)
                    outs += 1
                dve.wait_ge(emptied["proj"], me.at(36, "proj"))
                for j in range(KD):
                    dve.wait_ge(filled["mg"], me.next("mg"))
                    free("mg", v.tensor_tensor(tM, bank[j % 8][:, :].rearrange("p (a n) -> p a n", a=2),
                                               sig[:, :, j, :], ALU.mult))
                    flush()
                    v.tensor_tensor(mT[:, j, :], tM[:, 0, :], tM[:, 1, :], ALU.add)
                    flush().then_inc(S["mT_ready"], 1)
                for half in range(2):
                    for t in range(LAT):
                        dve.wait_ge(filled["By"], me.next("By"))
                        cut = slice(half * CH, (half + 1) * CH)
                        free("By", v.tensor_tensor(x[:, t, cut], x[:, t, cut], bank[half * LAT + t][:, :], ALU.add))
                flush()
                dve.wait_ge(S["gain_in"], me.at(16, "gain_in"))
                row_stats(LAT)
                for t in range(LAT):
                    row_norm(t, xn[:, t, :])
                    flush()
                    v.tensor_tensor(ttok[:, t, :], xn[:, t, :], wide[:, :], ALU.mult).then_inc(S["Bxn"], 1)
                for t in range(LAT):
                    dve.wait_ge(filled["BxTv"], me.next("BxTv"))
                    free("BxTv", v.tensor_copy(h2[:, 0:4, t * P:(t + 1) * P],
                                               bank[2 * t][:, :].rearrange("p (a n) -> p a n", a=4)))

                def top16(src, spare, o, where, n, w):
                    s = [src[:, i * w:(i + 1) * w] for i in range(n)]
                    r = [spare[:, i * w:(i + 1) * w] for i in range(n)]
                    for i in range(n):
                        v.max(out=o[:, i, 0:8], in_=s[i])
                    flush()
                    for i in range(n):
                        v.max_index(out=where[:, i, 0:8], in_max=o[:, i, 0:8], in_values=s[i])
                        v.match_replace(out=r[i], in_to_replace=o[:, i, 0:8], in_values=s[i], imm_value=-3.0e38)
                    flush()
                    yield
                    for i in range(n):
                        v.max(out=o[:, i, 8:16], in_=r[i])
                    flush()
                    for i in range(n):
                        v.max_index(out=where[:, i, 8:16], in_max=o[:, i, 8:16], in_values=r[i])
                    flush()

                def search(t, c):
                    dve.wait_ge(emptied["sc"], me.at(2 * c + t + 1, "sc"))
                    dve.nop(nofuse=True)
                    yield from top16(scores[t][:, 4 * c * NK:4 * (c + 1) * NK], w1, tv, ti, 4, NK)
                    v.tensor_copy(tif, ti)
                    for h in range(2):
                        v.tensor_tensor(w1[:, h * 256:(h + 1) * 256].rearrange("p (a b) -> p a b", a=16),
                                        spread(tv[:, 2 * h, :], 2, 16), spread(tv[:, 2 * h + 1, :], 1, 16), ALU.add)
                    flush()
                    yield
                    yield from top16(w1, w2, bv, bp, 2, 256)
                    mine = slice(32 * c, 32 * c + 32)
                    v.tensor_single_scalar(bi[:, 0], bp, 4, ALU.logical_shift_right)
                    v.tensor_single_scalar(bi[:, 1], bp, 15, ALU.bitwise_and)
                    v.tensor_tensor(gates[:, t, mine].rearrange("p (h n) -> p h n", n=16), bv,
                                    bv[:, :, 0:1].broadcast_to([P, 2, 16]), ALU.subtract)
                    flush()
                    v.tensor_copy(bf, bi)
                    flush()
                    for a in range(2):
                        one = w1[:, a * 512:(a + 1) * 512]
                        v.tensor_tensor(one.rearrange("p (a b) -> p a b", b=16),
                                        spread(bf[:, a].rearrange("p h n -> p (h n)"), 2, 16),
                                        spread(iota[:, :], 1, 32), ALU.is_equal)
                    flush()
                    yield
                    for a in range(2):
                        for h in range(2):
                            wv = w1[:, a * 512 + h * 256:a * 512 + (h + 1) * 256].rearrange("p (a b) -> p a b", a=16)
                            v.tensor_tensor(wv, wv, spread(tif[:, 2 * h + a, :], 1, 16), ALU.mult)
                    flush()
                    yield
                    v.tensor_reduce(ei[:, 0, :], w1.rearrange("p (a b) -> p a b", b=16), AX.X, ALU.add)
                    flush()
                    v.tensor_scalar(ei[:, 1, 0:32], ei[:, 0, 0:32], float(NK), layerE[:, :], ALU.mult, ALU.add)
                    flush()
                    v.tensor_tensor(ei[:, 1, 0:32], ei[:, 1, 0:32], ei[:, 0, 32:64], ALU.add)
                    flush()
                    pick = v.tensor_copy(picks[:, t, mine], ei[:, 1, 0:32])
                    if c == 3:
                        pick.then_inc(S["picked"], 1)
                        flush().then_inc(S["gate_z"], 1)
                    yield

                for c in range(4):
                    for _ in search(0, c):
                        pass

                for t in range(LAT):
                    dve.wait_ge(S["gate_e"], me.at(t + 1, "gate_e"))
                    gt = gates[:, t, :].rearrange("p (h n) -> p h n", n=16)
                    v.tensor_reduce(rr[:, :], gt, AX.X, ALU.add)
                    flush()
                    v.reciprocal(rr[:, :], rr[:, :])
                    flush()
                    v.tensor_tensor(gt, gt, spread(rr[:, :], 2, 16), ALU.mult)
                    flush()
                    with dve.Fori(0, RUN) as i:
                        for j in range(ROWS):
                            dve.wait_ge(row_in[j], me.at(i * 16 + 2 * t * RUN * 16 + 16, "row_in"))
                            v.tensor_tensor_reduce(out=junk[j % 2], in0=expert[:, j, :], in1=ttok[:, t, :], scale=1.0,
                                                   scalar=0.0, op0=ALU.mult, op1=ALU.add, accum_out=d16[:, j:j + 1]
                                                   ).then_inc(S["free_v"], 1)
                            if j % 2:
                                flush()
                        v.tensor_copy(dots[:, t, bass.ts(i, ROWS)], d16[:, :])
                        flush()
                    flush().then_inc(S["dotted"], 1)
                    v.memset(acc, 0.0)
                    dve.wait_ge(S["acted"], me.at(t + 1, "acted"))
                    v.tensor_tensor(dots[:, t, :], dots[:, t, :], gates[:, t, :], ALU.mult)
                    flush().then_inc(S["weighed"], 1)
                    def add_row(i, j):
                        dve.wait_ge(row_in[j], me.at(i * 16 + (2 * t + 1) * RUN * 16 + 16, "row_in"))
                        v.scalar_tensor_tensor(acc, expert[:, j, :],
                                               dots[:, t, bass.ds(i * ROWS + j, 1)], acc,
                                               ALU.mult, ALU.add).then_inc(S["free_v"], 1)
                        flush()

                    if t == 0:
                        parts = (part for c in range(4) for part in search(1, c))
                        for i in range(RUN):
                            for j in VROWS:
                                add_row(i, j)
                                next(parts, None)
                        dve.drain().then_inc(scratch_free, 1)
                    else:
                        with dve.Fori(0, RUN) as i:
                            for j in VROWS:
                                add_row(i, j)
                    flush().then_inc(S["acc_ready"], 1)
                    if t == LAT - 1:
                        for u in range(LAT):
                            dve.wait_ge(filled["acc"], me.next("acc"))
                            for half in range(2):
                                last = v.tensor_copy(x[:, u, half * CH:(half + 1) * CH], bank[2 * u + half][:, :])
                            free("acc", last)
                    else:
                        dve.wait_ge(filled["acc"], me.at(t + 1, "acc"))
                        dve.nop(nofuse=True)
                v.tensor_scalar(layerE[:, :], layerE[:, :], float(NE), None, ALU.add)
                flush().then_inc(layer_done, 1)

            dve.wait_ge(final_in, 16)
            row_stats(LAT)
            for t in range(LAT):
                row_norm(t, xn[:, t, :])
                flush()
                v.tensor_tensor(xn[:, t, :], xn[:, t, :], wide[:, :], ALU.mult)
            flush().then_inc(result_ready, 1)
        return nc


_INS = ["x", "c", "ctx", "c_ctx", "w_mod", "b_mod", "norm1_g", "w_in", "q_norm_g", "k_norm_g",
        "gmlp_norm_g", "w_spatial", "b_spatial", "w_out", "norm2_g", "w_ff1", "w_ff2", "norm1_g_2",
        "w_in_2", "b_forget_2", "diff_lambda_2", "diff_subln_g_2", "w_diff_o_2", "w_fox_o_2",
        "w_out_2", "norm2_g_2", "w_query_2", "sub_keys_2", "expert_u_2", "expert_v_2",
        "rel_bias_2", "final_norm_g_2"]


def kernel(**inputs):
    import concourse.bacc as bacc
    from concourse.bass_utils import run_bass_kernel_spmd as run

    nc = bacc.Bacc("TRN2", target_bir_lowering=False, num_devices=1)
    arrays, views = {}, {}
    named = {k: np.ascontiguousarray(inputs[k]) for k in _INS}
    for name, a in {**named, **constants()}.items():
        arrays[f"in_{name}"] = a
        views[name] = nc.dram_tensor(f"in_{name}", a.shape, mybir.dt.from_np(a.dtype), kind="ExternalInput").ap()
    out = nc.dram_tensor("out_x", (1, SEQ, D), F32, kind="ExternalOutput").ap()
    build(nc, views, out)
    r = run(nc, [arrays], core_ids=[0])
    return r.results[0]["out_x"]
```

```python
import math
from contextlib import ExitStack

import numpy as np

import concourse.bass as bass
from concourse import mybir

F32 = mybir.dt.float32
F32R = mybir.dt.float32r
U32 = mybir.dt.uint32
ALU = mybir.AluOpType
ACT = mybir.ActivationFunctionType
AX = mybir.AxisListType

P = 128
D = 1024
KD = D // P
LAYERS = 2
LAT = 2
TILES = 4
SEQ = LAT * P
HD = 64
AH, AKV = 8, 2
QW, KVW, GW = 512, 128, 512
ZW = QW + 2 * KVW
FF = 4 * D
EPS = 1e-6
CH = 512
SLOTS = 4
SCALE = HD ** -0.5
DH, FH = 4, 8
W2IN = 5128
FFCOL = 3072
PH, TOPK, NK = 8, 16, 128
NE = NK * NK
VECTORS, CONSTS = 8, 9
CHUNKS_A, CHUNKS_B = 84, 18
STEPS = [(0, 0)] + [s for c in range(1, 8) for s in ((0, c), (1, c - 1))] + [(1, 7)]
QUARTERS = 4 * len(STEPS)
SEARCH_SLOT = (CHUNKS_B - 4) % SLOTS
PICKS = PH * TOPK
ROWS = 16
HALF = ROWS // 2
NEG = -1.0e30
REL = 384


def t5_bucket(dist, buckets=32, far=128):
    n = np.maximum(dist, 0)
    exact = buckets // 2
    nf = np.maximum(n, 1).astype(np.float32)
    large = exact + (np.log(nf / np.float32(exact)) / np.float32(math.log(far / exact))
                     * np.float32(buckets - exact)).astype(np.int32)
    return np.where(n < exact, n, np.minimum(large, buckets - 1))


def constants():
    tok = np.arange(SEQ)
    pos = np.stack([tok // 64, tok % 64], 1).astype(np.float32)
    freq = (10000.0 ** (-np.arange(16, dtype=np.float32) / 16)).astype(np.float32)
    ang = (pos[:, :, None] * freq).astype(np.float32)
    cos, sin = np.cos(ang), np.sin(ang)
    rope = np.zeros((SEQ, 2, 2, 2, 16), np.float32)
    rope[:, 0] = cos[:, :, None, :]
    rope[:, 1, :, 0], rope[:, 1, :, 1] = -sin, sin
    dist = 255 - np.arange(REL)
    onehot = np.zeros((33, REL), np.float32)
    onehot[t5_bucket(dist), np.arange(REL)] = dist >= 0
    onehot[32] = np.where(dist >= 0, 0.0, NEG)
    q, k = np.arange(P)[:, None], np.arange(SEQ)[None]
    mask = np.where(128 + q - k >= 0, 0.0, NEG).astype(np.float32)
    lam = [0.8 - 0.6 * math.exp(-0.3 * i) for i in range(LAYERS)]
    fold = np.zeros((P, 32), np.float32)
    fold[32 * np.arange(4), 0] = fold[32 * np.arange(4) + 1, 1] = 1.0
    pickv = np.zeros((2, 2, P), np.float32)
    pickv[np.arange(2), np.arange(2)] = 1.0
    return {
        "rope": rope.reshape(SEQ, 128), "onehot": onehot, "mask": mask,
        "ones4": np.ones((1, DH), np.float32),
        "fold": fold,
        "pickv": pickv.reshape(2, 256),
        "lam": np.array([[a, 1 - a] for a in lam], np.float32),
        "iota16": np.arange(16, dtype=np.float32)[None], "eye": np.eye(P, dtype=np.float32),
    }


def build(nc, A, out):
    ctx = ExitStack()
    with ctx:
        ctx.enter_context(nc.allow_non_contiguous_dma("small strided loads"))

        def sb(name, shape, dt=F32):
            return ctx.enter_context(nc.sbuf_tensor(name, shape, dt))

        def sem(name):
            return ctx.enter_context(nc.semaphore(name))

        def spread(ap, axis, n):
            ap = ap.unsqueeze(axis)
            shape = list(ap.shape)
            shape[axis] = n
            return ap.broadcast_to(shape)

        ring = sb("ring", [P, SLOTS, KD * CH])
        x = sb("x", [P, TILES, D])
        hT = sb("hT", [P, KD, TILES * P])
        big_at = nc.sbuf_base
        big = sb("big", [P, 16384])

        def over_big(name, shape, word):
            return nc.alloc_sbuf_tensor_at(name, shape, F32R, offset=big_at + 4 * word)

        w_hi = over_big("w_hi", [P, 4, KD * P], 0)
        w_lo = over_big("w_lo", [P, 4, KD * P], 4096)
        h_hi = over_big("h_hi", [P, KD, SEQ], 8192)
        h_lo = over_big("h_lo", [P, KD, SEQ], 10240)
        u_hi = over_big("u_hi", [P, 2, 4, SEQ], 12288)
        u_lo = over_big("u_lo", [P, 2, 4, SEQ], 14336)
        gate = sb("gate", [P, 2, 2, D])
        xn = sb("xn", [P, 2, D])
        kT = sb("kT", [P, 2, TILES * P])
        wide = sb("wide", [P, D])
        ggain = sb("ggain", [P, GW])
        wsp = sb("wsp", [P, 4, P])
        wsT = sb("wsT", [P, 4, P])
        eye = sb("eye", [P, P])
        rows = sb("rows", [72, P])
        cols = sb("cols", [P, 72])
        fold = sb("fold", [P, 32])
        cond = sb("cond", [P, KD, 32])
        pickv = sb("pickv", [P, 2, P])
        rope = sb("rope", [P, LAT, 2, HD])
        modcol = sb("modcol", [P, 4, KD, 2])
        modA = sb("modA", [P, 2, KD, 2])
        ss = sb("ss", [P, 4])
        rst = sb("rst", [P, 4])
        st = sb("st", [P, 72])
        nw = sb("nw", [P, 4, 40])
        nm = sb("nm", [P, 4])
        rs = sb("rs", [P, 32])
        rr = sb("rr", [P, 8])
        lam2 = sb("lam2", [P, 8])
        layerE = sb("layerE", [P, 1])
        gcol = sb("gcol", [P, KD])
        iota = sb("iota", [P, 16])
        rel = sb("rel", [33, DH])
        bfc = sb("bfc", [FH, 1])
        picks = sb("picks", [P, LAT, PICKS], U32)
        gates = sb("gates", [P, LAT, PICKS])
        dots = sb("dots", [P, LAT, PICKS])
        d16 = sb("d16", [P, ROWS])
        pick_now = sb("pick_now", [P, 2, HALF], U32)
        bias_rows = nc.dram_tensor("bias_rows", [DH, P, REL], F32).ap()

        modrow = [kT[:, 0, :], kT[:, 1, :], wsT[:, :, :].rearrange("p g n -> p (g n)")]
        bmod = [wide[:, 0:CH], wide[:, CH:2 * CH], ggain[:, :]]
        modt = xn[:, :, CH:2 * CH]
        z = big[:, 0:3072].rearrange("p (t n) -> p t n", t=TILES)
        ug = big[:, 3072:7168].rearrange("p (a t n) -> p a t n", a=2, t=TILES)
        gm = big[:, 7168:9216].rearrange("p (t n) -> p t n", t=TILES)
        qT = big[:, 9216:11264].rearrange("p (b t) -> p b t", b=4)
        pr = big[:, 11264:12800].rearrange("p (a n) -> p a n", a=3)
        prT = big[:, 12800:14336].rearrange("p (a n) -> p a n", a=3)
        tA = big[:, 14336:14976]
        tB = big[:, 14976:15616]
        qn = big[:, 15616:16384]
        gq = wide[:, 0:640]
        onehot = hT[0:33, 4, 0:REL]
        brow = hT[0:DH, 5, 0:REL]

        dfT = big[:, 0:4096].rearrange("p (a b t) -> p a b t", a=4, b=4)
        dfv = big[:, 4096:6144].rearrange("p (a t n) -> p a t n", a=2, t=LAT)
        sig = big[:, 6144:10240].rearrange("p (a b t) -> p a b t", a=2, b=KD)
        yy = big[:, 10240:12288].rearrange("p (a t n) -> p a t n", a=2, t=LAT)
        lg = big[:, 12288:13312].rearrange("p (a n) -> p a n", a=4)
        pb = big[:, 13312:14336].rearrange("p (a n) -> p a n", a=4)
        wd = big[:, 14336:14848].rearrange("p (a n) -> p a n", a=2)
        pbT = big[:, 14848:15616].rearrange("p (a n) -> p a n", a=3)
        tM = big[:, 15616:16128].rearrange("p (a n) -> p a n", a=2)
        h2 = hT[:, 0:4, :].rearrange("p a (b t) -> p (a b) t", b=2)
        yT = hT[:, 4:8, :].rearrange("p a (b t) -> p (a b) t", b=2)
        mT = xn[:, :, :].rearrange("p a (b t) -> p (a b) t", b=4)
        qq = big[:, 0:4096].rearrange("p (a t) -> p a t", a=2 * PH)
        scratch = ring[:, SEARCH_SLOT, :]
        late = ring[:, SEARCH_SLOT + 1, 0:1024]
        early = hT[:, 4:6, :].rearrange("p a n -> p (a n)")
        scores = [[(early, late)[c // 2][:, c % 2 * 512:(c % 2 + 1) * 512] for c in range(4)],
                  [scratch[:, c * 512:(c + 1) * 512] for c in range(4)]]
        w1 = scratch[:, 2048:3072]
        w2 = scratch[:, 3072:3584]
        tv = scratch[:, 3584:3648].rearrange("p (a n) -> p a n", n=16)
        tif = scratch[:, 3648:3712].rearrange("p (a n) -> p a n", n=16)
        ti = scratch[:, 3712:3776].bitcast(U32).rearrange("p (a n) -> p a n", n=16)
        bv = scratch[:, 3776:3808].rearrange("p (a n) -> p a n", n=16)
        bp = scratch[:, 3808:3840].bitcast(U32).rearrange("p (a n) -> p a n", n=16)
        bf = scratch[:, 3840:3904].rearrange("p (c a n) -> p c a n", c=2, n=16)
        bi = scratch[:, 3904:3968].bitcast(U32).rearrange("p (c a n) -> p c a n", c=2, n=16)
        ei = scratch[:, 3968:4096].rearrange("p (c n) -> p c n", c=2)
        expert = [big[:, (j + ROWS // 2) % ROWS * D:((j + ROWS // 2) % ROWS + 1) * D] for j in range(ROWS)]
        diag = hT[:, 0:3, :].rearrange("p a (b n) -> p (a b) n", n=P)
        junk = [xn[:, 0, :], hT[:, 6:8, :].rearrange("p a n -> p (a n)")]
        acc = xn[:, 1, :]
        ttok = gate[:, 0, :, :]
        bias = gate[:, 1, 0, :].rearrange("p (h n) -> p h n", h=DH)
        mask = gate[:, 1, 1, 0:SEQ]
        sk = wsp[:, 0:2, :]
        skT = wsT[:, 0:2, :]
        wff = kT[:, 0, 0:64].rearrange("p (k n) -> p k n", k=KD)
        lamrow = kT[:, 0, 64:320].rearrange("p (a n) -> p a n", a=4)
        lamp = kT[:, 0, 320:448].rearrange("p (a n) -> p a n", a=2)
        subln = ggain[:, 0:P]
        fcv = x[0:FH, 2:4, :].rearrange("p a (b n) -> p (a b) n", n=SEQ)

        bank = [ctx.enter_context(nc.psum_tensor(f"bank{i}", [P, 512], F32)) for i in range(8)]

        FIRST = ["col", "rel", "mod", "msum", "modT", "gate", "xTv", "xTs", "z", "ws", "qkT", "sp", "s",
                 "pT", "o", "mT", "y", "f1", "f2"]
        SECOND = {"BxTv": 4, "BxTs": 4, "proj": 36, "ff": 1, "sk": 1, "Bs": 32, "BpT": 24, "Bo": 4,
                  "yT": 4, "mg": 8, "By": 4, "q2": 16, "sc": 8, "acc": 2}
        filled = {f: sem("filled_" + f) for f in FIRST + list(SECOND)}
        emptied = {f: sem("emptied_" + f) for f in FIRST + list(SECOND)}
        landed = [sem(f"chunk_landed{i}") for i in range(SLOTS)]
        chunk_used = sem("chunk_used")
        hi_ready, lo_ready, quarter_used = sem("hi_ready"), sem("lo_ready"), sem("quarter_used")
        h_hi_ready, h_ready, hidden_ready = sem("h_hi_ready"), sem("h_ready"), sem("hidden_ready")
        scratch_free = sem("scratch_free")
        vectors_in, consts_in, x_in, bmod_in, wide_in = sem("vectors_in"), sem("consts_in"), sem("x_in"), sem("bmod_in"), sem("wide_in")
        bias_out, bias_in, final_in = sem("bias_out"), sem("bias_in"), sem("final_in")
        cond_zero, modA_ready = sem("cond_zero"), sem("modA_ready")
        xn_ready, qn_ready, vn_ready = sem("xn_ready"), sem("qn_ready"), sem("vn_ready")
        nm_ready, pv_done, mix_ready = sem("nm_ready"), sem("pv_done"), sem("mix_ready")
        layer_done = sem("layer_done")
        result_ready, out_done = sem("result_ready"), sem("out_done")
        row_in = [sem(f"row_in{i}") for i in range(ROWS)]
        VROWS = [j for j in range(ROWS) if j % 4 == 3]
        PROWS = [j for j in range(ROWS) if j % 4 != 3]
        NV, NP, RUN = len(VROWS), len(PROWS), PICKS // ROWS
        PER = {"Bxn": 4, "ff_z": 1, "ff_e": 1, "c_ready": 1, "p_ready": 32, "w_ready": 8,
               "Bpv": 24, "y_ready": 4, "mT_ready": 8, "lam_z": 1, "lam_e": 1, "gate_z": 2,
               "gate_e": 2, "first_picks": 1, "picked": 2, "dotted": 2, "acted": 2, "weighed": 2, "acc_ready": 2,
               "small_in": 6 * 16, "gain_in": 16, "picks_now": 2 * RUN * 2 * LAT,
               "free_v": LAT * (PICKS + NV * RUN), "free_p": LAT * NP * RUN,
               "diag_ready": LAT * NP * RUN}
        S = {f: sem(f) for f in PER}
        PER |= SECOND | {"layer_done": 1, "row_in": 16 * RUN * 2 * LAT}
        PER |= {f"landed{s}": 16 * len(range(s, CHUNKS_B, SLOTS)) for s in range(SLOTS)}

        block = ctx.enter_context(nc.Block())

        class Side:

            def __init__(self):
                self.layer, self.n, self.held = None, {}, [None] * 8

            def at(self, n, name):
                return n if self.layer is None else self.layer * PER[name] + n

            def next(self, fam):
                self.n[fam] = self.n.get(fam, 0) + 1
                return self.at(self.n[fam], fam)

            def freed(self, b):
                if self.held[b] is None:
                    return (consts_in, 16 * CONSTS) if self.layer is None else (layer_done, self.layer + 1)
                old, n = self.held[b]
                return emptied[old], self.at(n, old)

            def claim(self, fam, b):
                self.n[fam] = self.n.get(fam, 0) + 1
                self.held[b] = (fam, self.n[fam])
                return bank[b]

            def new_layer(self, layer):
                self.layer, self.n, self.held = layer, {}, [None] * 8

        GROUPS, n = [], 0
        for kind, heads, maps in ((0, DH, 2), (1, FH, 1)):
            for qt in range(LAT):
                for h in range(heads):
                    GROUPS.append((kind, qt, h, n))
                    n += maps
        GROUP_OF = [g for g, (kind, *_) in enumerate(GROUPS) for _ in range(2 - kind)]
        LAST_GROUP = [3, 7, 15, 23]

        BETWEEN = [("ff", 0, 0)] + [("cols", c, i) for c in (3, 4) for i in range(4)]
        BETWEEN += [("rows", 5, t) for t in range(LAT)] + [("cols", c, i) for c in range(6, 10) for i in range(4)]
        assert len(BETWEEN) == len(GROUPS) + 3

        COLUMN = {0: 0, 1: 1, 3: 2, 4: 3}
        SHIFTS = [[(kind, half) for kind in COLUMN for half in range(2) if (2 * kind + half) % 4 == g] for g in range(4)]

        def heads_after(c, t, n):
            done = (c - 2) * n + t
            if n == TILES:
                return [done // 2] if done % 2 else []
            return {1: [0], 2: [1], 3: [2, 3]}.get(done, [])

        def ff_chunk(layer, g, step):
            if layer:
                return CHUNKS_A - len(STEPS) + step
            return 18 + (step + min(step, 12) if g == 0 else len(STEPS) + 12 + step)

        def quarter(ap, kind, i):
            if kind == 0:
                return ap.rearrange("p (k n) -> p k n", k=KD)[:, :, i * P:(i + 1) * P]
            return ap[:, i * D:(i + 1) * D]

        def shaped(ap, kind):
            return ap.rearrange("p (k n) -> p k n", k=KD) if kind == 0 else ap

        @block.sync
        def _(sp):
            count = 0

            def put(src, slot):
                k, w = src.shape[1], src.shape[2]
                dst = ring[:, slot, 0:k * w].rearrange("p (k n) -> p k n", k=k)
                sp.dma_start(dst, src).then_inc(landed[slot], 16)

            def chunk(src):
                nonlocal count
                if count >= SLOTS:
                    sp.wait_ge(chunk_used, count - SLOTS + 1)
                put(src, count % SLOTS)
                count += 1

            def mod_chunk(layer, c):
                chunk(A["w_mod"][layer].rearrange("(k p) n -> p k n", p=P)[:, :, c * CH:(c + 1) * CH])

            for c in range(12):
                if c == 1:
                    sp.wait_ge(vectors_in, 16 * VECTORS)
                mod_chunk(0, c)
            for layer in range(LAYERS):
                w = A["w_in"][layer].rearrange("(k p) n -> p k n", p=P)
                for a, b in ((0, 512), (512, 768), (768, 1280), (1280, 1792)):
                    chunk(w[:, :, a:b])
                w = A["w_out"][layer].rearrange("(k p) n -> p k n", p=P)
                for c in range(2):
                    chunk(w[:, :, c * CH:(c + 1) * CH])
                w_ff1 = A["w_ff1"][layer].rearrange("(k p) n -> p k n", p=P)
                w_ff2 = A["w_ff2"][layer].rearrange("(c k p) n -> c p k n", p=P, k=4)
                for g in range(2 if layer == 0 else 1):
                    for step, (kind, c) in enumerate(STEPS):
                        assert count == ff_chunk(layer, g, step)
                        chunk(w_ff2[c] if kind else w_ff1[:, :, c * CH:(c + 1) * CH])
                        if layer == g == 0 and step < 12:
                            mod_chunk(1, step)
            assert count == CHUNKS_A

            with sp.Fori(0, LAYERS) as l:
                c = 0

                def chunk_of_layer(src):
                    nonlocal c
                    sp.wait_ge(chunk_used, l * CHUNKS_B + CHUNKS_A + max(0, c - SLOTS + 1))
                    sp.nop(nofuse=True)
                    if c == SEARCH_SLOT:
                        sp.wait_ge(scratch_free, l + 1)
                        sp.nop(nofuse=True)
                    put(src, c % SLOTS)
                    c += 1

                def of_layer(name):
                    w = A[name].rearrange("l (k p) n -> l p k n", p=P)
                    return w[bass.ds(l, 1)].rearrange("l p k n -> (l p) k n")

                w = of_layer("w_in_2")
                for a in (0, 512, 1024, 1536, 2048, 2560, 3080, 3592, 4104, 4616):
                    chunk_of_layer(w[:, :, a:a + CH])
                chunk_of_layer(of_layer("w_diff_o_2"))
                chunk_of_layer(of_layer("w_fox_o_2"))
                for name, m in (("w_out_2", 2), ("w_query_2", 4)):
                    w = of_layer(name)
                    for i in range(m):
                        chunk_of_layer(w[:, :, i * CH:(i + 1) * CH])
                assert c == CHUNKS_B
            sp.wait_ge(result_ready, 1)
            sp.dma_start(out.rearrange("o (t p) n -> (o p) t n", p=P), xn[:, :, :]).then_inc(out_done, 16)
            sp.wait_ge(out_done, 16)

        @block.gpsimd
        def _(pool):
            me = Side()

            def load(dst, src, s):
                pool.dma_start(dst, src).then_inc(s, 16)

            load(onehot, A["onehot"], consts_in)
            load(rel[0:32, :], A["rel_bias_2"], consts_in)
            load(rel[32:33, :], A["ones4"], consts_in)
            for q in range(4):
                load(pickv[32 * q:32 * q + 2, :, :], A["pickv"].rearrange("a (b p) -> a b p", b=2), consts_in)
            load(rope[:, :, :, :], A["rope"].rearrange("(t p) (a n) -> p t a n", p=P, a=2), consts_in)
            load(iota[:, :], A["iota16"].broadcast_to([P, 16]), consts_in)
            for layer in range(LAYERS):
                if layer:
                    pool.wait_ge(emptied["sp"], me.at(TILES, "sp"))
                for c in range(12):
                    q = 32 * (c % 4)
                    load(bmod[c // 4][q:q + 2, :], A["b_mod"][layer:layer + 1, c * CH:(c + 1) * CH].broadcast_to([2, CH]),
                         bmod_in)
                pool.wait_ge(emptied["msum"], me.at(12 * (layer + 1), "msum"))
                for a in range(AH + AKV):
                    g = A["q_norm_g" if a < AH else "k_norm_g"][layer:layer + 1]
                    load(gq[:, a * HD:(a + 1) * HD], g.broadcast_to([P, HD]), wide_in)
                load(ggain[:, :], A["gmlp_norm_g"][layer:layer + 1].broadcast_to([P, GW]), wide_in)
                load(wsp[:, :, :], A["w_spatial"][layer].rearrange("g p q -> p g q"), wide_in)
                if layer == 0:
                    pool.wait_ge(emptied["rel"], 1)
                    load(bias_rows, spread(brow, 1, P), bias_out)
            pool.wait_ge(bias_out, 16)
            pool.wait_ge(layer_done, 1)
            load(bias, bass.AP(tensor=bias_rows.tensor, offset=P - 1, ap=[[REL - 1, P], [P * REL, DH], [1, SEQ]]), bias_in)
            load(mask, A["mask"], bias_in)
            pool.sem_inc(S["free_v"], ROWS)
            pool.sem_inc(S["free_p"], NP)

            with pool.Fori(0, LAYERS) as l:
                me.new_layer(l)
                pool.wait_ge(layer_done, me.at(1, "layer_done"))

                def of_layer(name):
                    return A[name][bass.ds(l, 1)]

                load(wff, A["w_in_2"].rearrange("l (k p) n -> l p k n", p=P)[bass.ds(l, 1), :, :, FFCOL:FFCOL + FH]
                     .rearrange("l p k n -> (l p) k n"), S["small_in"])
                load(bfc[:, :], of_layer("b_forget_2").rearrange("l (h o) -> (l h) o", o=1), S["small_in"])
                load(lamrow, of_layer("diff_lambda_2").rearrange("l a n -> l (a n)").broadcast_to([P, 4 * HD])
                     .rearrange("p (a n) -> p a n", a=4), S["small_in"])
                load(lam2[:, 0:2], of_layer("lam").broadcast_to([P, 2]), S["small_in"])
                load(subln, of_layer("diff_subln_g_2").broadcast_to([P, P]), S["small_in"])
                load(sk, A["sub_keys_2"].rearrange("l a n d -> l n a d")[bass.ds(l, 1)]
                     .rearrange("l n a d -> (l n) a d"), S["small_in"])
                load(wide[:, :], of_layer("norm2_g_2").broadcast_to([P, D]), S["gain_in"])

                def gather(table, t, v, i, half):
                    pool.tensor_copy(pick_now[:, half, :],
                                     picks[:, t, bass.ds(i * ROWS + half * HALF, HALF)]).then_inc(S["picks_now"], 1)
                    pool.wait_ge(S["picks_now"], me.at(i * 2 + (2 * t + v) * 2 * RUN + half + 1, "picks_now"))
                    pool.nop(nofuse=True)
                    for j in range(HALF):
                        s = half * HALF + j
                        pool.indirect_dma_start(
                            out=expert[s], out_offset=None, in_=table,
                            in_offset=bass.IndirectOffsetOnAxis(ap=pick_now[:, half, j:j + 1], axis=0),
                        ).then_inc(row_in[s], 16)

                for t in range(LAT):
                    for v, name in enumerate(("expert_u_2", "expert_v_2")):
                        table = A[name].rearrange("l e n -> (l e) n")
                        base_v = t * (PICKS + NV * RUN) + v * PICKS
                        base_p = t * NP * RUN
                        if t == v == 0:
                            pool.wait_ge(S["first_picks"], me.at(1, "first_picks"))
                            pool.nop(nofuse=True)
                            gather(table, t, v, 0, 0)
                            pool.wait_ge(emptied["sc"], me.at(8, "sc"))
                            pool.nop(nofuse=True)
                            gather(table, t, v, 0, 1)
                        elif v:
                            pool.wait_ge(S["free_v"], me.at(ROWS + base_v - HALF, "free_v"))
                        else:
                            pool.wait_ge(S["free_v"], me.at(ROWS + base_v - NV // 2, "free_v"))
                            pool.wait_ge(S["free_p"], me.at(NP + base_p - NP // 2, "free_p"))
                        if v == 0:
                            pool.wait_ge(S["picked"], me.at(t + 1, "picked"))
                        pool.nop(nofuse=True)
                        with pool.Fori(1 if t == v == 0 else 0, RUN) as i:
                            for half in range(2):
                                rate = NV if v else ROWS
                                pool.wait_ge(S["free_v"], me.at(i * rate + ROWS + base_v - rate + rate // 2 * (half + 1), "free_v"))
                                if v:
                                    pool.wait_ge(S["free_p"], me.at(i * NP + base_p + NP // 2 * (half + 1), "free_p"))
                                elif half:
                                    pool.wait_ge(S["free_p"], me.at(NP + base_p, "free_p"))
                                gather(table, t, v, i, half)
            pool.wait_ge(layer_done, 1 + LAYERS)
            load(wide[:, :], A["final_norm_g_2"].rearrange("(o n) -> o n", o=1).broadcast_to([P, D]), final_in)

        @block.tensor
        def _(pe):
            me = Side()
            chunks = 0

            def next_chunk():
                nonlocal chunks
                slot, n = chunks % SLOTS, chunks // SLOTS + 1
                if me.layer is None:
                    pe.wait_ge(landed[slot], 16 * n)
                else:
                    before = len(range(slot, CHUNKS_A, SLOTS))
                    pe.wait_ge(landed[slot], me.at(16 * (n + before), f"landed{slot}"))
                chunks += 1
                return slot

            def fill(fam, ins):
                ins.then_inc(filled[fam], 1)

            read = 0

            def used(m=1):
                nonlocal read
                read += m

            def tell(ins):
                nonlocal read
                if read:
                    ins.then_inc(chunk_used, read)
                    read = 0

            def norm_T(fams, source, ready, tiles, name=None, first=0):
                for t in range(tiles):
                    pe.wait_ge(ready, me.at(first + t + 1, name))
                    for half, fam in enumerate(fams):
                        pe.wait_ge(*me.freed((2 * t + half) % 8))
                        o = me.claim(fam, (2 * t + half) % 8)
                        for b in range(4):
                            k = 4 * half + b
                            last = nc.tensor.transpose(o[:, b * P:(b + 1) * P], source(t)[:, k * P:(k + 1) * P], eye[:, :])
                            if b == 0:
                                tell(last)
                        fill(fam, last)

            def product(o, lhs, rhs):
                n = len(lhs)
                last = None
                for k in range(n):
                    last = nc.tensor.matmul(o, lhs[k], rhs[k], start=k == 0, stop=k == n - 1)
                    if k == 0 and n == KD:
                        tell(last)
                return last

            pe.wait_ge(vectors_in, 16 * VECTORS)
            pe.wait_ge(*me.freed(0))
            fill("col", nc.tensor.transpose(me.claim("col", 0)[:, 0:72], rows[:, :], eye[0:72, 0:72]))
            pe.wait_ge(emptied["col"], me.at(1, "col"))

            def modulation(b):
                slot = next_chunk()
                pe.wait_ge(*me.freed(b))
                o = me.claim("mod", b)
                for i in range(2):
                    for g in range(4):
                        k = 2 * g + i
                        last = nc.tensor.matmul(o[32 * g:32 * g + 32, :], cond[:, k, :], ring[:, slot, k * CH:(k + 1) * CH],
                                                start=i == 0, stop=i == 1)
                        if i == g == 0:
                            tell(last)
                fill("mod", last)
                used()

            def modulation_sum(n, b):
                q = 32 * (n % 4)
                pe.wait_ge(emptied["mod"], n + 1)
                pe.wait_ge(*me.freed(b))
                o = me.claim("msum", b)
                fill("msum", nc.tensor.matmul(o[q:q + 32, :], fold[:, :], modt[:, n % 2, :], start=True, stop=True))

            for c in range(12):
                modulation(c % 4)
                if c:
                    modulation_sum(c - 1, 4 + (c - 1) % 4)
            modulation_sum(11, 7)
            pe.wait_ge(consts_in, 16 * CONSTS)
            pe.wait_ge(*me.freed(5))
            fill("rel", nc.tensor.matmul(me.claim("rel", 5)[0:DH, 0:REL], rel[:, :], onehot, start=True, stop=True))
            units, tiles_before, groups_before, blocks_before = 0, 0, 0, 0
            for layer in range(LAYERS):
                NT = TILES if layer == 0 else LAT
                pe.wait_ge(emptied["msum"], me.at(12 * (layer + 1), "msum"))
                for g in range(4):
                    q = 32 * g
                    pe.wait_ge(*me.freed(1 + g))
                    o = me.claim("modT", 1 + g)
                    for n, (kind, half) in enumerate(SHIFTS[g]):
                        c = 2 * kind + half
                        for i in range(4):
                            last = nc.tensor.matmul(o[:, 8 * n + 2 * i:8 * n + 2 * i + 2],
                                                    modrow[c // 4][q:q + 2, i * P:(i + 1) * P], eye[q:q + 2, q:q + 2],
                                                    start=True, stop=True)
                            if g == n == i == 0:
                                tell(last)
                    fill("modT", last)
                b = 6
                for g, kind in enumerate((2, 5)):
                    for v in range(2 if layer == 0 else 1):
                        for half in range(2):
                            c = kind * 2 + half
                            q = 32 * (c % 4)
                            pe.wait_ge(*me.freed(b % 8))
                            o = me.claim("gate", b % 8)
                            fill("gate", nc.tensor.matmul(o[:, :], pickv[q:q + 2, v, :], modrow[c // 4][q:q + 2, :],
                                                          start=True, stop=True))
                            b += 1
                norm_T(("xTv", "xTs"), lambda t: xn[:, t % 2, :], xn_ready, TILES, first=tiles_before)
                tiles_before += TILES
                pe.wait_ge(emptied["xTv"], me.at(me.n["xTv"], "xTv"))
                pe.wait_ge(emptied["xTs"], me.at(me.n["xTs"], "xTs"))
                b = 0

                def queries_keys(t):
                    nonlocal b
                    pe.wait_ge(qn_ready, layer * TILES + t + 1)
                    for a, m in ((0, 4), (4, 2)):
                        if a == 0 and t >= NT:
                            continue
                        pe.wait_ge(*me.freed(b % 8))
                        o = me.claim("qkT", b % 8)
                        for i in range(m):
                            last = nc.tensor.transpose(o[:, i * P:(i + 1) * P], qn[:, (a + i) * P:(a + i + 1) * P], eye[:, :])
                        fill("qkT", last)
                        b += 1

                for c in range(4):
                    slot, w = next_chunk(), (512, 256, 512, 512)[c]
                    for t in range(TILES if c == 1 else NT):
                        pe.wait_ge(*me.freed(b % 8))
                        o = me.claim("z", b % 8)
                        last = product(o[:, 0:w], [hT[:, k, t * P:(t + 1) * P] for k in range(KD)],
                                       [ring[:, slot, k * w:(k + 1) * w] for k in range(KD)])
                        fill("z", last)
                        b += 1
                        if c >= 2:
                            for u in heads_after(c, t, NT):
                                queries_keys(u)
                    used()
                pe.wait_ge(wide_in, 12 * 16 * (layer + 1))
                pe.wait_ge(*me.freed(b % 8))
                o = me.claim("ws", b % 8)
                for g in range(4):
                    last = nc.tensor.transpose(o[:, g * P:(g + 1) * P], wsp[:, g, :], eye[:, :])
                    if g == 0:
                        tell(last)
                fill("ws", last)
                pe.wait_ge(emptied["qkT"], me.at(me.n["qkT"], "qkT"))
                N = NT * AH
                for n in range(N + 3):
                    if n < N:
                        t, h = divmod(n, AH)
                        a = HD * (h % 2)
                        lo, hi = (0, 512) if t < LAT else (256, 512)
                        pe.wait_ge(*me.freed(n % 3))
                        o = me.claim("s", n % 3)
                        fill("s", nc.tensor.matmul(o[:, 0:hi - lo], qT[a:a + HD, h // 2, t * P:(t + 1) * P],
                                                   kT[a:a + HD, h // 4, lo:hi], start=True, stop=True))
                    if 2 <= n <= N + 1:
                        m = n - 2
                        pe.wait_ge(emptied["s"], me.at(units + m + 1, "s"))
                        pe.wait_ge(*me.freed(3 + m % 3))
                        o = me.claim("pT", 3 + m % 3)
                        for i in range(4 if m // AH < LAT else 2):
                            last = nc.tensor.transpose(o[:, i * P:(i + 1) * P], pr[:, m % 3, i * P:(i + 1) * P], eye[:, :])
                        fill("pT", last)
                    if n >= 3:
                        m = n - 3
                        t, h = divmod(m, AH)
                        pe.wait_ge(emptied["pT"], me.at(units + m + 1, "pT"))
                        if h == 0:
                            pe.wait_ge(*me.freed(6 + t % 2))
                            o_bank = me.claim("o", 6 + t % 2)
                        blocks = range(4) if t < LAT else range(2, 4)
                        v0 = QW + KVW + HD * (h // 4)
                        last = product(o_bank[:, h * HD:(h + 1) * HD],
                                       [prT[:, m % 3, (i - blocks[0]) * P:(i - blocks[0] + 1) * P] for i in blocks],
                                       [z[:, i, v0:v0 + HD] for i in blocks])
                        last.then_inc(pv_done, 1)
                units += N
                pe.wait_ge(emptied["ws"], me.at(me.n["ws"], "ws"))
                for t in range(NT):
                    pe.wait_ge(vn_ready, (TILES if layer else 0) + t + 1)
                    pe.wait_ge(*me.freed(t))
                    o = me.claim("sp", t)
                    for g in range(4):
                        last = nc.tensor.matmul(o[:, g * P:(g + 1) * P], wsT[:, g, :], ug[:, 1, t, g * P:(g + 1) * P],
                                                start=True, stop=True)
                    fill("sp", last)
                for t in range(NT):
                    pe.wait_ge(mix_ready, (TILES if layer else 0) + t + 1)
                    for half, src in enumerate((z[:, t, 0:512], gm[:, t, :])):
                        if half:
                            pe.wait_ge(emptied["sp"], (TILES if layer else 0) + t + 1)
                        pe.wait_ge(*me.freed((2 * t + half) % 8))
                        o = me.claim("mT", (2 * t + half) % 8)
                        for i in range(4):
                            last = nc.tensor.transpose(o[:, i * P:(i + 1) * P], src[:, i * P:(i + 1) * P], eye[:, :])
                        fill("mT", last)
                pe.wait_ge(emptied["mT"], me.at(me.n["mT"], "mT"))
                for half in range(2):
                    slot = next_chunk()
                    for t in range(NT):
                        pe.wait_ge(*me.freed((half * NT + t) % 8))
                        o = me.claim("y", (half * NT + t) % 8)
                        last = product(o[:, :], [hT[:, k, t * P:(t + 1) * P] for k in range(KD)],
                                       [ring[:, slot, k * CH:(k + 1) * CH] for k in range(KD)])
                        fill("y", last)
                    used()
                norm_T(("xTv", "xTs"), lambda t: xn[:, t % 2, :], xn_ready, NT, first=tiles_before)
                tiles_before += NT
                pe.wait_ge(emptied["xTv"], me.at(me.n["xTv"], "xTv"))
                pe.wait_ge(emptied["xTs"], me.at(me.n["xTs"], "xTs"))
                for g in range(NT // LAT):
                    pe.wait_ge(h_ready, groups_before + 1)
                    for step, (kind, c) in enumerate(STEPS):
                        chunks += 1
                        for i in range(4):
                            m = QUARTERS * g + 4 * step + i
                            pe.wait_ge(lo_ready, QUARTERS * (groups_before - g) + m + 1)
                            if kind == 0:
                                b = 4 + blocks_before % 3
                                pe.wait_ge(*me.freed(b))
                                o = me.claim("f1", b)
                                blocks_before += 1
                                pairs = []
                                for k in range(KD):
                                    hi, lo = (w[:, m % 4, k * P:(k + 1) * P] for w in (w_hi, w_lo))
                                    pairs += [(hi, h_hi[:, k, :]), (hi, h_lo[:, k, :]), (lo, h_hi[:, k, :])]
                                for n, (w, h) in enumerate(pairs):
                                    last = nc.tensor.matmul(o[:, 0:SEQ], w, h, start=n == 0, stop=n == len(pairs) - 1)
                                    if n == 0:
                                        tell(last)
                                    if n == 1 and m:
                                        last.then_inc(quarter_used, 1)
                                fill("f1", last)
                            else:
                                pe.wait_ge(hidden_ready, 32 * groups_before + 4 * c + i + 1)
                                for t in range(LAT):
                                    for half in range(2):
                                        if c == i == 0:
                                            pe.wait_ge(*me.freed(2 * t + half))
                                            me.claim("f2", 2 * t + half)
                                        o = bank[2 * t + half]
                                        h = [u[:, c % 2, i, t * P:(t + 1) * P] for u in (u_hi, u_lo)]
                                        w = [w[:, m % 4, half * CH:(half + 1) * CH] for w in (w_hi, w_lo)]
                                        for n, (a, b) in enumerate(((0, 0), (0, 1), (1, 0))):
                                            last = nc.tensor.matmul(o[:, :], h[a], w[b], start=c == i == n == 0,
                                                                    stop=c == 7 and i == 3 and n == 2)
                                            if t == half == n == 0:
                                                tell(last)
                                            if t == half == 0 and n == 1:
                                                last.then_inc(quarter_used, 1)
                                        if c == 7 and i == 3:
                                            fill("f2", last)
                            if layer == g == 0 and i == 1 and 1 <= step <= 12:
                                modulation_sum(11 + step, 7)
                        used()
                        if layer == g == 0 and step < 12:
                            modulation(7)
                    groups_before += 1

            tell(pe.drain())

            with pe.Fori(0, LAYERS) as l:
                me.new_layer(l)
                chunks = 0
                pe.wait_ge(layer_done, me.at(1, "layer_done"))
                norm_T(("BxTv", "BxTs"), lambda t: xn[:, t, :], S["Bxn"], LAT, name="Bxn")
                pe.wait_ge(emptied["BxTv"], me.at(2, "BxTv"))
                pe.wait_ge(emptied["BxTs"], me.at(2, "BxTs"))
                b = 4

                def columns(fam, b, slot, block):
                    pe.wait_ge(*me.freed(b % 8))
                    o = me.claim(fam, b % 8)
                    fill(fam, product(o[:, 0:SEQ],
                                      [ring[:, slot, k * CH + block * P:k * CH + (block + 1) * P] for k in range(KD)],
                                      [h2[:, k, :] for k in range(KD)]))

                def tokens(b, slot, t):
                    pe.wait_ge(*me.freed(b % 8))
                    o = me.claim("proj", b % 8)
                    fill("proj", product(o[:, :], [h2[:, k, t * P:(t + 1) * P] for k in range(KD)],
                                         [ring[:, slot, k * CH:(k + 1) * CH] for k in range(KD)]))

                for c in range(3):
                    slot = next_chunk()
                    for i in range(LAT if c == 2 else 4):
                        if c == 2:
                            tokens(b, slot, i)
                        else:
                            columns("proj", b, slot, i)
                        b += 1
                    used()
                pe.wait_ge(S["small_in"], me.at(PER["small_in"], "small_in"))
                pe.wait_ge(*me.freed(b % 8))
                o = me.claim("sk", b % 8)
                for i in range(2):
                    last = nc.tensor.transpose(o[:, i * P:(i + 1) * P], sk[:, i, :], eye[:, :])
                    if i == 0:
                        tell(last)
                fill("sk", last)
                pe.wait_ge(emptied["proj"], me.at(10, "proj"))
                for g, (what, c, i) in enumerate(BETWEEN):
                    if what == "ff":
                        pe.wait_ge(*me.freed(2))
                        o = me.claim("ff", 2)
                        fill("ff", product(o[0:FH, 0:SEQ], [wff[:, k, :] for k in range(KD)],
                                           [h2[:, k, :] for k in range(KD)]))
                    else:
                        if i == 0:
                            slot = next_chunk()
                        if what == "cols":
                            columns("proj", 2 + g % 2, slot, i)
                        else:
                            tokens(2 + g % 2, slot, i)
                        if i == (3 if what == "cols" else 1):
                            used()
                    if g < len(GROUPS):
                        kind, qt, h, s = GROUPS[g]
                        nk = (qt + 1) * P
                        if s == 16:
                            pe.wait_ge(emptied["proj"], me.at(18, "proj"))
                            pe.wait_ge(S["c_ready"], me.at(1, "c_ready"))
                        for m in range(2 - kind):
                            if kind == 0:
                                a, blk = HD * m, h
                            else:
                                a, blk = HD * (h % 2), h // 2
                            pe.wait_ge(*me.freed((s + m) % 2))
                            o = me.claim("Bs", (s + m) % 2)
                            last = nc.tensor.matmul(o[:, 0:nk], dfT[a:a + HD, 2 * kind, blk, qt * P:(qt + 1) * P],
                                                    dfT[a:a + HD, 2 * kind + 1, blk, 0:nk], start=True, stop=kind == 0)
                            if kind:
                                one = eye[0:FH, h:h + 1]
                                nc.tensor.matmul(o[:, 0:nk], fcv[:, 3, qt * P:(qt + 1) * P], one.broadcast_to([FH, nk]),
                                                 start=False, stop=False)
                                last = nc.tensor.matmul(o[:, 0:nk], one.broadcast_to([FH, P]), fcv[:, 4, 0:nk],
                                                        start=False, stop=True)
                            fill("Bs", last)
                    if 2 <= g < len(GROUPS) + 2:
                        kind, qt, h, s = GROUPS[g - 2]
                        if kind == 0:
                            pe.wait_ge(S["w_ready"], me.at(g - 1, "w_ready"))
                        else:
                            pe.wait_ge(S["p_ready"], me.at(s + 1, "p_ready"))
                        pe.wait_ge(*me.freed(4 + g % 2))
                        o = me.claim("BpT", 4 + g % 2)
                        src = pb[:, s % 4, :] if kind else wd[:, (g - 2) % 2, :]
                        for i in range(qt + 1):
                            last = nc.tensor.transpose(o[:, i * P:(i + 1) * P], src[:, i * P:(i + 1) * P], eye[:, :])
                        fill("BpT", last)
                    if g >= 3:
                        kind, qt, h, s = GROUPS[g - 3]
                        if kind and g - 3 == 2 * DH:
                            pe.wait_ge(emptied["proj"], me.at(20, "proj"))
                        pe.wait_ge(emptied["BpT"], me.at(g - 2, "BpT"))
                        vw = 2 * HD if kind == 0 else HD
                        if h == 0:
                            pe.wait_ge(*me.freed(6 + qt))
                            o_bank = me.claim("Bo", 6 + qt)
                        last = product(o_bank[:, h * vw:(h + 1) * vw],
                                       [pbT[:, (g - 3) % 3, i * P:(i + 1) * P] for i in range(qt + 1)],
                                       [dfv[:, kind, i, h * vw:(h + 1) * vw] for i in range(qt + 1)])
                        last.then_inc(S["Bpv"], 1)
                for n in range(4):
                    kind, qt = divmod(n, 2)
                    pe.wait_ge(S["y_ready"], me.at(n + 1, "y_ready"))
                    pe.wait_ge(*me.freed(n))
                    o = me.claim("yT", n)
                    for i in range(4):
                        last = nc.tensor.transpose(o[:, i * P:(i + 1) * P], yy[:, kind, qt, i * P:(i + 1) * P], eye[:, :])
                    fill("yT", last)
                pe.wait_ge(emptied["yT"], me.at(4, "yT"))
                slots = [next_chunk(), next_chunk()]
                for j in range(KD):
                    pe.wait_ge(*me.freed(j % 8))
                    o = me.claim("mg", j % 8)
                    for a in range(2):
                        last = product(o[:, a * SEQ:(a + 1) * SEQ],
                                       [ring[:, slots[a], k * D + j * P:k * D + (j + 1) * P] for k in range(4)],
                                       [yT[:, 4 * a + k, :] for k in range(4)])
                    fill("mg", last)
                used(2)
                pe.wait_ge(S["mT_ready"], me.at(KD, "mT_ready"))
                for half in range(2):
                    slot = next_chunk()
                    for t in range(LAT):
                        pe.wait_ge(*me.freed(half * LAT + t))
                        o = me.claim("By", half * LAT + t)
                        last = product(o[:, :], [mT[:, k, t * P:(t + 1) * P] for k in range(KD)],
                                       [ring[:, slot, k * CH:(k + 1) * CH] for k in range(KD)])
                        fill("By", last)
                    used()
                norm_T(("BxTv", "BxTs"), lambda t: ttok[:, t, :], S["Bxn"], LAT, name="Bxn", first=LAT)
                pe.wait_ge(emptied["BxTv"], me.at(4, "BxTv"))
                pe.wait_ge(emptied["BxTs"], me.at(4, "BxTs"))
                def scores_of(c):
                    pe.wait_ge(emptied["q2"], me.at(4 * c + 4, "q2"))
                    for t in range(LAT):
                        pe.wait_ge(*me.freed(4 * (c % 2) + t))
                        o = me.claim("sc", 4 * (c % 2) + t)
                        for i in range(4):
                            last = nc.tensor.matmul(o[:, i * P:(i + 1) * P], qq[:, 4 * c + i, t * P:(t + 1) * P],
                                                    skT[:, i % 2, :], start=True, stop=True)
                            if i == 0:
                                tell(last)
                        fill("sc", last)

                for c in range(4):
                    slot = next_chunk()
                    for i in range(4):
                        columns("q2", 4 * (c % 2) + i, slot, i)
                        if c and i == 0:
                            scores_of(c - 1)
                    used()
                scores_of(3)
                for t in range(LAT):
                    outs = [bank[2 * t], bank[2 * t + 1]]
                    if t == 0:
                        pe.wait_ge(emptied["sc"], me.at(8, "sc"))
                    for half in range(2):
                        nc.tensor.matmul(outs[half][:, :], eye[:, :], x[:, t, half * CH:(half + 1) * CH],
                                         start=True, stop=False, skip_group_check=True)
                    with pe.Fori(0, RUN) as i:
                        for n, j in enumerate(PROWS):
                            pe.wait_ge(row_in[j], me.at(i * 16 + (2 * t + 1) * RUN * 16 + 16, "row_in"))
                            pe.wait_ge(S["diag_ready"], me.at(i * NP + t * NP * RUN + n + 1, "diag_ready"))
                            for half in range(2):
                                last = nc.tensor.matmul(outs[half][:, :], diag[:, n, :],
                                                        expert[j][:, half * CH:(half + 1) * CH],
                                                        start=False, stop=False, skip_group_check=True)
                            last.then_inc(S["free_p"], 1)
                    pe.wait_ge(S["acc_ready"], me.at(t + 1, "acc_ready"))
                    for half in range(2):
                        last = nc.tensor.matmul(outs[half][:, :], eye[:, :], acc[:, half * CH:(half + 1) * CH],
                                                start=False, stop=True, skip_group_check=True)
                    fill("acc", last)

        @block.scalar
        def _(act):
            me = Side()

            def free(fam, ins):
                ins.then_inc(emptied[fam], 1)

            def load(dst, src, s):
                act.dma_start(dst, src).then_inc(s, 16)

            load(eye[:, :], A["eye"], vectors_in)
            load(fold[:, :], A["fold"], vectors_in)
            load(rows[0:8, :], A["c"].rearrange("a (k p) -> (a k) p", p=P), vectors_in)
            load(rows[8:16, :], A["c_ctx"].rearrange("(k p) -> k p", p=P), vectors_in)
            for i, name in enumerate(("norm1_g", "norm2_g", "norm1_g_2")):
                load(rows[16 + 16 * i:32 + 16 * i, :], A[name].rearrange("l (k p) -> (l k) p", p=P), vectors_in)
            load(rows[64:72, :], A["b_spatial"].rearrange("l g p -> (l g) p"), vectors_in)
            load(x[:, 0:2, :], A["x"].rearrange("o (t p) n -> (o p) t n", p=P), x_in)
            load(x[:, 2:4, :], A["ctx"].rearrange("o (t p) n -> (o p) t n", p=P), x_in)
            act.wait_ge(filled["col"], me.next("col"))
            nc.scalar.activation(cols[:, :], bank[0][:, 0:72], ACT.Copy)
            act.wait_ge(cond_zero, 1)
            free("col", nc.scalar.activation(cond[:, :, 0:2], bank[0][:, 0:16].rearrange("p (v k) -> p k v", v=2), ACT.Silu))

            def partials(n, b):
                act.wait_ge(filled["mod"], n + 1)
                if n >= 2:
                    act.wait_ge(filled["msum"], n - 1)
                free("mod", nc.scalar.activation(modt[:, n % 2, :], bank[b][:, :], ACT.Copy))

            for c in range(12):
                partials(c, c % 4)
            act.wait_ge(filled["rel"], me.next("rel"))
            free("rel", nc.scalar.activation(brow, bank[5][0:DH, 0:REL], ACT.Copy))
            units = 0
            for layer in range(LAYERS):
                NT = TILES if layer == 0 else LAT
                b = 6
                for g in range(2):
                    for v in range(2 if layer == 0 else 1):
                        for half in range(2):
                            act.wait_ge(filled["gate"], me.next("gate"))
                            free("gate", nc.scalar.activation(gate[:, g, v, half * CH:(half + 1) * CH],
                                                              bank[b % 8][:, :], ACT.Copy))
                            b += 1

                def norm_evac(which, tiles):
                    act.wait_ge(modA_ready, layer + 1)
                    for t in range(tiles):
                        act.wait_ge(filled["xTs"], me.next("xTs"))
                        for i in range(4):
                            k = 4 + i
                            last = nc.scalar.activation(hT[:, k, t * P:(t + 1) * P],
                                                        bank[(2 * t + 1) % 8][:, i * P:(i + 1) * P], ACT.Identity,
                                                        bias=modcol[:, 2 * which, k, t // 2:t // 2 + 1],
                                                        scale=modA[:, which, k, t // 2:t // 2 + 1])
                        free("xTs", last)

                if layer == 0:
                    act.wait_ge(bias_out, 16)
                norm_evac(0, TILES)
                b = 0

                def queries_keys(t):
                    nonlocal b
                    if t < NT:
                        act.wait_ge(filled["qkT"], me.next("qkT"))
                        free("qkT", nc.scalar.activation(
                            qT[:, :, t * P:(t + 1) * P], bank[b % 8][:, :].rearrange("p (a n) -> p a n", a=4),
                            ACT.Copy, scale=SCALE))
                        b += 1
                    act.wait_ge(filled["qkT"], me.next("qkT"))
                    free("qkT", nc.scalar.activation(
                        kT[:, :, t * P:(t + 1) * P], bank[b % 8][:, 0:256].rearrange("p (a n) -> p a n", a=2), ACT.Copy))
                    b += 1

                for c in range(4):
                    for t in range(TILES if c == 1 else NT):
                        act.wait_ge(filled["z"], me.next("z"))
                        if c == 0:
                            o, i, f = z[:, t, 0:512], bank[b % 8][:, :], ACT.Copy
                        elif c == 1:
                            o, i, f = z[:, t, 512:768], bank[b % 8][:, 0:256], ACT.Copy
                        else:
                            o, i, f = ug[:, c - 2, t, :], bank[b % 8][:, :], ACT.Gelu_apprx_tanh
                        free("z", nc.scalar.activation(o, i, f))
                        b += 1
                        if c >= 2:
                            for u in heads_after(c, t, NT):
                                queries_keys(u)
                act.wait_ge(filled["ws"], me.next("ws"))
                free("ws", nc.scalar.activation(wsT[:, :, :].rearrange("p g n -> p (g n)"), bank[b % 8][:, :], ACT.Copy))
                N = NT * AH
                for n in range(N + 2):
                    if n < N:
                        t, h = divmod(n, AH)
                        w = 512 if t < LAT else 256
                        act.wait_ge(nm_ready, units + n + 1)
                        if n >= 3:
                            act.wait_ge(filled["pT"], units + n - 2)
                        free("s", nc.scalar.activation(pr[:, n % 3, 0:w], bank[n % 3][:, 0:w], ACT.Exp,
                                                       bias=nm[:, n % 4:n % 4 + 1], accum_out=rs[:, n:n + 1]))
                    if n >= 2:
                        m = n - 2
                        w = 512 if m // AH < LAT else 256
                        act.wait_ge(filled["pT"], me.next("pT"))
                        if m >= 3:
                            act.wait_ge(pv_done, units + m - 2)
                        free("pT", nc.scalar.activation(prT[:, m % 3, 0:w], bank[3 + m % 3][:, 0:w], ACT.Copy))
                units += N
                for t in range(NT):
                    for half in range(2):
                        act.wait_ge(filled["mT"], me.next("mT"))
                        free("mT", nc.scalar.activation(
                            hT[:, 4 * half:4 * half + 4, t * P:(t + 1) * P],
                            bank[(2 * t + half) % 8][:, :].rearrange("p (a n) -> p a n", a=4), ACT.Copy))
                norm_evac(1, NT)
                act.drain()
                act.wait_ge(emptied["xTv"], (TILES + NT if layer == 0 else 3 * TILES + LAT))
                for m in range(QUARTERS * (NT // LAT)):
                    g, step, i = m // QUARTERS, m % QUARTERS // 4, m % 4
                    kind = STEPS[step][0]
                    if m % QUARTERS == 0:
                        if g:
                            act.wait_ge(filled["f1"], 32)
                        nc.scalar.activation(h_hi[:, :, :], hT[:, :, g * SEQ:(g + 1) * SEQ], ACT.Copy
                                             ).then_inc(h_hi_ready, 1)
                    chunk = ff_chunk(layer, g, step)
                    if layer == g == 0 and i == 3 and 1 <= step <= 12:
                        partials(11 + step, 7)
                    if i == 0:
                        act.wait_ge(landed[chunk % SLOTS], 16 * (chunk // SLOTS + 1))
                    if m >= 4:
                        act.wait_ge(quarter_used, layer * (2 * QUARTERS - 1) + m - 3)
                    nc.scalar.activation(shaped(w_hi[:, m % 4, :], kind), quarter(ring[:, chunk % SLOTS, :], kind, i),
                                         ACT.Copy).then_inc(hi_ready, 1)

            with act.Fori(0, LAYERS) as l:
                me.new_layer(l)
                for t in range(LAT):
                    act.wait_ge(filled["BxTs"], me.next("BxTs"))
                    for i in range(4):
                        last = nc.scalar.activation(h2[:, 4 + i, t * P:(t + 1) * P],
                                                    bank[2 * t + 1][:, i * P:(i + 1) * P], ACT.Copy,
                                                    scale=gcol[:, 4 + i:5 + i])
                    free("BxTs", last)

                def projected(c, i, b):
                    act.wait_ge(filled["proj"], me.next("proj"))
                    if c >= 6:
                        ins = nc.scalar.activation(sig[:, c // 8, c % 2 * 4 + i, :], bank[b][:, 0:SEQ], ACT.Sigmoid)
                    elif c % 3 == 2:
                        ins = nc.scalar.activation(dfv[:, c // 3, i, :], bank[b][:, :], ACT.Copy)
                    else:
                        ins = nc.scalar.activation(dfT[:, c // 3 * 2 + c % 3, i, :], bank[b][:, 0:SEQ], ACT.Copy,
                                                   scale=SCALE if c % 3 == 0 else 1.0)
                    free("proj", ins)

                b = 4
                for c in range(3):
                    for i in range(LAT if c == 2 else 4):
                        projected(c, i, b % 8)
                        b += 1
                act.wait_ge(filled["sk"], me.next("sk"))
                free("sk", nc.scalar.activation(skT.rearrange("p a n -> p (a n)"), bank[b % 8][:, 0:256], ACT.Copy))
                act.wait_ge(S["lam_z"], me.at(1, "lam_z"))
                nc.scalar.activation(lam2[:, 4:6], lam2[:, 2:4], ACT.Exp).then_inc(S["lam_e"], 1)
                act.wait_ge(S["ff_z"], me.at(1, "ff_z"))
                nc.scalar.activation(fcv[:, 1, :], fcv[:, 1, :], ACT.Exp)
                act.drain()
                nc.scalar.activation(fcv[:, 2, :], fcv[:, 1, :], ACT.Ln, bias=1.0).then_inc(S["ff_e"], 1)
                for g, (what, c, i) in enumerate(BETWEEN):
                    if what != "ff":
                        projected(c, i, 2 + g % 2)
                    if g < len(GROUPS):
                        kind, qt, h, s0 = GROUPS[g]
                        nk = (qt + 1) * P
                        for s in range(s0, s0 + 2 - kind):
                            act.wait_ge(emptied["Bs"], me.at(s + 1, "Bs"))
                            if s >= 4:
                                old = GROUP_OF[s - 4]
                                if old < 2 * DH:
                                    act.wait_ge(S["w_ready"], me.at(old + 1, "w_ready"))
                                else:
                                    act.wait_ge(filled["BpT"], me.at(old + 1, "BpT"))
                            nc.scalar.activation(pb[:, s % 4, 0:nk], lg[:, s % 4, 0:nk], ACT.Exp, scale=-1.0,
                                                 bias=nm[:, s % 4:s % 4 + 1], accum_out=rs[:, s:s + 1]
                                                 ).then_inc(S["p_ready"], 1)
                    if 2 <= g < len(GROUPS) + 2:
                        kind, qt, h, s = GROUPS[g - 2]
                        act.wait_ge(filled["BpT"], me.next("BpT"))
                        if g >= 5:
                            act.wait_ge(S["Bpv"], me.at(g - 4, "Bpv"))
                        w = (qt + 1) * P
                        free("BpT", nc.scalar.activation(pbT[:, (g - 2) % 3, 0:w], bank[4 + g % 2][:, 0:w], ACT.Copy))
                for n in range(4):
                    kind, qt = divmod(n, 2)
                    act.wait_ge(filled["yT"], me.next("yT"))
                    free("yT", nc.scalar.activation(yT[:, 4 * kind:4 * kind + 4, qt * P:(qt + 1) * P],
                                                    bank[n][:, :].rearrange("p (a n) -> p a n", a=4), ACT.Copy))
                for t in range(LAT):
                    act.wait_ge(filled["BxTs"], me.next("BxTs"))
                    free("BxTs", nc.scalar.activation(h2[:, 4:8, t * P:(t + 1) * P],
                                                      bank[2 * t + 1][:, :].rearrange("p (a n) -> p a n", a=4), ACT.Copy))
                def scores_out(c):
                    for t in range(LAT):
                        act.wait_ge(filled["sc"], me.next("sc"))
                        free("sc", nc.scalar.activation(scores[t][c].rearrange("p (a n) -> p a n", a=4),
                                                        bank[4 * (c % 2) + t][:, :].rearrange("p (a n) -> p a n", a=4),
                                                        ACT.Copy))

                for c in range(4):
                    for i in range(4):
                        act.wait_ge(filled["q2"], me.next("q2"))
                        free("q2", nc.scalar.activation(qq[:, 4 * c + i, :], bank[4 * (c % 2) + i][:, 0:SEQ], ACT.Copy))
                        if c and i == 0:
                            scores_out(c - 1)
                scores_out(3)
                for t in range(LAT):
                    act.wait_ge(S["gate_z"], me.at(t + 1, "gate_z"))
                    nc.scalar.activation(gates[:, t, :], gates[:, t, :], ACT.Exp).then_inc(S["gate_e"], 1)
                    act.wait_ge(S["dotted"], me.at(t + 1, "dotted"))
                    nc.scalar.activation(dots[:, t, :], dots[:, t, :], ACT.Gelu).then_inc(S["acted"], 1)
                    act.wait_ge(S["weighed"], me.at(t + 1, "weighed"))
                    with act.Fori(0, RUN) as i:
                        for n, j in enumerate(PROWS):
                            act.wait_ge(S["free_p"], me.at(i * NP + t * NP * RUN + n + 1, "free_p"))
                            nc.scalar.activation(diag[:, n, :], eye[:, :], ACT.Copy,
                                                 scale=dots[:, t, bass.ds(i * ROWS + j, 1)]).then_inc(S["diag_ready"], 1)

        @block.vector
        def _(dve):
            me = Side()
            v = nc.vector

            def flush():
                return dve.drain()

            def free(fam, ins):
                ins.then_inc(emptied[fam], 1)

            def rstd(o, i, n):
                w = i.shape[1]
                m, y, a, b = (nw[:, k, 0:w] for k in range(4))
                v.tensor_scalar(m, i, 1.0 / n, EPS, ALU.mult, ALU.add)
                flush()
                v.tensor_single_scalar(a.bitcast(U32), m.bitcast(U32), 1, ALU.logical_shift_right)
                flush()
                v.tensor_scalar(y.bitcast(U32), a.bitcast(U32), -1.0, float(0x5F3759DF), ALU.mult, ALU.add)
                flush()
                for step in range(3):
                    v.tensor_tensor(a, y, y, ALU.mult)
                    flush()
                    v.scalar_tensor_tensor(b, a, -0.5, m, ALU.mult, ALU.mult)
                    flush()
                    v.scalar_tensor_tensor(y if step < 2 else o, b, 1.5, y, ALU.add, ALU.mult)
                    flush()

            def row_stats(tiles):
                for t in range(tiles):
                    v.tensor_tensor_reduce(out=xn[:, t % 2, :], in0=x[:, t, :], in1=x[:, t, :], scale=1.0,
                                           scalar=0.0, op0=ALU.mult, op1=ALU.add, accum_out=ss[:, t:t + 1])
                    if t % 2:
                        flush()
                rstd(rst[:, 0:tiles], ss[:, 0:tiles], D)

            def row_norm(t, o):
                return v.tensor_scalar(o, x[:, t, :], rst[:, t:t + 1], None, ALU.mult)

            v.memset(cond[:, :, :], 0.0).then_inc(cond_zero, 1)
            dve.wait_ge(emptied["col"], me.at(1, "col"))
            dve.wait_ge(x_in, 32)
            v.memset(st[:, :], 1.0)

            def modulation(c, b):
                q = 32 * (c % 4)
                dve.wait_ge(filled["msum"], me.next("msum"))
                free("msum", v.tensor_tensor(modrow[c // 4][q:q + 2, :], bank[b][q:q + 2, :], bmod[c // 4][q:q + 2, :], ALU.add))
                flush()

            dve.wait_ge(bmod_in, 16 * 12)
            for c in range(12):
                modulation(c, 4 + c % 4)
            transposed, units = 0, 0
            for layer in range(LAYERS):
                NT = TILES if layer == 0 else LAT
                for g in range(4):
                    dve.wait_ge(filled["modT"], me.next("modT"))
                    for n, (kind, half) in enumerate(SHIFTS[g]):
                        last = v.tensor_copy(modcol[:, COLUMN[kind], 4 * half:4 * half + 4, :],
                                             bank[1 + g][:, 8 * n:8 * n + 8].rearrange("p (k v) -> p k v", v=2))
                    free("modT", last)
                flush()
                for which in range(2):
                    g = cols[:, 16 + 16 * which + 8 * layer:24 + 16 * which + 8 * layer]
                    v.scalar_tensor_tensor(modA[:, which, :, :], modcol[:, 2 * which + 1, :, :], 1.0,
                                           spread(g, 2, 2), ALU.add, ALU.mult)
                flush().then_inc(modA_ready, 1)

                def norm(which, tiles):
                    nonlocal transposed
                    if transposed:
                        dve.wait_ge(filled["xTs"], transposed)
                    row_stats(tiles)
                    for t in range(tiles + 1):
                        if t < tiles:
                            if transposed + t - 2 >= 0:
                                dve.wait_ge(filled["xTs"], transposed + t - 1)
                            row_norm(t, xn[:, t % 2, :]).then_inc(xn_ready, 1)
                        if t >= 1:
                            dve.wait_ge(filled["xTv"], me.next("xTv"))
                            u = t - 1
                            for i in range(4):
                                last = v.tensor_scalar(hT[:, i, u * P:(u + 1) * P], bank[2 * u % 8][:, i * P:(i + 1) * P],
                                                       modA[:, which, i, u // 2:u // 2 + 1],
                                                       modcol[:, 2 * which, i, u // 2:u // 2 + 1], ALU.mult, ALU.add)
                            free("xTv", last)
                    transposed += tiles

                norm(0, TILES)
                zcount = (0 if layer == 0 else 16)
                dve.wait_ge(wide_in, 12 * 16 * (layer + 1))
                def heads(ap, t):
                    return ap[:, (0 if t < NT else AH) * HD:(AH + AKV) * HD].rearrange("p (h n) -> p h n", n=HD)

                def head_stats(t):
                    return st[:, t * 10 + (0 if t < NT else AH):t * 10 + 10]

                for t in range(TILES):
                    dve.wait_ge(emptied["z"], me.at(zcount + NT + t + 1, "z"))
                    a, zt = heads(tA, t), heads(z[:, t, :], t)
                    v.tensor_tensor(a, zt, zt, ALU.mult)
                    flush()
                    v.tensor_reduce(head_stats(t), a, AX.X, ALU.add)
                    flush()
                rstd(st[:, 0:40], st[:, 0:40], HD)
                for t in range(TILES):
                    a, b, zt = heads(tA, t), heads(tB, t), heads(z[:, t, :], t)
                    nh = a.shape[1]
                    v.tensor_tensor(a, zt, spread(head_stats(t), 2, HD), ALU.mult)
                    flush()
                    v.tensor_tensor(a, a, heads(gq, t), ALU.mult)
                    flush()
                    if t < LAT:
                        for off in range(0, HD, 16):
                            oth = off + 16 if off % 32 == 0 else off - 16
                            v.tensor_tensor(b[:, :, off:off + 16], a[:, :, oth:oth + 16],
                                            spread(rope[:, t, 1, off:off + 16], 1, nh), ALU.mult)
                        flush()
                        v.tensor_tensor(a, a, spread(rope[:, t, 0, :], 1, nh), ALU.mult)
                        flush()
                    if layer or t:
                        dve.wait_ge(filled["qkT"], 2 * TILES * layer + t + min(t, NT))
                    kq, kb = a[:, nh - AKV:nh, :], b[:, nh - AKV:nh, :]
                    qo = qn[:, 0:QW].rearrange("p (h n) -> p h n", n=HD)
                    ko = qn[:, QW:768].rearrange("p (j c n) -> p j c n", j=AKV, c=2)
                    if t < LAT:
                        v.tensor_tensor(qo, a[:, 0:AH, :], b[:, 0:AH, :], ALU.add)
                    elif t < NT:
                        v.tensor_copy(qo, a[:, 0:AH, :])
                    for c in range(2):
                        if t < LAT:
                            v.tensor_tensor(ko[:, :, c, :], kq, kb, ALU.add)
                        else:
                            v.tensor_copy(ko[:, :, c, :], kq)
                    flush().then_inc(qn_ready, 1)
                groups = lambda t: ug[:, 1, t, :].rearrange("p (g n) -> p g n", g=4)

                def gating():
                    for t in range(NT):
                        dve.wait_ge(emptied["z"], me.at(zcount + NT + TILES + NT + t + 1, "z"))
                        v.tensor_reduce(st[:, 40 + 4 * t:44 + 4 * t], groups(t), AX.X, ALU.add)
                        yield
                    flush()
                    yield
                    v.tensor_scalar(st[:, 40:40 + 4 * NT], st[:, 40:40 + 4 * NT], 1.0 / P, None, ALU.mult)
                    flush()
                    yield
                    for t in range(NT):
                        v.tensor_tensor(groups(t), groups(t), spread(st[:, 40 + 4 * t:44 + 4 * t], 2, P), ALU.subtract)
                        flush()
                        yield
                        v.tensor_tensor(tA[:, 0:GW], ug[:, 1, t, :], ug[:, 1, t, :], ALU.mult)
                        flush()
                        yield
                        v.tensor_reduce(st[:, 56 + 4 * t:60 + 4 * t], tA[:, 0:GW].rearrange("p (g n) -> p g n", g=4),
                                        AX.X, ALU.add)
                        flush()
                        yield
                    rstd(st[:, 56:56 + 4 * NT], st[:, 56:56 + 4 * NT], P)
                    yield
                    for t in range(NT):
                        v.tensor_tensor(groups(t), groups(t), spread(st[:, 56 + 4 * t:60 + 4 * t], 2, P), ALU.mult)
                        flush()
                        yield
                        v.tensor_tensor(ug[:, 1, t, :], ug[:, 1, t, :], ggain[:, :], ALU.mult)
                        flush().then_inc(vn_ready, 1)
                        yield

                N = NT * AH

                def attn_out(t):
                    w = rs[:, t * AH:(t + 1) * AH]
                    dve.wait_ge(pv_done, units + (t + 1) * AH)
                    v.reciprocal(rr[:, :], w)
                    flush()
                    free("o", v.tensor_tensor(z[:, t, 0:512].rearrange("p (h n) -> p h n", n=HD),
                                              bank[6 + t % 2][:, :].rearrange("p (h n) -> p h n", n=HD),
                                              spread(rr[:, :], 2, HD), ALU.mult))
                    flush().then_inc(mix_ready, 1)

                between = gating()
                for n in range(N):
                    t = n // AH
                    w = 512 if t < LAT else 256
                    if t and n % AH == 3:
                        attn_out(t - 1)
                    dve.wait_ge(filled["s"], me.next("s"))
                    if n >= 4:
                        dve.wait_ge(emptied["s"], me.at(units + n - 3, "s"))
                    v.tensor_reduce(nm[:, n % 4:n % 4 + 1], bank[n % 3][:, 0:w], AX.X, ALU.max, negate=True
                                    ).then_inc(nm_ready, 1)
                    next(between, None)
                for _ in between:
                    pass
                attn_out(NT - 1)
                units += N
                for t in range(NT):
                    dve.wait_ge(filled["sp"], me.next("sp"))
                    for g in range(4):
                        at = slice(g * P, (g + 1) * P)
                        c = 64 + 4 * layer + g
                        last = v.scalar_tensor_tensor(gm[:, t, at], bank[t][:, at], cols[:, c:c + 1], ug[:, 0, t, at],
                                                      ALU.add, ALU.mult)
                    free("sp", last)

                def gated(fam, which, order, banks):
                    for half, t in order:
                        dve.wait_ge(filled[fam], me.next(fam))
                        cut = slice(half * CH, (half + 1) * CH)
                        tmp = xn[:, t % 2, 0:CH]
                        free(fam, v.tensor_tensor(tmp, bank[banks(half, t)][:, :], gate[:, which, t // 2, cut], ALU.mult))
                        flush()
                        v.tensor_tensor(x[:, t, cut], x[:, t, cut], tmp, ALU.add)
                        flush()

                gated("y", 0, [(half, t) for half in range(2) for t in range(NT)], lambda half, t: (half * NT + t) % 8)
                norm(1, NT)
                before = 2 * layer
                for m in range(QUARTERS * (NT // LAT) + 3):
                    g, step, i = m // QUARTERS, m % QUARTERS // 4, m % 4
                    if m < QUARTERS * (NT // LAT):
                        if m % QUARTERS == 0:
                            dve.wait_ge(h_hi_ready, before + g + 1)
                            v.tensor_tensor(h_lo[:, :, :], hT[:, :, g * SEQ:(g + 1) * SEQ], h_hi[:, :, :], ALU.subtract
                                            ).then_inc(h_ready, 1)
                        kind, slot = STEPS[step][0], ff_chunk(layer, g, step) % SLOTS
                        dve.wait_ge(hi_ready, QUARTERS * before + m + 1)
                        v.tensor_tensor(shaped(w_lo[:, i, :], kind), quarter(ring[:, slot, :], kind, i),
                                        shaped(w_hi[:, i, :], kind), ALU.subtract).then_inc(lo_ready, 1)
                    if m < 3:
                        continue
                    g, step, i = (m - 3) // QUARTERS, (m - 3) % QUARTERS // 4, (m - 3) % 4
                    kind, c = STEPS[step]
                    if kind == 0:
                        dve.wait_ge(filled["f1"], me.next("f1"))
                        n = me.n["f1"] - 1
                        s, relu = bank[4 + n % 3][:, 0:SEQ], xn[:, n % 2, 0:SEQ]
                        hi, lo = u_hi[:, c % 2, i, :], u_lo[:, c % 2, i, :]
                        v.tensor_scalar(relu, s, 0.0, None, ALU.max)
                        flush()
                        free("f1", v.tensor_tensor(relu, s, relu, ALU.mult))
                        flush()
                        v.tensor_copy(hi, relu)
                        flush()
                        v.tensor_tensor(lo, relu, hi, ALU.subtract).then_inc(hidden_ready, 1)
                    if layer == g == 0 and 1 <= step <= 12 and i == 1:
                        if step == 1:
                            dve.wait_ge(bmod_in, 2 * 16 * 12)
                        modulation(step - 1, 7)
                    if step == len(STEPS) - 1 and i == 3:
                        gated("f2", 1, [(half, t) for t in (2 * g, 2 * g + 1) for half in range(2)],
                              lambda half, t: t % 2 * 2 + half)
            v.memset(layerE[:, :], 0.0)
            flush().then_inc(layer_done, 1)

            dve.drain().then_inc(scratch_free, 1)
            with dve.Fori(0, LAYERS) as l:
                me.new_layer(l)
                v.tensor_copy(gcol[:, :], cols[:, bass.ds(l * KD + 48, KD)])
                flush()
                row_stats(LAT)
                for t in range(LAT):
                    row_norm(t, xn[:, t, :]).then_inc(S["Bxn"], 1)
                for t in range(LAT):
                    dve.wait_ge(filled["BxTv"], me.next("BxTv"))
                    for i in range(4):
                        last = v.tensor_scalar(h2[:, i, t * P:(t + 1) * P], bank[2 * t][:, i * P:(i + 1) * P],
                                               gcol[:, i:i + 1], None, ALU.mult)
                    free("BxTv", last)
                dve.wait_ge(S["small_in"], me.at(PER["small_in"], "small_in"))
                v.tensor_tensor(lamp, lamrow[:, 0::2, :], lamrow[:, 1::2, :], ALU.mult)
                v.tensor_scalar(subln, subln, lam2[:, 1:2], None, ALU.mult)
                flush()
                v.tensor_reduce(lam2[:, 2:4], lamp, AX.X, ALU.add)
                flush().then_inc(S["lam_z"], 1)
                dve.wait_ge(filled["ff"], me.next("ff"))
                free("ff", v.tensor_scalar(fcv[:, 0, :], bank[2][0:FH, 0:SEQ], bfc[:, :], None, ALU.add))
                flush()
                v.tensor_scalar(fcv[:, 1, :], fcv[:, 0, :], -1.0, None, ALU.mult)
                v.memset(fcv[:, 5, :], 1.0)
                flush()
                v.tensor_tensor(fcv[:, 1, :], fcv[:, 1, :], fcv[:, 0, :], ALU.min)
                flush().then_inc(S["ff_z"], 1)
                dve.wait_ge(S["ff_e"], me.at(1, "ff_e"))
                v.scalar_tensor_tensor(fcv[:, 2, :], fcv[:, 0, :], 0.0, fcv[:, 2, :], ALU.min, ALU.subtract)
                flush()
                v.tensor_tensor_scan(fcv[:, 3, :], fcv[:, 5, :], fcv[:, 2, :], 0.0, ALU.mult, ALU.add)
                flush()
                v.tensor_scalar(fcv[:, 4, :], fcv[:, 3, :], -1.0, None, ALU.mult)
                dve.wait_ge(S["lam_e"], me.at(1, "lam_e"))
                v.tensor_tensor(lam2[:, 6:7], lam2[:, 5:6], lam2[:, 4:5], ALU.subtract)
                flush().then_inc(S["c_ready"], 1)
                v.tensor_tensor(lam2[:, 7:8], lam2[:, 6:7], lam2[:, 0:1], ALU.subtract)
                flush()

                def heads_out(n):
                    kind, qt = divmod(n, 2)
                    dve.wait_ge(S["Bpv"], me.at(LAST_GROUP[n] + 1, "Bpv"))
                    y = yy[:, kind, qt, :]
                    if kind:
                        v.reciprocal(rr[:, :], rs[:, 16 + 8 * qt:24 + 8 * qt])
                        flush()
                        free("Bo", v.tensor_tensor(y.rearrange("p (h n) -> p h n", n=HD),
                                                   bank[6 + qt][:, :].rearrange("p (h n) -> p h n", n=HD),
                                                   spread(rr[:, :], 2, HD), ALU.mult))
                        flush().then_inc(S["y_ready"], 1)
                        return
                    free("Bo", v.tensor_copy(y, bank[6 + qt][:, :]))
                    flush()
                    v.tensor_tensor(tM.rearrange("p a n -> p (a n)"), y, y, ALU.mult)
                    flush()
                    v.tensor_reduce(st[:, 0:4], tM.rearrange("p a (b n) -> p (a b) n", n=P), AX.X, ALU.add)
                    flush()
                    rstd(st[:, 0:4], st[:, 0:4], P)
                    yv = y.rearrange("p (h n) -> p h n", n=P)
                    v.tensor_tensor(yv, yv, spread(st[:, 0:4], 2, P), ALU.mult)
                    flush()
                    v.tensor_tensor(yv, yv, spread(subln, 1, DH), ALU.mult)
                    flush().then_inc(S["y_ready"], 1)

                dve.wait_ge(bias_in, 32)
                outs = 0
                for g in range(len(GROUPS) + 1):
                    if outs < 4 and g - 5 >= LAST_GROUP[outs]:
                        heads_out(outs)
                        outs += 1
                    if g < len(GROUPS):
                        kind, qt, h, s0 = GROUPS[g]
                        nk = (qt + 1) * P
                        for s in range(s0, s0 + 2 - kind):
                            dve.wait_ge(filled["Bs"], me.next("Bs"))
                            dve.nop(nofuse=True)
                            if s >= 4:
                                dve.wait_ge(S["p_ready"], me.at(s - 3, "p_ready"))
                                dve.nop(nofuse=True)
                            add = mask if kind else bias[:, h, :]
                            v.tensor_tensor_reduce(out=lg[:, s % 4, 0:nk], in0=bank[s % 2][:, 0:nk],
                                                   in1=add[:, SEQ - nk:SEQ], scale=-1.0, scalar=3.0e38, op0=ALU.add,
                                                   op1=ALU.min, accum_out=nm[:, s % 4:s % 4 + 1]
                                                   ).then_inc(emptied["Bs"], 1)
                    if g >= 1:
                        kind, qt, h, s = GROUPS[g - 1]
                        if kind == 0:
                            nk = (qt + 1) * P
                            dve.wait_ge(S["p_ready"], me.at(s + 2, "p_ready"))
                            v.reciprocal(rr[:, 0:2], rs[:, s:s + 2])
                            flush()
                            v.tensor_scalar(rr[:, 2:3], rr[:, 1:2], lam2[:, 7:8], None, ALU.mult)
                            if g >= 3:
                                dve.wait_ge(filled["BpT"], me.at(g - 2, "BpT"))
                            wv = wd[:, (g - 1) % 2, 0:nk]
                            v.tensor_scalar(wv, pb[:, s % 4, 0:nk], rr[:, 0:1], None, ALU.mult)
                            flush()
                            v.scalar_tensor_tensor(wv, pb[:, (s + 1) % 4, 0:nk], rr[:, 2:3], wv, ALU.mult, ALU.add)
                            flush().then_inc(S["w_ready"], 1)
                while outs < 4:
                    heads_out(outs)
                    outs += 1
                dve.wait_ge(emptied["proj"], me.at(36, "proj"))
                for j in range(KD):
                    dve.wait_ge(filled["mg"], me.next("mg"))
                    free("mg", v.tensor_tensor(tM, bank[j % 8][:, :].rearrange("p (a n) -> p a n", a=2),
                                               sig[:, :, j, :], ALU.mult))
                    flush()
                    v.tensor_tensor(mT[:, j, :], tM[:, 0, :], tM[:, 1, :], ALU.add)
                    flush().then_inc(S["mT_ready"], 1)
                for half in range(2):
                    for t in range(LAT):
                        dve.wait_ge(filled["By"], me.next("By"))
                        cut = slice(half * CH, (half + 1) * CH)
                        free("By", v.tensor_tensor(x[:, t, cut], x[:, t, cut], bank[half * LAT + t][:, :], ALU.add))
                flush()
                dve.wait_ge(S["gain_in"], me.at(16, "gain_in"))
                row_stats(LAT)
                for t in range(LAT):
                    row_norm(t, xn[:, t, :])
                    flush()
                    v.tensor_tensor(ttok[:, t, :], xn[:, t, :], wide[:, :], ALU.mult).then_inc(S["Bxn"], 1)
                for t in range(LAT):
                    dve.wait_ge(filled["BxTv"], me.next("BxTv"))
                    free("BxTv", v.tensor_copy(h2[:, 0:4, t * P:(t + 1) * P],
                                               bank[2 * t][:, :].rearrange("p (a n) -> p a n", a=4)))

                def top16(src, spare, o, where, n, w):
                    s = [src[:, i * w:(i + 1) * w] for i in range(n)]
                    r = [spare[:, i * w:(i + 1) * w] for i in range(n)]
                    for i in range(n):
                        v.max(out=o[:, i, 0:8], in_=s[i])
                    flush()
                    for i in range(n):
                        v.max_index(out=where[:, i, 0:8], in_max=o[:, i, 0:8], in_values=s[i])
                        v.match_replace(out=r[i], in_to_replace=o[:, i, 0:8], in_values=s[i], imm_value=-3.0e38)
                    flush()
                    yield
                    for i in range(n):
                        v.max(out=o[:, i, 8:16], in_=r[i])
                    flush()
                    for i in range(n):
                        v.max_index(out=where[:, i, 8:16], in_max=o[:, i, 8:16], in_values=r[i])
                    flush()

                def search(t, c):
                    dve.wait_ge(emptied["sc"], me.at(2 * c + t + 1, "sc"))
                    dve.nop(nofuse=True)
                    yield from top16(scores[t][c], w1, tv, ti, 4, NK)
                    v.tensor_copy(tif, ti)
                    for h in range(2):
                        v.tensor_tensor(w1[:, h * 256:(h + 1) * 256].rearrange("p (a b) -> p a b", a=16),
                                        spread(tv[:, 2 * h, :], 2, 16), spread(tv[:, 2 * h + 1, :], 1, 16), ALU.add)
                    flush()
                    yield
                    yield from top16(w1, w2, bv, bp, 2, 256)
                    mine = slice(32 * c, 32 * c + 32)
                    v.tensor_single_scalar(bi[:, 0], bp, 4, ALU.logical_shift_right)
                    v.tensor_single_scalar(bi[:, 1], bp, 15, ALU.bitwise_and)
                    v.tensor_tensor(gates[:, t, mine].rearrange("p (h n) -> p h n", n=16), bv,
                                    bv[:, :, 0:1].broadcast_to([P, 2, 16]), ALU.subtract)
                    flush()
                    v.tensor_copy(bf, bi)
                    flush()
                    for a in range(2):
                        one = w1[:, a * 512:(a + 1) * 512]
                        v.tensor_tensor(one.rearrange("p (a b) -> p a b", b=16),
                                        spread(bf[:, a].rearrange("p h n -> p (h n)"), 2, 16),
                                        spread(iota[:, :], 1, 32), ALU.is_equal)
                    flush()
                    yield
                    for a in range(2):
                        for h in range(2):
                            wv = w1[:, a * 512 + h * 256:a * 512 + (h + 1) * 256].rearrange("p (a b) -> p a b", a=16)
                            v.tensor_tensor(wv, wv, spread(tif[:, 2 * h + a, :], 1, 16), ALU.mult)
                    flush()
                    yield
                    v.tensor_reduce(ei[:, 0, :], w1.rearrange("p (a b) -> p a b", b=16), AX.X, ALU.add)
                    flush()
                    v.tensor_scalar(ei[:, 1, 0:32], ei[:, 0, 0:32], float(NK), layerE[:, :], ALU.mult, ALU.add)
                    flush()
                    v.tensor_tensor(ei[:, 1, 0:32], ei[:, 1, 0:32], ei[:, 0, 32:64], ALU.add)
                    flush()
                    pick = v.tensor_copy(picks[:, t, mine], ei[:, 1, 0:32])
                    if t == c == 0:
                        pick.then_inc(S["first_picks"], 1)
                    if c == 3:
                        pick.then_inc(S["picked"], 1)
                        flush().then_inc(S["gate_z"], 1)
                    yield

                for c in range(4):
                    for _ in search(0, c):
                        pass

                for t in range(LAT):
                    dve.wait_ge(S["gate_e"], me.at(t + 1, "gate_e"))
                    gt = gates[:, t, :].rearrange("p (h n) -> p h n", n=16)
                    v.tensor_reduce(rr[:, :], gt, AX.X, ALU.add)
                    flush()
                    v.reciprocal(rr[:, :], rr[:, :])
                    flush()
                    v.tensor_tensor(gt, gt, spread(rr[:, :], 2, 16), ALU.mult)
                    flush()
                    with dve.Fori(0, RUN) as i:
                        for j in range(ROWS):
                            dve.wait_ge(row_in[j], me.at(i * 16 + 2 * t * RUN * 16 + 16, "row_in"))
                            v.tensor_tensor_reduce(out=junk[j % 2], in0=expert[j], in1=ttok[:, t, :], scale=1.0,
                                                   scalar=0.0, op0=ALU.mult, op1=ALU.add, accum_out=d16[:, j:j + 1]
                                                   ).then_inc(S["free_v"], 1)
                            if j % 2:
                                flush()
                        v.tensor_copy(dots[:, t, bass.ts(i, ROWS)], d16[:, :])
                        flush()
                    flush().then_inc(S["dotted"], 1)
                    v.memset(acc, 0.0)
                    dve.wait_ge(S["acted"], me.at(t + 1, "acted"))
                    v.tensor_tensor(dots[:, t, :], dots[:, t, :], gates[:, t, :], ALU.mult)
                    flush().then_inc(S["weighed"], 1)
                    def add_row(i, j):
                        dve.wait_ge(row_in[j], me.at(i * 16 + (2 * t + 1) * RUN * 16 + 16, "row_in"))
                        v.scalar_tensor_tensor(acc, expert[j],
                                               dots[:, t, bass.ds(i * ROWS + j, 1)], acc,
                                               ALU.mult, ALU.add).then_inc(S["free_v"], 1)
                        flush()

                    if t == 0:
                        parts = (part for c in range(4) for part in search(1, c))
                        for i in range(RUN):
                            for j in VROWS:
                                add_row(i, j)
                                next(parts, None)
                        dve.drain().then_inc(scratch_free, 1)
                    else:
                        with dve.Fori(0, RUN) as i:
                            for j in VROWS:
                                add_row(i, j)
                    flush().then_inc(S["acc_ready"], 1)
                    if t == LAT - 1:
                        for u in range(LAT):
                            dve.wait_ge(filled["acc"], me.next("acc"))
                            for half in range(2):
                                last = v.tensor_copy(x[:, u, half * CH:(half + 1) * CH], bank[2 * u + half][:, :])
                            free("acc", last)
                    else:
                        dve.wait_ge(filled["acc"], me.at(t + 1, "acc"))
                        dve.nop(nofuse=True)
                v.tensor_scalar(layerE[:, :], layerE[:, :], float(NE), None, ALU.add)
                flush().then_inc(layer_done, 1)

            dve.wait_ge(final_in, 16)
            row_stats(LAT)
            for t in range(LAT):
                row_norm(t, xn[:, t, :])
                flush()
                v.tensor_tensor(xn[:, t, :], xn[:, t, :], wide[:, :], ALU.mult)
            flush().then_inc(result_ready, 1)
        return nc


_INS = ["x", "c", "ctx", "c_ctx", "w_mod", "b_mod", "norm1_g", "w_in", "q_norm_g", "k_norm_g",
        "gmlp_norm_g", "w_spatial", "b_spatial", "w_out", "norm2_g", "w_ff1", "w_ff2", "norm1_g_2",
        "w_in_2", "b_forget_2", "diff_lambda_2", "diff_subln_g_2", "w_diff_o_2", "w_fox_o_2",
        "w_out_2", "norm2_g_2", "w_query_2", "sub_keys_2", "expert_u_2", "expert_v_2",
        "rel_bias_2", "final_norm_g_2"]


def kernel(**inputs):
    import concourse.bacc as bacc
    from concourse.bass_utils import run_bass_kernel_spmd as run

    nc = bacc.Bacc("TRN2", target_bir_lowering=False, num_devices=1)
    arrays, views = {}, {}
    named = {k: np.ascontiguousarray(inputs[k]) for k in _INS}
    for name, a in {**named, **constants()}.items():
        arrays[f"in_{name}"] = a
        views[name] = nc.dram_tensor(f"in_{name}", a.shape, mybir.dt.from_np(a.dtype), kind="ExternalInput").ap()
    out = nc.dram_tensor("out_x", (1, SEQ, D), F32, kind="ExternalOutput").ap()
    build(nc, views, out)
    r = run(nc, [arrays], core_ids=[0])
    return r.results[0]["out_x"]
```
